# Optimizing a Trainium2 kernel written in Bass

```python
import jax
import jax.numpy as jnp
from jax import lax
import numpy as np

D_MODEL = 1024
BATCH = 1
SEQ = 256
DEPTH = 1

HEAD_DIM = 64
ROPE_THETA = 10000.0
NORM_EPS = 1e-6
NEG_INF = -1e30

NSA_HEADS = 8
NSA_KV_HEADS = 2
NSA_GROUP = NSA_HEADS // NSA_KV_HEADS
CMP_BLOCK = 32
CMP_STRIDE = 16
SLC_BLOCK = 64
SLC_TOPN = 16
WINDOW = 512
SLC_QBLOCK = 64
WIN_QBLOCK = 128

DSA_HEADS = 8
DSA_KV_RANK = 128
IDX_HEADS = 8
IDX_DIM = 64
DSA_TOPK = 256
DSA_QBLOCK = 128

PEER_HEADS = 8
PEER_KEYS = 128
PEER_EXPERTS = PEER_KEYS * PEER_KEYS
PEER_KEY_DIM = 128
PEER_HALF = PEER_KEY_DIM // 2
PEER_TOPK = 16
PEER_CHUNK = 128

NSA_Q_DIM = NSA_HEADS * HEAD_DIM
NSA_KV_DIM = NSA_KV_HEADS * HEAD_DIM
DSA_Q_DIM = DSA_HEADS * HEAD_DIM
IDX_Q_DIM = IDX_HEADS * IDX_DIM
IN_SPLITS = (NSA_Q_DIM, NSA_KV_DIM, NSA_KV_DIM, NSA_KV_DIM, NSA_KV_DIM, NSA_KV_DIM, NSA_KV_DIM,
             3 * NSA_HEADS, DSA_Q_DIM, DSA_KV_RANK, IDX_Q_DIM, IDX_DIM, IDX_HEADS, 2 * D_MODEL)
D_IN = sum(IN_SPLITS)

kernel_name = "hybrid_nsa_dsa_peer_adaln_block"

def rms_norm(x, g):
    xf = x.astype(jnp.float32)
    y = xf * lax.rsqrt(jnp.mean(xf * xf, axis=-1, keepdims=True) + NORM_EPS)
    return (y * g.astype(jnp.float32)).astype(x.dtype)

def rope(x, pos):
    half = x.shape[-1] // 2
    inv = ROPE_THETA ** (-jnp.arange(half, dtype=jnp.float32) / half)
    ang = pos[:, None] * inv[None, :]
    cos = jnp.cos(ang)[:, None, :]
    sin = jnp.sin(ang)[:, None, :]
    xf = x.astype(jnp.float32)
    x1, x2 = xf[..., :half], xf[..., half:]
    return jnp.concatenate([x1 * cos - x2 * sin, x2 * cos + x1 * sin], axis=-1).astype(x.dtype)

def masked_softmax(s, mask):
    s = jnp.where(mask, s.astype(jnp.float32), NEG_INF)
    m = jnp.max(s, axis=-1, keepdims=True)
    p = jnp.where(mask, jnp.exp(s - m), 0.0)
    return p / jnp.maximum(jnp.sum(p, axis=-1, keepdims=True), 1e-30)

def compress_blocks(x, pos_emb, w1, w2):
    B, S, G, dh = x.shape
    r = CMP_BLOCK // CMP_STRIDE
    n_chunk = S // CMP_STRIDE
    ch = x.reshape(B, n_chunk, CMP_STRIDE, G, dh)
    blk = jnp.concatenate([ch[:, i:n_chunk - r + 1 + i] for i in range(r)], axis=2)
    blk = blk + pos_emb[:, None, :]
    hid = jax.nn.gelu(jnp.einsum("bnlgd,lde->bnge", blk, w1))
    return jnp.einsum("bnge,ef->bngf", hid, w2)

def selected_attention(qg, ks, vs, sel, scale):
    B, S, G, hg, dh = qg.shape
    n_slc = S // SLC_BLOCK
    nqb = S // SLC_QBLOCK
    kb = ks.reshape(B, n_slc, SLC_BLOCK, G, dh).transpose(0, 3, 1, 2, 4)
    vb = vs.reshape(B, n_slc, SLC_BLOCK, G, dh).transpose(0, 3, 1, 2, 4)
    q_blk = jnp.moveaxis(qg.reshape(B, nqb, SLC_QBLOCK, G, hg, dh), 1, 0)
    sel_blk = jnp.moveaxis(sel.reshape(B, G, nqb, SLC_QBLOCK, -1), 2, 0)
    t_blk = jnp.arange(S).reshape(nqb, SLC_QBLOCK)
    bi = jnp.arange(B)[:, None, None, None]
    gi = jnp.arange(G)[None, :, None, None]

    def one_block(args):
        qb, sb, tb = args
        n = sb.shape[-1]
        kg = kb[bi, gi, sb].reshape(B, G, SLC_QBLOCK, n * SLC_BLOCK, dh)
        vg = vb[bi, gi, sb].reshape(B, G, SLC_QBLOCK, n * SLC_BLOCK, dh)
        kpos = (sb[..., None] * SLC_BLOCK + jnp.arange(SLC_BLOCK)).reshape(B, G, SLC_QBLOCK, n * SLC_BLOCK)
        mask = (kpos <= tb[None, None, :, None])[:, :, None]
        s = jnp.einsum("bqghd,bgqkd->bghqk", qb, kg) * scale
        p = masked_softmax(s, mask)
        return jnp.einsum("bghqk,bgqkd->bqghd", p.astype(vg.dtype), vg)

    o = lax.map(one_block, (q_blk, sel_blk, t_blk))
    return jnp.moveaxis(o, 0, 1).reshape(B, S, G, hg, dh)

def window_attention(qg, kw, vw, scale):
    B, S, G, hg, dh = qg.shape
    nwb = S // WIN_QBLOCK
    kspan = WINDOW + WIN_QBLOCK
    pad = ((0, 0), (WINDOW, 0), (0, 0), (0, 0))
    kpad = jnp.pad(kw, pad)
    vpad = jnp.pad(vw, pad)
    q_blk = jnp.moveaxis(qg.reshape(B, nwb, WIN_QBLOCK, G, hg, dh), 1, 0)

    def one_block(args):
        qb, i = args
        start = i * WIN_QBLOCK
        kb = lax.dynamic_slice_in_dim(kpad, start, kspan, axis=1)
        vb = lax.dynamic_slice_in_dim(vpad, start, kspan, axis=1)
        tq = start + jnp.arange(WIN_QBLOCK)
        tk = start - WINDOW + jnp.arange(kspan)
        diff = tq[:, None] - tk[None, :]
        mask = (tk[None, :] >= 0) & (diff >= 0) & (diff < WINDOW)
        s = jnp.einsum("bqghd,bkgd->bghqk", qb, kb) * scale
        p = masked_softmax(s, mask)
        return jnp.einsum("bghqk,bkgd->bqghd", p.astype(vb.dtype), vb)

    o = lax.map(one_block, (q_blk, jnp.arange(nwb)))
    return jnp.moveaxis(o, 0, 1).reshape(B, S, G, hg, dh)

def nsa_attention(q, kc, vc, ks, vs, kw, vw, gate_logits, cmp_pos, w1k, w2k, w1v, w2v):
    B, S, H, dh = q.shape
    G, hg = NSA_KV_HEADS, NSA_GROUP
    scale = dh ** -0.5
    t = jnp.arange(S)
    qg = q.reshape(B, S, G, hg, dh)

    k_cmp = compress_blocks(kc, cmp_pos, w1k, w2k)
    v_cmp = compress_blocks(vc, cmp_pos, w1v, w2v)
    nc = k_cmp.shape[1]
    blk_end = jnp.arange(nc) * CMP_STRIDE + CMP_BLOCK - 1
    m_cmp = blk_end[None, :] <= t[:, None]
    s_cmp = jnp.einsum("bsghd,bngd->bghsn", qg, k_cmp) * scale
    p_cmp = masked_softmax(s_cmp, m_cmp)
    o_cmp = jnp.einsum("bghsn,bngd->bsghd", p_cmp.astype(v_cmp.dtype), v_cmp)

    r = CMP_BLOCK // CMP_STRIDE
    imp = jnp.sum(p_cmp, axis=2)
    imp = sum(jnp.pad(imp, ((0, 0), (0, 0), (0, 0), (i, r - 1 - i))) for i in range(r))
    n_slc = S // SLC_BLOCK
    imp = imp.reshape(B, G, S, n_slc, SLC_BLOCK // CMP_STRIDE).sum(-1)
    j = jnp.arange(n_slc)[None, :]
    cur = (t // SLC_BLOCK)[:, None]
    forced = (j == 0) | (j == cur) | (j == cur - 1)
    admissible = j * SLC_BLOCK <= t[:, None]
    imp = jnp.where(forced, jnp.inf, jnp.where(admissible, imp, -jnp.inf))
    n_sel = min(SLC_TOPN, n_slc)
    _, sel = lax.top_k(imp, n_sel)
    o_slc = selected_attention(qg, ks, vs, sel, scale)

    o_win = window_attention(qg, kw, vw, scale)

    g = jax.nn.sigmoid(gate_logits)
    o = (g[..., 0:1] * o_cmp.reshape(B, S, H, dh)
         + g[..., 1:2] * o_slc.reshape(B, S, H, dh)
         + g[..., 2:3] * o_win.reshape(B, S, H, dh))
    return o.reshape(B, S, H * dh)

def dsa_attention(q, k, v, qi, ki, wi):
    B, S, H, dh = q.shape
    scale = dh ** -0.5
    topk = min(DSA_TOPK, S // 4)
    nqb = S // DSA_QBLOCK
    q_blk = jnp.moveaxis(q.reshape(B, nqb, DSA_QBLOCK, H, dh), 1, 0)
    qi_blk = jnp.moveaxis(qi.reshape(B, nqb, DSA_QBLOCK, IDX_HEADS, IDX_DIM), 1, 0)
    wi_blk = jnp.moveaxis(wi.reshape(B, nqb, DSA_QBLOCK, IDX_HEADS), 1, 0)
    t_blk = jnp.arange(S).reshape(nqb, DSA_QBLOCK)
    kpos = jnp.arange(S)
    ki32 = ki.astype(jnp.float32)

    def one_block(args):
        qb, qib, wib, tb = args
        logits = jnp.einsum("bqhd,bkd->bqhk", qib.astype(jnp.float32), ki32) * (IDX_DIM ** -0.5)
        score = jnp.einsum("bqh,bqhk->bqk", wib.astype(jnp.float32) * (IDX_HEADS ** -0.5), jax.nn.relu(logits))
        score = jnp.where(kpos[None, None, :] <= tb[None, :, None], score, -jnp.inf)
        _, sel = lax.top_k(score, topk)
        kg = jax.vmap(lambda kk, ss: kk[ss])(k, sel)
        vg = jax.vmap(lambda vv, ss: vv[ss])(v, sel)
        mask = (sel <= tb[None, :, None])[:, None]
        s = jnp.einsum("bqhd,bqkd->bhqk", qb, kg) * scale
        p = masked_softmax(s, mask)
        return jnp.einsum("bhqk,bqkd->bqhd", p.astype(vg.dtype), vg)

    o = lax.map(one_block, (q_blk, qi_blk, wi_blk, t_blk))
    return jnp.moveaxis(o, 0, 1).reshape(B, S, H * dh)

def token_mixer(h, w_in, cmp_pos, cmp_w1_k, cmp_w2_k, cmp_w1_v, cmp_w2_v,
                kv_norm_g, w_uk, w_uv, w_br_nsa, w_br_dsa, w_out):
    B, S, _ = h.shape
    pos = jnp.arange(S, dtype=jnp.float32)
    z = h @ w_in
    offs = [int(o) for o in np.cumsum(IN_SPLITS)[:-1]]
    (q_n, kc, vc, ks, vs, kw, vw, g_n, q_d, ckv, qi, ki, wi, g_m) = jnp.split(z, offs, axis=-1)
    G = NSA_KV_HEADS
    heads = lambda a, n: a.reshape(B, S, n, -1)

    o_nsa = nsa_attention(
        rope(heads(q_n, NSA_HEADS), pos),
        rope(heads(kc, G), pos), heads(vc, G),
        rope(heads(ks, G), pos), heads(vs, G),
        rope(heads(kw, G), pos), heads(vw, G),
        g_n.reshape(B, S, NSA_HEADS, 3), cmp_pos, cmp_w1_k, cmp_w2_k, cmp_w1_v, cmp_w2_v)

    c_kv = rms_norm(ckv, kv_norm_g)
    k_d = rope((c_kv @ w_uk)[:, :, None, :], pos)[:, :, 0]
    v_d = c_kv @ w_uv
    o_dsa = dsa_attention(
        rope(heads(q_d, DSA_HEADS), pos), k_d, v_d,
        rope(heads(qi, IDX_HEADS), pos), rope(ki[:, :, None, :], pos)[:, :, 0], wi)

    g_nsa, g_dsa = jnp.split(g_m, 2, axis=-1)
    merged = jax.nn.sigmoid(g_nsa) * (o_nsa @ w_br_nsa) + jax.nn.sigmoid(g_dsa) * (o_dsa @ w_br_dsa)
    return merged @ w_out

def peer_ffn(h, wq, subkeys, u, v):
    B, S, D = h.shape
    T = B * S
    xf = h.reshape(T, D)
    q = (xf @ wq).reshape(T, PEER_HEADS, 2, PEER_HALF)
    s_sub = jnp.einsum("thcd,hcnd->thcn", q, subkeys).astype(jnp.float32)
    s_half, i_half = lax.top_k(s_sub, PEER_TOPK)
    cand = s_half[:, :, 0, :, None] + s_half[:, :, 1, None, :]
    cidx = i_half[:, :, 0, :, None] * PEER_KEYS + i_half[:, :, 1, None, :]
    cand = cand.reshape(T, PEER_HEADS, PEER_TOPK * PEER_TOPK)
    cidx = cidx.reshape(T, PEER_HEADS, PEER_TOPK * PEER_TOPK)
    top_s, top_p = lax.top_k(cand, PEER_TOPK)
    eidx = jnp.take_along_axis(cidx, top_p, axis=-1)
    gate = jax.nn.softmax(top_s, axis=-1)
    nch = T // PEER_CHUNK

    def one_chunk(args):
        xc, ec, gc = args
        ue = u[ec]
        ve = v[ec]
        act = jax.nn.gelu(jnp.einsum("cd,chkd->chk", xc, ue), approximate=False)
        return jnp.einsum("chk,chkd->cd", (gc * act).astype(ve.dtype), ve)

    out = lax.map(one_chunk, (xf.reshape(nch, PEER_CHUNK, D),
                              eidx.reshape(nch, PEER_CHUNK, PEER_HEADS, PEER_TOPK),
                              gate.reshape(nch, PEER_CHUNK, PEER_HEADS, PEER_TOPK)))
    return out.reshape(B, S, D).astype(h.dtype)

def setup_inputs(seed: int = 0) -> dict:
    key = jax.random.key(seed)
    ks = jax.random.split(key, 24)
    L, D = DEPTH, D_MODEL
    nrm = lambda k, shape, std: jax.random.normal(k, shape, jnp.float32) * std
    gain = lambda k, shape: 1.0 + 0.05 * jax.random.normal(k, shape, jnp.float32)
    return {
        "x": nrm(ks[0], (BATCH, SEQ, D), 1.0),
        "c": nrm(ks[1], (BATCH, D), 1.0),
        "ada_w": nrm(ks[2], (L, D, 6 * D), 0.5 * D ** -0.5),
        "ada_b": nrm(ks[3], (L, 6 * D), 0.01),
        "norm1_g": gain(ks[4], (L, D)),
        "w_in": nrm(ks[5], (L, D, D_IN), D ** -0.5),
        "cmp_pos": nrm(ks[6], (L, CMP_BLOCK, HEAD_DIM), 0.1),
        "cmp_w1_k": nrm(ks[7], (L, CMP_BLOCK, HEAD_DIM, HEAD_DIM), (CMP_BLOCK * HEAD_DIM) ** -0.5),
        "cmp_w2_k": nrm(ks[8], (L, HEAD_DIM, HEAD_DIM), HEAD_DIM ** -0.5),
        "cmp_w1_v": nrm(ks[9], (L, CMP_BLOCK, HEAD_DIM, HEAD_DIM), (CMP_BLOCK * HEAD_DIM) ** -0.5),
        "cmp_w2_v": nrm(ks[10], (L, HEAD_DIM, HEAD_DIM), HEAD_DIM ** -0.5),
        "kv_norm_g": gain(ks[11], (L, DSA_KV_RANK)),
        "w_uk": nrm(ks[12], (L, DSA_KV_RANK, HEAD_DIM), DSA_KV_RANK ** -0.5),
        "w_uv": nrm(ks[13], (L, DSA_KV_RANK, HEAD_DIM), DSA_KV_RANK ** -0.5),
        "w_br_nsa": nrm(ks[14], (L, NSA_Q_DIM, D), NSA_Q_DIM ** -0.5),
        "w_br_dsa": nrm(ks[15], (L, DSA_Q_DIM, D), DSA_Q_DIM ** -0.5),
        "w_out": nrm(ks[16], (L, D, D), D ** -0.5),
        "norm2_g": gain(ks[17], (L, D)),
        "peer_wq": nrm(ks[18], (L, D, PEER_HEADS * PEER_KEY_DIM), D ** -0.5),
        "peer_subkeys": nrm(ks[19], (L, PEER_HEADS, 2, PEER_KEYS, PEER_HALF), PEER_HALF ** -0.5),
        "peer_u": nrm(ks[20], (L, PEER_EXPERTS, D), D ** -0.5),
        "peer_v": nrm(ks[21], (L, PEER_EXPERTS, D), 0.5),
        "final_g": gain(ks[22], (D,)),
    }

def reference(x, c, ada_w, ada_b, norm1_g, w_in, cmp_pos, cmp_w1_k, cmp_w2_k, cmp_w1_v, cmp_w2_v,
              kv_norm_g, w_uk, w_uv, w_br_nsa, w_br_dsa, w_out, norm2_g,
              peer_wq, peer_subkeys, peer_u, peer_v, final_g):
    for l in range(DEPTH):
        mod = jax.nn.silu(c) @ ada_w[l] + ada_b[l]
        sh1, sc1, g1, sh2, sc2, g2 = jnp.split(mod[:, None, :], 6, axis=-1)
        h = rms_norm(x, norm1_g[l]) * (1.0 + sc1) + sh1
        x = x + g1 * token_mixer(h, w_in[l], cmp_pos[l], cmp_w1_k[l], cmp_w2_k[l], cmp_w1_v[l], cmp_w2_v[l],
                                 kv_norm_g[l], w_uk[l], w_uv[l], w_br_nsa[l], w_br_dsa[l], w_out[l])
        h = rms_norm(x, norm2_g[l]) * (1.0 + sc2) + sh2
        x = x + g2 * peer_ffn(h, peer_wq[l], peer_subkeys[l], peer_u[l], peer_v[l])
    return rms_norm(x, final_g)


_drawn_inputs = setup_inputs


def setup_inputs(seed=0):
    import zlib

    import numpy as np

    out = dict(_drawn_inputs(seed))
    spreads = {}
    factors = {'ada_b': 4.758,
     'norm1_g': 4.893,
     'cmp_pos': 7.117,
     'cmp_w1_k': 3.693,
     'cmp_w2_k': 3.697,
     'kv_norm_g': 8.0,
     'norm2_g': 3.009}
    for name, (base, spread) in spreads.items():
        noise = np.random.default_rng([zlib.crc32(name.encode()), seed]).standard_normal(out[name].shape)
        drawn = base * np.exp(spread * noise) if base else spread * noise
        out[name] = jnp.asarray(drawn.astype(out[name].dtype))
    for name, factor in factors.items():
        out[name] = (out[name] * factor).astype(out[name].dtype)
    return out
```

```python
from contextlib import ExitStack

import concourse.bass as bass
import numpy as np
from concourse import mybir

F32 = mybir.dt.float32
I32 = mybir.dt.int32
U32 = mybir.dt.uint32
ALU = mybir.AluOpType
ACT = mybir.ActivationFunctionType
AX = mybir.AxisListType

P = 128
D = 1024
KT = D // P
T = 256
TT = T // P
DH = 64
HALF = DH // 2
HEADS = 8
EPS = 1e-6
NEG = -1e30
TAKEN = -3e38
CMP_LEN, CMP_STEP = 32, 16
NCMP = T // CMP_STEP - 1
TOPK_DSA = min(256, T // 4)
KEYS = 128
TOPK = 16

SPLITS = (512, 128, 128, 128, 128, 128, 128, 24, 512, 128, 512, 64, 8, 2048)
NAMES = ("q_n", "kc", "vc", "ks", "vs", "kw", "vw", "g_n", "q_d", "ckv", "qi", "ki", "wi", "g_m")
CHUNKS = (("qi",), ("kc", "ks", "kw", "ki", "g_n", "wi"), ("ckv", "vc", "vs", "vw"), ("q_d",), ("q_n",))
START = dict(zip(NAMES, np.cumsum((0,) + SPLITS[:-1]).tolist()))
SIZE = dict(zip(NAMES, SPLITS))
CHUNK_COLS = [sum(SIZE[n] for n in c) for c in CHUNKS]
CHUNK_AT = [sum(CHUNK_COLS[:i]) for i in range(len(CHUNKS))]

CAND = [(a, b) for a in range(TOPK) for b in range(TOPK) if (a + 1) * (b + 1) <= TOPK]
NCAND = len(CAND)
CAND_ROWS = [(a, TOPK // (a + 1)) for a in range(TOPK // 2)]

TAB = {}
_at = 0
for _n, _w in (("ident", P), ("cmask", T), ("iota", P), ("cos", TT * HALF), ("sin", TT * 2 * HALF),
               ("cmp_add", TT * NCMP), ("cmp_mul", TT * NCMP), ("bmask", HEADS), ("pos", NCAND)):
    TAB[_n] = (_at, _at + _w)
    _at += _w
TAB_W = _at

PAR = {}
_at = 0
for _n, _w in (("c", KT), ("ada_b", 6 * KT), ("g1", KT), ("g2", KT), ("gf", KT), ("kvg", 1)):
    PAR[_n] = (_at, _at + _w)
    _at += _w
PAR_W = _at

FILL = []
for _i in range(4):
    FILL += [("gate", 4 * _i + j) for j in range(4)] + [("ada", 4 + 2 * _i + j) for j in range(2)]
LOADS = [("ada", m) for m in range(4)] + [("win", m) for m in range(len(CHUNKS))]
for _i in range(4):
    LOADS += [("gate", _i), ("ada", 4 + 2 * _i), ("ada", 5 + 2 * _i)]
LOADS += [("br", 0), ("br", 1), ("out", 0), ("out", 1), ("wq", 0), ("wq", 1)]
WSLOTS = 4
WCOLS = KT * 512

QI, QD, QN = 0, 8, 16
KC, KS, KW, KI, VC, KD = 0, 2, 4, 6, 7, 9
ROPES = [(0, 0), (0, 1), (1, 0), (1, 1), (3, 0), (3, 1), ("kd", 0), ("kd", 1), (4, 0), (4, 1)]
ROPE_HEADS = {0: 8, 1: 7, 3: 8, 4: 8, "kd": 1}


def transpose_jobs():
    jobs = []

    def heads(r):
        c, tt = ROPES[r]
        dst, first = {0: ("q", QI), 3: ("q", QD), 4: ("q", QN), 1: ("k", KC), "kd": ("k", KD)}[c]
        n = ROPE_HEADS[c]
        for h in range(0, n, 4):
            jobs.append(("rope", r, h, min(4, n - h), dst, first + h, tt))

    for r in (0, 1, 2, 3):
        heads(r)
    for tt in range(TT):
        jobs.append(("ckv", tt))
    for tt in range(TT):
        jobs.append(("kdvd", tt))
    for r in (4, 5, 6, 7, 8, 9):
        heads(r)
    return jobs


JOBS = transpose_jobs()
BRANCHES = (("slc", QN, KS, 1), ("win", QN, KW, 2), ("dsa", QD, KD, None))
UNITS = [(b, tt, hp) for b in range(3) for tt in range(TT) for hp in range(HEADS // 2)]
GROUPS = len(UNITS) // 4

TOK_LOOP = 8
SLOTS = 4


def build(nc, A, out):
    with ExitStack() as ctx:
        def sb(name, cols, parts=P):
            return ctx.enter_context(nc.sbuf_tensor(name, [parts, cols], F32))

        def sem(name):
            return ctx.enter_context(nc.semaphore(name))

        arena = sb("arena", KEYS * T)
        experts = sb("experts", 2 * SLOTS * D)
        xT = sb("xT", KT * T)
        h2T = sb("h2T", KT * T)
        oneh = sb("oneh", 2 * TOK_LOOP * P)
        tab = sb("tab", TAB_W)
        par = sb("par", PAR_W)
        skT = sb("skT", HEADS * KEYS)
        mod = sb("mod", 6 * KT)
        scale1 = sb("scale1", KT)
        scale2 = sb("scale2", KT)
        silu = sb("silu", 3 * KT)
        ones = sb("ones", P)
        eps = sb("eps", 1)
        rstd = sb("rstd", T)
        ssig = sb("ssig", TT * 24)
        wis = sb("wis", TT * HEADS)
        small = sb("small", 64)
        rowmax = sb("rowmax", 4)
        negmax = sb("negmax", 4)
        rowsum = sb("rowsum", GROUPS * HEADS)
        recip = sb("recip", 2 * HEADS)
        best8 = sb("best8", 8)
        wukv = sb("wukv", 2 * DH)
        w2kv = sb("w2kv", 2 * DH, DH)
        posT = sb("posT", CMP_LEN, DH)
        gel = sb("gel", 2 * T)
        prod = sb("prod", 2 * T)
        routeT = sb("routeT", 3 * T)

        def table(name):
            return tab[:, TAB[name][0]:TAB[name][1]]

        def param(name):
            return par[:, PAR[name][0]:PAR[name][1]]

        ident = table("ident")
        wslot = [arena[:, s * WCOLS:(s + 1) * WCOLS] for s in range(WSLOTS)]
        at = WSLOTS * WCOLS
        hT = arena[:, at:at + KT * T].rearrange("p (k t) -> p k t", k=KT)
        at += KT * T
        qT_at = at
        qT = arena[0:DH, at:at + 24 * T].rearrange("p (h t) -> p h t", h=24)
        oT = arena[:, at:at + 8 * T].rearrange("p (b k t) -> p b k t", b=2, k=4)
        at += 24 * T
        kT = arena[0:DH, at:at + 10 * T].rearrange("p (h t) -> p h t", h=10)
        at += 10 * T
        gates = arena[:, at:at + 16 * T].rearrange("p (m t) -> p m t", m=16)
        at += 16 * T
        blk = arena[0:DH, at - 16 * T:at - 16 * T + 2 * CMP_LEN * 2 * NCMP].rearrange(
            "p (v l n) -> p v l n", v=2, l=CMP_LEN)
        ckvT = arena[:, at:at + T]
        kdv = arena[:, at + T:at + 2 * T].rearrange("p (a n) -> p a n", a=TT)
        at += 2 * T
        assert at <= KEYS * T

        q2T = arena[:, WSLOTS * WCOLS + KT * T + 24 * T:][:, 0:KT * T].rearrange("p (h t) -> p h t", h=8)
        sub = [arena[:, qT_at + i * 2048:qT_at + (i + 1) * 2048].rearrange("p (s n) -> p s n", n=KEYS)
               for i in range(TT)]
        eqbuf = arena[:, 0:HEADS * TOPK * NCAND]
        tk = arena[:, 8192:16384]

        w1k = experts[0:DH, 0:2048].rearrange("p (l e) -> p l e", l=CMP_LEN)
        w1v = experts[0:DH, 2048:4096].rearrange("p (l e) -> p l e", l=CMP_LEN)
        ssb = [experts[:, i * 512:(i + 1) * 512] for i in range(2)]
        pT = [experts[:, 1024 + i * 512:1024 + (i + 1) * 512] for i in range(2)]
        zv = experts[:, 4096:5120].rearrange("p (a n) -> p a n", a=TT)
        zk = experts[:, 5120:5184].rearrange("p (a n) -> p a n", a=TT)
        rope_a = experts[:, 5184:5696]
        rope_b = experts[:, 5696:6208]
        rq = [experts[:, 6208 + i * 512:6208 + (i + 1) * 512] for i in range(2)]
        hid = experts[0:DH, 7232:7232 + 6 * 60]
        hidrep = experts[0:DH, 7600:7720]
        kcmpT = experts[0:DH, 7720:7750]
        vbd = experts[:, 5184:5696]
        pc = experts[:, 5696:5936].rearrange("p (a n) -> p a n", a=TT)
        pcT = [experts[:, 5952 + i * 128:5952 + (i + 1) * 128] for i in range(2)]
        otmp = experts[:, 6208:6720]
        csum = experts[:, 7232 + 360:7232 + 368]

        relu = [h2T[:, i * 512:(i + 1) * 512] for i in range(2)]
        score = h2T[:, 1024:1536].rearrange("p (a n) -> p a n", a=TT)
        work = h2T[:, 1536:2048].rearrange("p (a n) -> p a n", a=TT)
        o_nsa = [oneh[:, i * 512:(i + 1) * 512] for i in range(2)]
        o_dsa = [oneh[:, 1024 + i * 512:1024 + (i + 1) * 512] for i in range(2)]
        x3 = xT[:, :].rearrange("p (k t) -> p k t", k=KT)
        h2 = h2T[:, :].rearrange("p (k t) -> p k t", k=KT)
        G = arena[:, :].rearrange("p (t i) -> p t i", i=KEYS)
        ut = [experts[:, s * D:(s + 1) * D].rearrange("p (k j) -> p k j", k=KT) for s in range(SLOTS)]
        vt = [experts[:, (SLOTS + s) * D:(SLOTS + s + 1) * D] for s in range(SLOTS)]
        ohj = [oneh[:, s * P:(s + 1) * P] for s in range(TOK_LOOP)]
        ohi = [oneh[:, (TOK_LOOP + s) * P:(TOK_LOOP + s + 1) * P] for s in range(TOK_LOOP)]

        B = [ctx.enter_context(nc.psum_tensor(f"bank{i}", [P, 512], F32)) for i in range(8)]

        par_in, x_in, tab_in, sk_in = sem("par_in"), sem("x_in"), sem("tab_in"), sem("sk_in")
        w1_in, w2_in, out_done = sem("w1_in"), sem("w2_in"), sem("out_done")
        w_in = [sem(f"w_in{s}") for s in range(WSLOTS)]
        u_in = [sem(f"u_in{s}") for s in range(SLOTS)]
        v_in = [sem(f"v_in{s}") for s in range(SLOTS)]
        const_set, dve_step, act_step = sem("const_set"), sem("dve_step"), sem("act_step")
        cexp, silu_ready, sq_ready, ssq_ready = sem("cexp"), sem("silu_ready"), sem("sq_ready"), sem("ssq_ready")
        root_ready, h_ready, ada_done = sem("root_ready"), sem("h_ready"), sem("ada_done")
        z_done, z_read, zv_ready, zk_ready = sem("z_done"), sem("z_read"), sem("zv_ready"), sem("zk_ready")
        roped, job_done, job_out = sem("roped"), sem("job_done"), sem("job_out")
        ck_sum, ck_root, ck_ready = sem("ck_sum"), sem("ck_root"), sem("ck_ready")
        gexp = sem("gexp")
        logit_done, relu_done, relu_used = sem("logit_done"), sem("relu_done"), sem("relu_used")
        blk_ready, hid_done, hid_in, tanh_done = sem("blk_ready"), sem("hid_done"), sem("hid_in"), sem("tanh_done")
        hid_ready, cmpkv_done, cmpkv_ready = sem("hid_ready"), sem("cmpkv_done"), sem("cmpkv_ready")
        cs_done, cs_in, cexp_done, pc_ready = sem("cs_done"), sem("cs_in"), sem("cexp_done"), sem("pc_ready")
        pct_done, pct_ready, oc_done, oc_read = sem("pct_done"), sem("pct_ready"), sem("oc_done"), sem("oc_read")
        s_done, s_masked, p_ready, pt_done = sem("s_done"), sem("s_masked"), sem("p_ready"), sem("pt_done")
        pt_ready, o_unit, o_read = sem("pt_ready"), sem("o_unit"), sem("o_read")
        fill_done, fill_out = sem("fill_done"), sem("fill_out")
        o_ready, ot_done, ot_ready = sem("o_ready"), sem("ot_done"), sem("ot_ready")
        gates_ready, br_done, merged_ready = sem("gates_ready"), sem("br_done"), sem("merged_ready")
        mo_done, x1_ready, sq2_ready = sem("mo_done"), sem("x1_ready"), sem("sq2_ready")
        ssq2_ready, root2_ready, h2_ready = sem("ssq2_ready"), sem("root2_ready"), sem("h2_ready")
        q2_done, q2_ready, sub_done, sub_ready = sem("q2_done"), sem("q2_ready"), sem("sub_done"), sem("sub_ready")
        top_ready, gate_exp, route_ready = sem("top_ready"), sem("gate_exp"), sem("route_ready")
        rt_done, rt_ready = sem("rt_done"), sem("rt_ready")
        oh_ready, g_done, g_out = sem("oh_ready"), sem("g_done"), sem("g_out")
        act_done, gelu_done, prod_ready, v_done = sem("act_done"), sem("gelu_done"), sem("prod_ready"), sem("v_done")
        x2_ready, sq3_ready, ssq3_ready, root3_ready = sem("x2_ready"), sem("sq3_ready"), sem("ssq3_ready"), sem("root3_ready")
        y_ready = sem("y_ready")

        def w_loaded(eng, n):
            eng.wait_ge(w_in[n % WSLOTS], 16 * (n // WSLOTS + 1))

        block = ctx.enter_context(nc.Block())

        @block.sync
        def _(sp):
            sp.dma_start(par[:, :], A["par"]).then_inc(par_in, 16)
            sp.dma_start(x3, A["x"].rearrange("(k p) t -> p k t", p=P)).then_inc(x_in, 16)
            split = {"ada": A["ada_w"], "win": A["w_in"], "gate": A["w_gate"], "out": A["w_out"], "wq": A["peer_wq"]}
            for n, (kind, m) in enumerate(LOADS):
                if n >= WSLOTS:
                    old, i = LOADS[n - WSLOTS]
                    sp.wait_ge(*{"ada": (ada_done, i + 1), "win": (z_done, 2 * i + 2), "gate": (fill_done, 4 * i + 4),
                                 "br": (br_done, KT), "out": (mo_done, 4 * i + 4)}[old])
                slot = wslot[n % WSLOTS]
                if kind == "br":
                    src = A["w_br"][m].rearrange("(k p) n -> p k n", p=P)
                    dst = slot.rearrange("p (k n) -> p k n", k=4)
                else:
                    first, cols = (CHUNK_AT[m], CHUNK_COLS[m]) if kind == "win" else (512 * m, 512)
                    src = split[kind].rearrange("(k p) n -> p k n", p=P)[:, :, first:first + cols]
                    dst = slot.rearrange("p (k n) -> p k n", k=KT)[:, :, 0:cols]
                sp.dma_start(dst, src).then_inc(w_in[n % WSLOTS], 16)
            sp.wait_ge(ot_ready, 4)
            for i in range(SLOTS):
                sp.dma_start(ut[i], A["uT"][i]).then_inc(u_in[i], 16)
                sp.dma_start(vt[i], A["v"][i]).then_inc(v_in[i], 16)
            with sp.Fori(1, KEYS // SLOTS) as turn:
                for s in range(SLOTS):
                    sp.wait_ge(act_done, turn * SLOTS + (s + 1 - SLOTS))
                    sp.dma_start(ut[s], A["uT"][bass.ds(turn * SLOTS + s, 1)].rearrange("a p k j -> p (a k) j")).then_inc(u_in[s], 16)
                    sp.wait_ge(v_done, turn * SLOTS + (s + 1 - SLOTS))
                    sp.dma_start(vt[s], A["v"][bass.ds(turn * SLOTS + s, 1)].rearrange("a p d -> p (a d)")).then_inc(v_in[s], 16)
            for m in range(KT):
                sp.wait_ge(y_ready, m + 1)
                sp.dma_start(out[m * P:(m + 1) * P, :], h2[:, m, :]).then_inc(out_done, 16)
            sp.wait_ge(out_done, 16 * KT)

        @block.tensor
        def _(pe):
            nth = [0]

            def chunk():
                n = nth[0]
                nth[0] += 1
                w_loaded(pe, n)
                return wslot[n % WSLOTS]

            def ada(m, slot):
                w = slot.rearrange("p (k n) -> p k n", k=KT)
                for c in range(4):
                    for k in range(KT):
                        last = nc.tensor.matmul(B[7][:, 4 * m + c:4 * m + c + 1], w[:, k, c * P:(c + 1) * P],
                                                silu[:, k:k + 1], start=(k == 0), stop=(k == KT - 1))
                return last

            def square_sum(bank, src, ready, done):
                for k in range(KT):
                    pe.wait_ge(ready, k + 1)
                    last = nc.tensor.matmul(B[bank][:, 0:T], ones[:, :], src[:, k, :], start=(k == 0), stop=(k == KT - 1))
                last.then_inc(done, 1)

            pe.wait_ge(const_set, 1)
            square_sum(0, h2, sq_ready, ssq_ready)
            pe.wait_ge(silu_ready, 1)
            for m in range(4):
                ada(m, chunk()).then_inc(ada_done, 1)

            def project(c, pos):
                w = chunk().rearrange("p (k n) -> p k n", k=KT)
                for tt in range(TT):
                    n = 2 * pos + tt
                    if c == 0 and tt == 0:
                        pe.wait_ge(h_ready, KT)
                    if pos in (2, 3):
                        pe.wait_ge(z_read, n - 3)
                    if pos == 4:
                        pe.wait_ge(zv_ready, tt + 1)
                    for k in range(KT):
                        last = nc.tensor.matmul(B[n % 4][:, 0:CHUNK_COLS[c]], hT[:, k, tt * P:(tt + 1) * P],
                                                w[:, k, 0:CHUNK_COLS[c]], start=(k == 0), stop=(k == KT - 1))
                    last.then_inc(z_done, 1)

            def job(n):
                kind, *what = JOBS[n]
                bank = B[4 + n % 3]
                if n >= 3:
                    pe.wait_ge(job_out, n - 2)
                if kind == "rope":
                    r, h, count, _, _, _ = what
                    pe.wait_ge(roped, r + 1)
                    for i in range(count):
                        last = nc.tensor.transpose(bank[0:DH, i * P:(i + 1) * P],
                                                   rq[r % 2][:, (h + i) * DH:(h + i + 1) * DH], ident)
                elif kind == "ckv":
                    tt, = what
                    pe.wait_ge(ck_ready, tt + 1)
                    nc.tensor.transpose(bank[:, 0:P], zv[:, tt, 0:P], ident)
                    for g in range(2):
                        last = nc.tensor.transpose(bank[0:DH, (1 + g) * P:(2 + g) * P],
                                                   zv[:, tt, P + g * DH:P + (g + 1) * DH], ident)
                else:
                    tt, = what
                    pe.wait_ge(job_out, n - 1)
                    last = nc.tensor.matmul(bank[:, 0:2 * DH], ckvT[:, tt * P:(tt + 1) * P], wukv[:, :], start=True, stop=True)
                last.then_inc(job_done, 1)

            pe.wait_ge(tab_in, 16)
            project(0, 0)
            project(1, 1)
            for n in range(0, 4):
                job(n)
            project(2, 2)
            for n in range(4, 8):
                job(n)
            project(3, 3)
            job(8)
            job(9)
            project(4, 4)
            pe.wait_ge(w2_in, 48)
            for n in range(10, len(JOBS)):
                job(n)

            for q in range(8):
                tt, hp = divmod(q, 4)
                ns = (tt + 1) * P
                if q == 0:
                    pe.wait_ge(job_out, len(JOBS))
                    pe.wait_ge(z_read, 10 - 2)
                if q >= 4:
                    pe.wait_ge(relu_done, q - 3)
                for i in range(2):
                    last = nc.tensor.matmul(B[q % 4][:, i * ns:(i + 1) * ns], qT[:, QI + 2 * hp + i, tt * P:(tt + 1) * P],
                                            kT[:, KI, 0:ns], start=True, stop=True)
                last.then_inc(logit_done, 1)

            pe.wait_ge(w1_in, 32)
            pe.wait_ge(blk_ready, 1)
            for v, w1 in enumerate((w1k, w1v)):
                for l in range(CMP_LEN):
                    last = nc.tensor.matmul(B[4 + v][0:DH, 0:2 * NCMP], w1[:, l, :], blk[:, v, l, :],
                                            start=(l == 0), stop=(l == CMP_LEN - 1))
            last.then_inc(hid_done, 1)
            pe.wait_ge(hid_ready, 1)
            nc.tensor.matmul(B[6][0:DH, 0:2 * NCMP], w2kv[:, 0:DH], hid[:, 300:330], start=True, stop=True)
            nc.tensor.matmul(B[6][0:HEADS * NCMP, 64:64 + DH], hidrep, w2kv[:, DH:2 * DH], start=True, stop=True).then_inc(cmpkv_done, 1)
            pe.wait_ge(cmpkv_ready, 2)
            pe.wait_ge(relu_done, 8)
            for tt in range(TT):
                for h in range(HEADS):
                    last = nc.tensor.matmul(B[tt][:, h * NCMP:(h + 1) * NCMP], qT[:, QN + h, tt * P:(tt + 1) * P],
                                            kcmpT[:, (h // 4) * NCMP:(h // 4 + 1) * NCMP], start=True, stop=True)
                last.then_inc(cs_done, 1)
            for tt in range(TT):
                pe.wait_ge(pc_ready, tt + 1)
                nc.tensor.transpose(B[2 + tt][0:HEADS * NCMP, 0:P], pc[:, tt, :], ident).then_inc(pct_done, 1)
            for tt in range(TT):
                pe.wait_ge(pct_ready, tt + 1)
                nc.tensor.matmul(B[4 + tt][:, :], pcT[tt][0:HEADS * NCMP, :], vbd[0:HEADS * NCMP, :],
                                 start=True, stop=True).then_inc(oc_done, 1)

            slot = None
            for u in range(len(UNITS) + 2):
                if u < len(UNITS):
                    b, tt, hp = UNITS[u]
                    ns = (tt + 1) * P
                    _, q0, k0, _ = BRANCHES[b]
                    if u >= 2:
                        pe.wait_ge(s_masked, u - 1)
                    for i in range(2):
                        h = 2 * hp + i
                        kh = k0 if b == 2 else k0 + h // 4
                        last = nc.tensor.matmul(B[u % 2][:, i * ns:(i + 1) * ns], qT[:, q0 + h, tt * P:(tt + 1) * P],
                                                kT[:, kh, 0:ns], start=True, stop=True)
                    last.then_inc(s_done, 1)
                    kind, m = FILL[u]
                    if kind == "ada":
                        ada(m, chunk()).then_inc(ada_done, 1)
                    else:
                        if m % 4 == 0:
                            slot = chunk().rearrange("p (k n) -> p k n", k=KT)
                        if m:
                            pe.wait_ge(fill_out, m)
                        for k in range(KT):
                            last = nc.tensor.matmul(B[6][:, 0:T], slot[:, k, (m % 4) * P:(m % 4 + 1) * P], hT[:, k, :],
                                                    start=(k == 0), stop=(k == KT - 1))
                        last.then_inc(fill_done, 1)
                if 0 <= u - 1 < len(UNITS):
                    b, tt, hp = UNITS[u - 1]
                    ns = (tt + 1) * P
                    pe.wait_ge(p_ready, u)
                    if u - 1 >= 2:
                        pe.wait_ge(pt_ready, u - 2)
                    for i in range(2):
                        for s in range(tt + 1):
                            last = nc.tensor.transpose(B[2 + (u - 1) % 2][:, (i * (tt + 1) + s) * P:(i * (tt + 1) + s + 1) * P],
                                                       ssb[(u - 1) % 2][:, i * ns + s * P:i * ns + (s + 1) * P], ident)
                    last.then_inc(pt_done, 1)
                if u - 2 >= 0:
                    b, tt, hp = UNITS[u - 2]
                    g = (u - 2) // 4
                    pe.wait_ge(pt_ready, u - 1)
                    if hp == 0:
                        if g < 2:
                            pe.wait_ge(oc_read, g + 1)
                        else:
                            pe.wait_ge(o_read, g - 1)
                    for i in range(2):
                        h = 2 * hp + i
                        for s in range(tt + 1):
                            if b == 2:
                                v = kdv[:, s, DH:2 * DH]
                            else:
                                first = (2 + b) * P + (h // 4) * DH
                                v = zv[:, s, first:first + DH]
                            last = nc.tensor.matmul(B[4 + g % 2][:, h * DH:(h + 1) * DH],
                                                    pT[(u - 2) % 2][:, (i * (tt + 1) + s) * P:(i * (tt + 1) + s + 1) * P],
                                                    v, start=(s == 0), stop=(s == tt))
                    last.then_inc(o_unit, 1)

            for n in range(4):
                b, tt = divmod(n, 2)
                pe.wait_ge(o_ready, 1)
                src = (o_nsa, o_dsa)[b][tt]
                for k in range(4):
                    last = nc.tensor.transpose(B[n][:, k * P:(k + 1) * P], src[:, k * P:(k + 1) * P], ident)
                last.then_inc(ot_done, 1)
            wb = [chunk().rearrange("p (k n) -> p k n", k=4) for _ in range(2)]
            pe.wait_ge(ot_ready, 4)
            for m in range(KT):
                if m >= 2:
                    pe.wait_ge(merged_ready, m - 1)
                for b in range(2):
                    for k in range(4):
                        last = nc.tensor.matmul(B[4 + m % 2][:, b * T:(b + 1) * T], wb[b][:, k, m * P:(m + 1) * P],
                                                oT[:, b, k, :], start=(k == 0), stop=(k == 3))
                last.then_inc(br_done, 1)
            pe.wait_ge(merged_ready, KT)
            for m in range(KT):
                if m % 4 == 0:
                    w = chunk().rearrange("p (k n) -> p k n", k=KT)
                if m >= 2:
                    pe.wait_ge(x1_ready, m - 1)
                for k in range(KT):
                    last = nc.tensor.matmul(B[m % 2][:, 0:T], w[:, k, (m % 4) * P:(m % 4 + 1) * P], hT[:, k, :],
                                            start=(k == 0), stop=(k == KT - 1))
                last.then_inc(mo_done, 1)
            square_sum(2, arena[:, 16384:18432].rearrange("p (k t) -> p k t", k=KT), sq2_ready, ssq2_ready)
            pe.wait_ge(h2_ready, KT)
            for m in range(KT):
                if m % 4 == 0:
                    w = chunk().rearrange("p (k n) -> p k n", k=KT)
                if m >= 2:
                    pe.wait_ge(q2_ready, m - 1)
                for k in range(KT):
                    last = nc.tensor.matmul(B[m % 2][:, 0:T], w[:, k, (m % 4) * P:(m % 4 + 1) * P], h2[:, k, :],
                                            start=(k == 0), stop=(k == KT - 1))
                last.then_inc(q2_done, 1)
            pe.wait_ge(q2_ready, KT)
            pe.wait_ge(sk_in, 16)
            for n in range(8):
                tt, hq, c = n // 4, n // 2 % 2, n % 2
                if n >= 4:
                    pe.wait_ge(sub_ready, n - 3)
                for i in range(4):
                    h = 4 * hq + i
                    last = nc.tensor.matmul(B[4 + n % 4][:, i * KEYS:(i + 1) * KEYS], q2T[c * DH:(c + 1) * DH, h, tt * P:(tt + 1) * P],
                                            skT[c * DH:(c + 1) * DH, h * KEYS:(h + 1) * KEYS], start=True, stop=True)
                last.then_inc(sub_done, 1)
            for tt in range(TT):
                pe.wait_ge(route_ready, tt + 1)
                for i in range(3):
                    last = nc.tensor.transpose(B[tt][:, i * P:(i + 1) * P], tk[:, 6000 + (3 * tt + i) * P:6000 + (3 * tt + i + 1) * P], ident)
                last.then_inc(rt_done, 1)

            pe.wait_ge(rt_ready, TT)

            def route_products(turn, first=False):
                for half in range(2):
                    pe.wait_ge(oh_ready, turn * 2 + (half + 1))
                    if not first:
                        pe.wait_ge(g_out, turn * 2 + (half - 1))
                    for i in range(4):
                        s = 4 * half + i
                        last = nc.tensor.matmul(B[2 + half][:, i * KEYS:(i + 1) * KEYS], ohj[s], ohi[s], start=True, stop=True)
                    last.then_inc(g_done, 1)

            route_products(0, first=True)
            with pe.Fori(1, T // TOK_LOOP) as turn:
                route_products(turn)

            def act_tile(s):
                for k in range(KT):
                    last = nc.tensor.matmul(B[4 + s % 2][:, 0:T], ut[s][:, k, :], h2[:, k, :], start=(k == 0), stop=(k == KT - 1))
                last.then_inc(act_done, 1)

            def v_tile(s, first=False, final=False):
                for m in range(KT):
                    last = nc.tensor.matmul(B[m // 2][:, (m % 2) * T:(m % 2 + 1) * T], vt[s][:, m * P:(m + 1) * P],
                                            prod[:, (s % 2) * T:(s % 2 + 1) * T], start=(first and m % 2 == 0), stop=final,
                                            skip_group_check=True)
                last.then_inc(v_done, 1)

            pe.wait_ge(g_out, 2 * (T // TOK_LOOP))
            pe.wait_ge(u_in[0], 16)
            act_tile(0)
            for s in range(SLOTS):
                pe.wait_ge(u_in[(s + 1) % SLOTS], 16 * (1 + (s + 1) // SLOTS))
                if s >= 1:
                    pe.wait_ge(gelu_done, s)
                act_tile((s + 1) % SLOTS)
                pe.wait_ge(prod_ready, s + 1)
                pe.wait_ge(v_in[s], 16)
                v_tile(s, first=(s == 0))
            with pe.Fori(1, KEYS // SLOTS - 1) as turn:
                for s in range(SLOTS):
                    pe.wait_ge(u_in[(s + 1) % SLOTS], turn * 16 + 16 * (1 + (s + 1) // SLOTS))
                    pe.wait_ge(gelu_done, turn * SLOTS + s)
                    act_tile((s + 1) % SLOTS)
                    pe.wait_ge(prod_ready, turn * SLOTS + (s + 1))
                    pe.wait_ge(v_in[s], turn * 16 + 16)
                    v_tile(s)
            base = KEYS - SLOTS
            for s in range(SLOTS):
                if s < SLOTS - 1:
                    pe.wait_ge(u_in[s + 1], 16 * (KEYS // SLOTS))
                    pe.wait_ge(gelu_done, base + s)
                    act_tile(s + 1)
                pe.wait_ge(prod_ready, base + s + 1)
                pe.wait_ge(v_in[s], 16 * (KEYS // SLOTS))
                v_tile(s, final=(s == SLOTS - 1))
            square_sum(6, arena[:, 0:2048].rearrange("p (k t) -> p k t", k=KT), sq3_ready, ssq3_ready)

        @block.scalar
        def _(act):
            steps = [0]

            def link(ins):
                steps[0] += 1
                ins.then_inc(act_step, 1)
                act.wait_ge(act_step, steps[0])

            act.dma_start(tab[:, :], A["tab"]).then_inc(tab_in, 16)
            act.dma_start(wukv[:, :], A["w_ukv"]).then_inc(w2_in, 16)
            act.dma_start(w2kv[:, :], A["cmp_w2"]).then_inc(w2_in, 16)
            act.dma_start(posT[:, :], A["cmp_pos"]).then_inc(w2_in, 16)
            act.dma_start(w1k, A["cmp_w1_k"]).then_inc(w1_in, 16)
            act.dma_start(w1v, A["cmp_w1_v"]).then_inc(w1_in, 16)
            act.dma_start(skT[:, :], A["subkeys"]).then_inc(sk_in, 16)
            act.wait_ge(par_in, 16)
            nc.scalar.activation(silu[:, KT:2 * KT], param("c"), ACT.Exp, scale=-1.0).then_inc(cexp, 1)
            act.wait_ge(x_in, 16)
            for k in range(KT):
                nc.scalar.activation(h2[:, k, :], x3[:, k, :], ACT.Square).then_inc(sq_ready, 1)
            act.wait_ge(const_set, 1)
            act.wait_ge(ssq_ready, 1)
            nc.scalar.activation(rstd[:, :], B[0][:, 0:T], ACT.Sqrt, bias=eps[:, 0:1], scale=1.0 / D).then_inc(root_ready, 1)

            def job_copy(n):
                kind, *what = JOBS[n]
                bank = B[4 + n % 3]
                act.wait_ge(job_done, n + 1)
                if kind == "rope":
                    r, _, count, to, head, tt = what
                    dst = (qT if to == "q" else kT)[:, head:head + count, tt * P:(tt + 1) * P]
                    last = nc.scalar.activation(dst, bank[0:DH, 0:count * P].rearrange("p (h t) -> p h t", h=count), ACT.Copy)
                elif kind == "ckv":
                    tt, = what
                    nc.scalar.activation(kT[:, VC:VC + 2, tt * P:(tt + 1) * P],
                                         bank[0:DH, P:3 * P].rearrange("p (h t) -> p h t", h=2), ACT.Copy)
                    last = nc.scalar.activation(ckvT[:, tt * P:(tt + 1) * P], bank[:, 0:P], ACT.Identity, scale=param("kvg"))
                else:
                    tt, = what
                    last = nc.scalar.activation(kdv[:, tt, :], bank[:, 0:2 * DH], ACT.Copy)
                last.then_inc(job_out, 1)

            for n in range(0, 4):
                job_copy(n)
            for tt in range(TT):
                act.wait_ge(z_done, 4 + tt + 1)
                nc.scalar.activation(zv[:, tt, :], B[tt][:, :], ACT.Copy).then_inc(zv_ready, 1)
            for n in range(4, 8):
                job_copy(n)
            for tt in range(TT):
                act.wait_ge(ck_sum, tt + 1)
                nc.scalar.activation(small[:, 2 + tt:3 + tt], small[:, tt:tt + 1], ACT.Sqrt,
                                     bias=eps[:, 0:1], scale=1.0 / P).then_inc(ck_root, 1)
            for n in range(8, len(JOBS)):
                job_copy(n)

            act.wait_ge(zk_ready, 2)
            nc.scalar.activation(ssig[:, :].rearrange("p (a n) -> p a n", a=TT), zk[:, :, 0:24], ACT.Exp, scale=-1.0).then_inc(gexp, 1)
            for q in range(8):
                ns = (q // 4 + 1) * P
                act.wait_ge(logit_done, q + 1)
                if q >= 2:
                    act.wait_ge(relu_used, q - 1)
                nc.scalar.activation(relu[q % 2][:, 0:2 * ns], B[q % 4][:, 0:2 * ns], ACT.Relu, scale=DH ** -0.5).then_inc(relu_done, 1)
            act.wait_ge(hid_in, 1)
            nc.scalar.activation(hid[:, 120:180], hid[:, 120:180], ACT.Tanh, scale=float(np.sqrt(2.0 / np.pi))).then_inc(tanh_done, 1)
            for tt in range(TT):
                act.wait_ge(cs_in, tt + 1)
                nc.scalar.activation(pc[:, tt, :], pc[:, tt, :], ACT.Exp, scale=DH ** -0.5).then_inc(cexp_done, 1)
            for tt in range(TT):
                act.wait_ge(pct_done, tt + 1)
                nc.scalar.activation(pcT[tt][0:HEADS * NCMP, :], B[2 + tt][0:HEADS * NCMP, 0:P], ACT.Copy).then_inc(pct_ready, 1)

            for u in range(len(UNITS) + 1):
                if u < len(UNITS):
                    b, tt, hp = UNITS[u]
                    ns = (tt + 1) * P
                    act.wait_ge(s_masked, u + 1)
                    for i in range(2):
                        last = nc.scalar.activation(ssb[u % 2][:, i * ns:(i + 1) * ns], ssb[u % 2][:, i * ns:(i + 1) * ns], ACT.Exp,
                                                    bias=negmax[:, 2 * (u % 2) + i:2 * (u % 2) + i + 1],
                                                    accum_out=rowsum[:, 2 * u + i:2 * u + i + 1])
                    last.then_inc(p_ready, 1)
                if u >= 1:
                    tt = UNITS[u - 1][1]
                    n = 2 * (tt + 1) * P
                    act.wait_ge(pt_done, u)
                    if u - 1 >= 2:
                        act.wait_ge(o_unit, u - 2)
                    nc.scalar.activation(pT[(u - 1) % 2][:, 0:n], B[2 + (u - 1) % 2][:, 0:n], ACT.Copy).then_inc(pt_ready, 1)
                if u < len(UNITS):
                    kind, m = FILL[u]
                    if kind == "gate":
                        act.wait_ge(fill_done, m + 1)
                        if m == 0:
                            act.wait_ge(hid_done, 1)
                        nc.scalar.activation(gates[:, m, :], B[6][:, 0:T], ACT.Exp, scale=-1.0).then_inc(fill_out, 1)
            for n in range(4):
                b, tt = divmod(n, 2)
                act.wait_ge(ot_done, n + 1)
                nc.scalar.activation(oT[:, b, :, tt * P:(tt + 1) * P], B[n][:, :].rearrange("p (k t) -> p k t", k=4),
                                     ACT.Copy).then_inc(ot_ready, 1)
            sq2 = arena[:, 16384:18432].rearrange("p (k t) -> p k t", k=KT)
            act.wait_ge(mo_done, KT)
            for k in range(KT):
                act.wait_ge(x1_ready, k + 1)
                nc.scalar.activation(sq2[:, k, :], x3[:, k, :], ACT.Square).then_inc(sq2_ready, 1)
            act.wait_ge(ssq2_ready, 1)
            nc.scalar.activation(rstd[:, :], B[2][:, 0:T], ACT.Sqrt, bias=eps[:, 0:1], scale=1.0 / D).then_inc(root2_ready, 1)
            for m in range(KT):
                act.wait_ge(q2_done, m + 1)
                nc.scalar.activation(q2T[:, m, :], B[m % 2][:, 0:T], ACT.Copy).then_inc(q2_ready, 1)
            for n in range(8):
                tt, hq, c = n // 4, n // 2 % 2, n % 2
                act.wait_ge(sub_done, n + 1)
                nc.scalar.activation(sub[tt].rearrange("p (h c) n -> p h c n", c=2)[:, 4 * hq:4 * hq + 4, c, :], B[4 + n % 4][:, :].rearrange("p (s n) -> p s n", s=4),
                                     ACT.Copy).then_inc(sub_ready, 1)
            for tt in range(TT):
                act.wait_ge(top_ready, tt + 1)
                w = tk[:, 6000 + (3 * tt + 2) * P:6000 + (3 * tt + 3) * P]
                nc.scalar.activation(w, w, ACT.Exp).then_inc(gate_exp, 1)
            for tt in range(TT):
                act.wait_ge(rt_done, tt + 1)
                nc.scalar.activation(routeT[:, :].rearrange("p (i t) -> p i t", i=3)[:, :, tt * P:(tt + 1) * P],
                                     B[tt][:, 0:3 * P].rearrange("p (i t) -> p i t", i=3), ACT.Copy).then_inc(rt_ready, 1)
            with act.Fori(0, T // TOK_LOOP) as turn:
                for half in range(2):
                    act.wait_ge(g_done, turn * 2 + (half + 1))
                    nc.scalar.activation(G[:, bass.ds(turn * TOK_LOOP + 4 * half, 4), :],
                                         B[2 + half][:, :].rearrange("p (t i) -> p t i", t=4), ACT.Copy).then_inc(g_out, 1)
            def gelu(turn, first=False):
                for s in range(2):
                    act.wait_ge(act_done, turn * 2 + (s + 1))
                    if not first:
                        act.wait_ge(prod_ready, turn * 2 + (s - 1))
                    nc.scalar.activation(gel[:, s * T:(s + 1) * T], B[4 + s][:, 0:T], ACT.Gelu).then_inc(gelu_done, 1)

            gelu(0, first=True)
            with act.Fori(1, KEYS // 2) as turn:
                gelu(turn)
            sq3 = arena[:, 0:2048].rearrange("p (k t) -> p k t", k=KT)
            for k in range(KT):
                act.wait_ge(x2_ready, k + 1)
                nc.scalar.activation(sq3[:, k, :], x3[:, k, :], ACT.Square).then_inc(sq3_ready, 1)
            act.wait_ge(ssq3_ready, 1)
            nc.scalar.activation(rstd[:, :], B[6][:, 0:T], ACT.Sqrt, bias=eps[:, 0:1], scale=1.0 / D).then_inc(root3_ready, 1)

        @block.vector
        def _(dve):
            steps = [0]
            V = nc.vector

            def link(ins):
                steps[0] += 1
                ins.then_inc(dve_step, 1)
                dve.wait_ge(dve_step, steps[0])

            V.memset(eps[:, :], EPS)
            V.memset(ones[:, :], 1.0).then_inc(const_set, 1)
            dve.wait_ge(cexp, 1)
            link(V.tensor_scalar(silu[:, KT:2 * KT], silu[:, KT:2 * KT], 1.0, None, ALU.add))
            link(V.reciprocal(silu[:, 2 * KT:3 * KT], silu[:, KT:2 * KT]))
            V.tensor_tensor(silu[:, 0:KT], silu[:, 2 * KT:3 * KT], param("c"), ALU.mult).then_inc(silu_ready, 1)

            dve.wait_ge(root_ready, 1)
            link(V.reciprocal(rstd[:, :], rstd[:, :]))
            link(V.tensor_tensor(hT, x3, rstd[:, :].unsqueeze(1).to_broadcast([P, KT, T]), ALU.mult))
            dve.wait_ge(ada_done, 4)
            link(V.tensor_tensor(mod[:, 0:2 * KT], B[7][:, 0:2 * KT], param("ada_b")[:, 0:2 * KT], ALU.add))
            link(V.tensor_scalar(scale1[:, :], mod[:, KT:2 * KT], 1.0, None, ALU.add))
            link(V.tensor_tensor(scale1[:, :], scale1[:, :], param("g1"), ALU.mult))
            for k in range(KT):
                V.tensor_scalar(hT[:, k, :], hT[:, k, :], scale1[:, k:k + 1], mod[:, k:k + 1], ALU.mult, ALU.add).then_inc(h_ready, 1)

            def rope(r):
                c, tt = ROPES[r]
                n = ROPE_HEADS[c]
                cols = n * DH
                if c == "kd":
                    dve.wait_ge(job_out, 10 + tt + 1)
                    src = kdv[:, tt, 0:DH]
                else:
                    pos = c
                    dve.wait_ge(z_done, 2 * pos + tt + 1)
                    src = B[(2 * pos + tt) % 4][:, 0:cols]
                z = src.rearrange("p (h s d) -> p h s d", s=2, d=HALF)
                ra = rope_a[:, 0:cols].rearrange("p (h s d) -> p h s d", s=2, d=HALF)
                rb = rope_b[:, 0:cols].rearrange("p (h s d) -> p h s d", s=2, d=HALF)
                cos = table("cos").rearrange("p (a d) -> p a d", a=TT)[:, tt, :]
                sin = table("sin").rearrange("p (a s d) -> p a s d", a=TT, s=2)[:, tt, :, :]
                cosb = cos.unsqueeze(1).unsqueeze(1).to_broadcast([P, n, 2, HALF])
                if r:
                    dve.wait_ge(roped, r)
                V.tensor_tensor(ra, z, cosb, ALU.mult)
                V.tensor_tensor(rb[:, :, 0, :], z[:, :, 1, :], sin[:, 0, :].unsqueeze(1).to_broadcast([P, n, HALF]), ALU.mult)
                last = V.tensor_tensor(rb[:, :, 1, :], z[:, :, 0, :], sin[:, 1, :].unsqueeze(1).to_broadcast([P, n, HALF]), ALU.mult)
                if c == "kd":
                    link(last)
                else:
                    last.then_inc(z_read, 1)
                    read[0] += 1
                    dve.wait_ge(z_read, read[0])
                if r >= 2:
                    dve.wait_ge(job_done, 1 + max(j for j, w in enumerate(JOBS) if w[0] == "rope" and w[1] == r - 2))
                V.tensor_tensor(rq[r % 2][:, 0:cols], rope_a[:, 0:cols], rope_b[:, 0:cols], ALU.add).then_inc(roped, 1)

            read = [0]
            dve.wait_ge(tab_in, 16)
            for r in range(2):
                rope(r)
            for r in range(2, 4):
                tt = ROPES[r][1]
                dve.wait_ge(z_done, 2 + tt + 1)
                V.tensor_copy(zk[:, tt, :], B[2 + tt][:, 448:480]).then_inc(zk_ready, 1)
                rope(r)
            for tt in range(TT):
                dve.wait_ge(zv_ready, tt + 1)
                dve.wait_ge(*((ck_sum, tt) if tt else (roped, 4)))
                V.tensor_tensor_reduce(out=rope_a[:, 0:P], in0=zv[:, tt, 0:P], in1=zv[:, tt, 0:P], scale=1.0, scalar=0.0,
                                       op0=ALU.mult, op1=ALU.add, accum_out=small[:, tt:tt + 1]).then_inc(ck_sum, 1)
            for tt in range(TT):
                dve.wait_ge(ck_root, tt + 1)
                link(V.reciprocal(small[:, 4 + tt:5 + tt], small[:, 2 + tt:3 + tt]))
                V.tensor_scalar(zv[:, tt, 0:P], zv[:, tt, 0:P], small[:, 4 + tt:5 + tt], None, ALU.mult).then_inc(ck_ready, 1)
            dve.wait_ge(ck_ready, 2)
            for r in range(4, len(ROPES)):
                rope(r)

            dve.wait_ge(gexp, 1)
            link(V.tensor_scalar(ssig[:, :], ssig[:, :], 1.0, None, ALU.add))
            link(V.reciprocal(ssig[:, :], ssig[:, :]))
            dve.wait_ge(zk_ready, 2)
            link(V.tensor_scalar(wis[:, :].rearrange("p (a n) -> p a n", a=TT), zk[:, :, 24:32], HEADS ** -0.5, None, ALU.mult))
            dve.wait_ge(job_out, len(JOBS))
            dve.wait_ge(w2_in, 48)
            for v, first in enumerate((KC, VC)):
                for half in range(2):
                    src = kT[:, first:first + 2, half * CMP_STEP:half * CMP_STEP + NCMP * CMP_STEP].rearrange(
                        "p g (n l) -> p g n l", l=CMP_STEP)
                    dst = blk[:, v, half * CMP_STEP:(half + 1) * CMP_STEP, :].rearrange("p l (g n) -> p g n l", g=2)
                    pos = posT[:, half * CMP_STEP:(half + 1) * CMP_STEP].unsqueeze(1).unsqueeze(1).to_broadcast(
                        [DH, 2, NCMP, CMP_STEP])
                    last = V.tensor_tensor(dst, src, pos, ALU.add)
            last.then_inc(blk_ready, 1)

            for q in range(8):
                tt, hp = divmod(q, 4)
                ns = (tt + 1) * P
                sc = score[:, tt, 0:ns]
                for i in range(2):
                    h = 2 * hp + i
                    r = relu[q % 2][:, i * ns:(i + 1) * ns]
                    wh = wis[:, tt * HEADS + h:tt * HEADS + h + 1]
                    if i == 0:
                        dve.wait_ge(relu_done, q + 1)
                    if h == 0:
                        link(V.tensor_scalar(sc, r, wh, None, ALU.mult))
                    elif i == 0:
                        link(V.scalar_tensor_tensor(sc, r, wh, sc, ALU.mult, ALU.add))
                    else:
                        V.scalar_tensor_tensor(sc, r, wh, sc, ALU.mult, ALU.add).then_inc(relu_used, 1)
                        dve.wait_ge(relu_used, q + 1)
                if hp == 3:
                    link(V.tensor_tensor(sc, sc, table("cmask")[:, T - ns:T], ALU.add))

            dve.wait_ge(hid_done, 1)
            V.tensor_copy(hid[:, 0:30], B[4][0:DH, 0:30])
            link(V.tensor_copy(hid[:, 30:60], B[5][0:DH, 0:30]))
            x = hid[:, 0:60]
            link(V.tensor_tensor(hid[:, 60:120], x, x, ALU.mult))
            link(V.tensor_scalar(hid[:, 60:120], hid[:, 60:120], 0.044715, 1.0, ALU.mult, ALU.add))
            V.tensor_tensor(hid[:, 120:180], hid[:, 60:120], x, ALU.mult).then_inc(hid_in, 1)
            dve.wait_ge(tanh_done, 1)
            link(V.tensor_scalar(hid[:, 180:240], hid[:, 120:180], 1.0, 0.5, ALU.add, ALU.mult))
            link(V.tensor_tensor(hid[:, 300:360], hid[:, 180:240], x, ALU.mult))
            V.tensor_copy(hidrep.rearrange("p (g r n) -> p g r n", g=2, r=4),
                          hid[:, 330:360].rearrange("p (g n) -> p g n", g=2).unsqueeze(2).to_broadcast([DH, 2, 4, NCMP])).then_inc(hid_ready, 1)
            dve.wait_ge(cmpkv_done, 1)
            V.tensor_copy(kcmpT, B[6][0:DH, 0:2 * NCMP]).then_inc(cmpkv_ready, 1)
            rows = HEADS * NCMP
            V.tensor_tensor(vbd[0:rows, :].rearrange("p (h f) -> p h f", h=HEADS),
                            B[6][0:rows, 64:64 + DH].unsqueeze(1).to_broadcast([rows, HEADS, DH]),
                            table("bmask")[0:rows, :].unsqueeze(2).to_broadcast([rows, HEADS, DH]), ALU.mult).then_inc(cmpkv_ready, 1)
            for tt in range(TT):
                dve.wait_ge(cs_done, tt + 1)
                s = pc[:, tt, :].rearrange("p (h n) -> p h n", h=HEADS)
                add = table("cmp_add").rearrange("p (a n) -> p a n", a=TT)[:, tt, :].unsqueeze(1).to_broadcast([P, HEADS, NCMP])
                link(V.tensor_tensor(s, B[tt][:, 0:rows].rearrange("p (h n) -> p h n", h=HEADS), add, ALU.add))
                link(V.tensor_reduce(csum[:, 0:8], s, AX.X, ALU.max))
                V.tensor_tensor(s, s, csum[:, 0:8].unsqueeze(2).to_broadcast([P, HEADS, NCMP]), ALU.subtract).then_inc(cs_in, 1)
            for tt in range(TT):
                dve.wait_ge(cexp_done, tt + 1)
                s = pc[:, tt, :].rearrange("p (h n) -> p h n", h=HEADS)
                mul = table("cmp_mul").rearrange("p (a n) -> p a n", a=TT)[:, tt, :].unsqueeze(1).to_broadcast([P, HEADS, NCMP])
                link(V.tensor_tensor(s, s, mul, ALU.mult))
                link(V.tensor_reduce(csum[:, 0:8], s, AX.X, ALU.add))
                link(V.tensor_scalar(csum[:, 0:8], csum[:, 0:8], 1e-30, None, ALU.max))
                link(V.reciprocal(csum[:, 0:8], csum[:, 0:8]))
                V.tensor_tensor(s, s, csum[:, 0:8].unsqueeze(2).to_broadcast([P, HEADS, NCMP]), ALU.mult).then_inc(pc_ready, 1)
            gate3 = ssig[:, :].rearrange("p (a h b) -> p a h b", a=TT, b=3)
            for tt in range(TT):
                dve.wait_ge(oc_done, tt + 1)
                V.tensor_tensor(o_nsa[tt].rearrange("p (h f) -> p h f", h=HEADS), B[4 + tt][:, :].rearrange("p (h f) -> p h f", h=HEADS),
                                gate3[:, tt, :, 0].unsqueeze(2).to_broadcast([P, HEADS, DH]), ALU.mult).then_inc(oc_read, 1)
            dve.wait_ge(oc_read, 2)

            def finish(g):
                b, tt, _ = UNITS[4 * g]
                dve.wait_ge(o_unit, 4 * g + 4)
                r = recip[:, 0:HEADS]
                link(V.tensor_scalar(r, rowsum[:, g * HEADS:(g + 1) * HEADS], 1e-30, None, ALU.max))
                link(V.reciprocal(r, r))
                o = B[4 + g % 2][:, :].rearrange("p (h f) -> p h f", h=HEADS)
                if b == 2:
                    V.tensor_tensor(o_dsa[tt].rearrange("p (h f) -> p h f", h=HEADS), o,
                                    r.unsqueeze(2).to_broadcast([P, HEADS, DH]), ALU.mult).then_inc(o_read, 1)
                    dve.wait_ge(o_read, g + 1)
                else:
                    link(V.tensor_tensor(r, r, gate3[:, tt, :, BRANCHES[b][3]], ALU.mult))
                    V.tensor_tensor(otmp.rearrange("p (h f) -> p h f", h=HEADS), o,
                                    r.unsqueeze(2).to_broadcast([P, HEADS, DH]), ALU.mult).then_inc(o_read, 1)
                    dve.wait_ge(o_read, g + 1)
                    link(V.tensor_tensor(o_nsa[tt], o_nsa[tt], otmp, ALU.add))

            for u in range(len(UNITS)):
                b, tt, hp = UNITS[u]
                ns = (tt + 1) * P
                dve.wait_ge(s_done, u + 1)
                if u >= 2:
                    dve.wait_ge(pt_done, u - 1)
                if u == 0:
                    dve.wait_ge(pct_ready, 2)
                for i in range(2):
                    mask = work[:, tt, 0:ns] if b == 2 else table("cmask")[:, T - ns:T]
                    last = V.tensor_tensor_reduce(out=ssb[u % 2][:, i * ns:(i + 1) * ns], in0=B[u % 2][:, i * ns:(i + 1) * ns], in1=mask,
                                                  scale=DH ** -0.5, scalar=-3.0e38, op0=ALU.add, op1=ALU.max,
                                                  accum_out=rowmax[:, 2 * (u % 2) + i:2 * (u % 2) + i + 1])
                link(last)
                V.tensor_scalar(negmax[:, 2 * (u % 2):2 * (u % 2) + 2], rowmax[:, 2 * (u % 2):2 * (u % 2) + 2], -1.0, None,
                                ALU.mult).then_inc(s_masked, 1)
                if u < 16:
                    t2, rnd = divmod(u, 8)
                    n2 = (t2 + 1) * P
                    left = score[:, t2, 0:n2] if rnd == 0 else work[:, t2, 0:n2]
                    link(V.max(best8[:, :], left))
                    link(V.match_replace(work[:, t2, 0:n2], best8[:, :], left, TAKEN))
                    if rnd == TOPK_DSA // 8 - 1:
                        link(V.tensor_scalar(work[:, t2, 0:n2], work[:, t2, 0:n2], TAKEN / 2, NEG, ALU.is_gt, ALU.mult))
                        link(V.tensor_tensor(work[:, t2, 0:n2], work[:, t2, 0:n2], table("cmask")[:, T - n2:T], ALU.add))
                if u >= 5 and (u - 5) % 4 == 0:
                    finish((u - 5) // 4)
            finish(GROUPS - 1)
            dve.wait_ge(o_read, GROUPS)
            V.tensor_copy(small[:, 8:9], small[:, 4:5]).then_inc(o_ready, 1)

            dve.wait_ge(ada_done, 12)
            link(V.tensor_tensor(mod[:, 2 * KT:6 * KT], B[7][:, 2 * KT:6 * KT], param("ada_b")[:, 2 * KT:6 * KT], ALU.add))
            link(V.tensor_scalar(scale2[:, :], mod[:, 4 * KT:5 * KT], 1.0, None, ALU.add))
            link(V.tensor_tensor(scale2[:, :], scale2[:, :], param("g2"), ALU.mult))
            dve.wait_ge(fill_out, 16)
            link(V.tensor_scalar(gates, gates, 1.0, None, ALU.add))
            link(V.reciprocal(gates, gates))
            for m in range(KT):
                dve.wait_ge(br_done, m + 1)
                if m == 0:
                    dve.wait_ge(fill_done, 16)
                link(V.tensor_tensor(hT[:, m, :], B[4 + m % 2][:, 0:T], gates[:, m, :], ALU.mult))
                link(V.tensor_tensor(gates[:, m, :], B[4 + m % 2][:, T:2 * T], gates[:, KT + m, :], ALU.mult))
                V.tensor_tensor(hT[:, m, :], hT[:, m, :], gates[:, m, :], ALU.add).then_inc(merged_ready, 1)
            for m in range(KT):
                dve.wait_ge(mo_done, m + 1)
                V.scalar_tensor_tensor(x3[:, m, :], B[m % 2][:, 0:T], mod[:, 2 * KT + m:2 * KT + m + 1], x3[:, m, :],
                                       ALU.mult, ALU.add).then_inc(x1_ready, 1)
            dve.wait_ge(root2_ready, 1)
            link(V.reciprocal(rstd[:, :], rstd[:, :]))
            link(V.tensor_tensor(h2, x3, rstd[:, :].unsqueeze(1).to_broadcast([P, KT, T]), ALU.mult))
            for k in range(KT):
                V.tensor_scalar(h2[:, k, :], h2[:, k, :], scale2[:, k:k + 1], mod[:, 3 * KT + k:3 * KT + k + 1],
                                ALU.mult, ALU.add).then_inc(h2_ready, 1)

            val = tk[:, 0:256].rearrange("p (s k) -> p s k", s=16)
            idx = tk[:, 256:512]
            idx_u = idx.bitcast(U32).rearrange("p (s k) -> p s k", s=16)
            idxf = tk[:, 512:768].rearrange("p (h c k) -> p h c k", h=HEADS, c=2)
            cand = tk[:, 768:768 + HEADS * NCAND].rearrange("p (h c) -> p h c", h=HEADS)
            cidx = tk[:, 1200:1200 + HEADS * NCAND].rearrange("p (h c) -> p h c", h=HEADS)
            cwork = tk[:, 1600:1600 + NCAND]
            top = tk[:, 1664:1664 + P].rearrange("p (h k) -> p h k", h=HEADS)
            pos = tk[:, 1792:1792 + P].bitcast(U32).rearrange("p (h k) -> p h k", h=HEADS)
            posf = tk[:, 1920:2048].rearrange("p (h k) -> p h k", h=HEADS)
            eid = tk[:, 2048:2176]
            eid_i = tk[:, 2176:2304].bitcast(I32)
            part_i = tk[:, 2304:2432].bitcast(I32)
            part_j = tk[:, 2432:2560].bitcast(I32)
            gsum = tk[:, 2560:2568]
            iwork = tk[:, 2600:2728]
            dve.wait_ge(w_in[(len(LOADS) - 1) % WSLOTS], 16 * ((len(LOADS) - 1) // WSLOTS + 1))
            dve.wait_ge(q2_done, KT)
            val4 = tk[:, 0:256].rearrange("p (h c k) -> p h c k", h=HEADS, c=2)
            for tt in range(TT):
                for s in range(16):
                    if s % 8 == 0:
                        dve.wait_ge(sub_ready, 4 * tt + s // 4 + 2)
                    src = sub[tt][:, s, :]
                    link(V.max(val[:, s, 0:8], src))
                    V.max_index(idx_u[:, s, 0:8], val[:, s, 0:8], src)
                    link(V.match_replace(iwork, val[:, s, 0:8], src, TAKEN))
                    link(V.max(val[:, s, 8:16], iwork))
                    link(V.max_index(idx_u[:, s, 8:16], val[:, s, 8:16], iwork))
                link(V.tensor_copy(tk[:, 512:768], idx.bitcast(U32)))
                link(V.tensor_scalar(idxf[:, :, 0, :], idxf[:, :, 0, :], float(KEYS), None, ALU.mult))
                for dst, src in ((cand, val4), (cidx, idxf)):
                    c0 = 0
                    for a, n in CAND_ROWS:
                        V.tensor_tensor(dst[:, :, c0:c0 + n], src[:, :, 0, a:a + 1].to_broadcast([P, HEADS, n]), src[:, :, 1, 0:n], ALU.add)
                        c0 += n
                    link(V.tensor_tensor(dst[:, :, c0:NCAND], src[:, :, 0, TOPK // 2:TOPK],
                                         src[:, :, 1, 0:1].to_broadcast([P, HEADS, TOPK // 2]), ALU.add))
                for h in range(HEADS):
                    src = cand[:, h, :]
                    link(V.max(top[:, h, 0:8], src))
                    V.max_index(pos[:, h, 0:8], top[:, h, 0:8], src)
                    link(V.match_replace(cwork, top[:, h, 0:8], src, TAKEN))
                    link(V.max(top[:, h, 8:16], cwork))
                    link(V.max_index(pos[:, h, 8:16], top[:, h, 8:16], cwork))
                w = tk[:, 6000 + (3 * tt + 2) * P:6000 + (3 * tt + 3) * P].rearrange("p (h k) -> p h k", h=HEADS)
                V.tensor_tensor(w, top, top[:, :, 0:1].to_broadcast([P, HEADS, TOPK]), ALU.subtract).then_inc(top_ready, 1)
                link(V.tensor_copy(posf, pos))
                eq = eqbuf.rearrange("p (h k c) -> p h k c", h=HEADS, k=TOPK)
                link(V.tensor_tensor(eqbuf.rearrange("p (k c) -> p k c", c=NCAND),
                                     table("pos").unsqueeze(1).to_broadcast([P, HEADS * TOPK, NCAND]),
                                     tk[:, 1920:2048].unsqueeze(2).to_broadcast([P, HEADS * TOPK, NCAND]), ALU.is_equal))
                link(V.tensor_tensor(eq, eq, cidx.unsqueeze(2).to_broadcast([P, HEADS, TOPK, NCAND]), ALU.mult))
                link(V.tensor_reduce(eid, eqbuf.rearrange("p (k c) -> p k c", c=NCAND), AX.X, ALU.add))
                link(V.tensor_copy(eid_i, eid))
                V.tensor_scalar(part_i, eid_i, 7, None, ALU.logical_shift_right)
                link(V.tensor_scalar(part_j, eid_i, KEYS - 1, None, ALU.bitwise_and))
                V.tensor_copy(tk[:, 6000 + 3 * tt * P:6000 + (3 * tt + 1) * P], part_i)
                V.tensor_copy(tk[:, 6000 + (3 * tt + 1) * P:6000 + (3 * tt + 2) * P], part_j)
                dve.wait_ge(gate_exp, tt + 1)
                link(V.tensor_reduce(gsum, w, AX.X, ALU.add))
                link(V.reciprocal(gsum, gsum))
                V.tensor_tensor(w, w, gsum.unsqueeze(2).to_broadcast([P, HEADS, TOPK]), ALU.mult).then_inc(route_ready, 1)

            dve.wait_ge(rt_ready, TT)
            iT = routeT[:, 0:T]
            jT = routeT[:, T:2 * T]
            wT = routeT[:, 2 * T:3 * T]

            def one_hots(turn, first=False):
                for half in range(2):
                    if not first:
                        dve.wait_ge(g_done, turn * 2 + (half - 1))
                    for i in range(4):
                        s = 4 * half + i
                        t = turn * TOK_LOOP + s
                        V.tensor_scalar(ohj[s], table("iota"), jT[:, bass.ds(t, 1)], None, ALU.is_equal)
                        last = V.tensor_scalar(ohi[s], table("iota"), iT[:, bass.ds(t, 1)], wT[:, bass.ds(t, 1)], ALU.is_equal, ALU.mult)
                    last.then_inc(oh_ready, 1)

            one_hots(0, first=True)
            with dve.Fori(1, T // TOK_LOOP) as turn:
                one_hots(turn)
            dve.wait_ge(g_out, 2 * (T // TOK_LOOP))

            def weigh(turn, first=False):
                for s in range(2):
                    dve.wait_ge(gelu_done, turn * 2 + (s + 1))
                    if not first:
                        dve.wait_ge(v_done, turn * 2 + (s - 1))
                    V.tensor_tensor(prod[:, s * T:(s + 1) * T], gel[:, s * T:(s + 1) * T],
                                    G[:, :, bass.ds(turn * 2 + s, 1)].rearrange("p t a -> p (t a)"), ALU.mult).then_inc(prod_ready, 1)

            weigh(0, first=True)
            with dve.Fori(1, KEYS // 2) as turn:
                weigh(turn)
            dve.wait_ge(v_done, KEYS)
            for m in range(KT):
                V.scalar_tensor_tensor(x3[:, m, :], B[m // 2][:, (m % 2) * T:(m % 2 + 1) * T], mod[:, 5 * KT + m:5 * KT + m + 1],
                                       x3[:, m, :], ALU.mult, ALU.add).then_inc(x2_ready, 1)
            dve.wait_ge(root3_ready, 1)
            link(V.reciprocal(rstd[:, :], rstd[:, :]))
            for m in range(KT):
                V.scalar_tensor_tensor(h2[:, m, :], x3[:, m, :], param("gf")[:, m:m + 1], rstd[:, :], ALU.mult, ALU.mult).then_inc(y_ready, 1)


def constants():
    tab = np.zeros((P, TAB_W), np.float32)

    def put(name, a):
        tab[:a.shape[0], TAB[name][0]:TAB[name][0] + a.shape[1]] = a

    t = np.arange(T)
    p = np.arange(P)
    put("ident", np.eye(P))
    put("cmask", np.concatenate([np.zeros((P, P)), np.where(p[None, :] <= p[:, None], 0.0, NEG)], 1))
    put("iota", np.tile(p.astype(np.float32), (P, 1)))
    inv = np.float32(10000.0) ** (-np.arange(HALF, dtype=np.float32) / np.float32(HALF))
    ang = t.astype(np.float32)[:, None] * inv.astype(np.float32)[None, :]
    cos, sin = np.cos(ang), np.sin(ang)
    put("cos", cos.reshape(TT, P, HALF).transpose(1, 0, 2).reshape(P, -1))
    put("sin", np.stack([-sin, sin], 1).reshape(TT, P, 2 * HALF).transpose(1, 0, 2).reshape(P, -1))
    ok = (np.arange(NCMP) * CMP_STEP + CMP_LEN - 1)[None, :] <= t[:, None]
    put("cmp_add", np.where(ok, 0.0, NEG).reshape(TT, P, NCMP).transpose(1, 0, 2).reshape(P, -1))
    put("cmp_mul", ok.astype(np.float32).reshape(TT, P, NCMP).transpose(1, 0, 2).reshape(P, -1))
    put("bmask", (np.arange(HEADS * NCMP)[:, None] // NCMP == np.arange(HEADS)[None, :]).astype(np.float32))
    put("pos", np.tile(np.arange(NCAND, dtype=np.float32), (P, 1)))
    return tab


def kernel(**inputs):
    import concourse.bacc as bacc
    from concourse.bass_utils import run_bass_kernel_spmd

    a = {k: np.asarray(v) for k, v in inputs.items()}

    def feature_tiles(v):
        return v.reshape(-1, P).T

    w_in = a["w_in"][0]
    par = np.concatenate([feature_tiles(a["c"][0]), feature_tiles(a["ada_b"][0]), feature_tiles(a["norm1_g"][0]),
                          feature_tiles(a["norm2_g"][0]), feature_tiles(a["final_g"]), a["kv_norm_g"][0][:, None]], 1)
    arrays = {
        "par": par,
        "tab": constants(),
        "x": a["x"][0].T,
        "ada_w": a["ada_w"][0],
        "w_in": np.concatenate([w_in[:, START[n]:START[n] + SIZE[n]] for c in CHUNKS for n in c], 1),
        "w_gate": w_in[:, START["g_m"]:],
        "w_br": np.stack([a["w_br_nsa"][0], a["w_br_dsa"][0]]),
        "w_out": a["w_out"][0],
        "peer_wq": a["peer_wq"][0],
        "w_ukv": np.concatenate([a["w_uk"][0], a["w_uv"][0]], 1),
        "cmp_w2": np.concatenate([a["cmp_w2_k"][0], a["cmp_w2_v"][0]], 1),
        "cmp_pos": a["cmp_pos"][0].T,
        "cmp_w1_k": a["cmp_w1_k"][0].transpose(1, 0, 2),
        "cmp_w1_v": a["cmp_w1_v"][0].transpose(1, 0, 2),
        "subkeys": a["peer_subkeys"][0].transpose(1, 3, 0, 2).reshape(P, HEADS * KEYS),
        "uT": a["peer_u"][0].reshape(KEYS, KEYS, KT, P).transpose(0, 3, 2, 1),
        "v": a["peer_v"][0].reshape(KEYS, KEYS, D),
    }
    nc = bacc.Bacc("TRN2", target_bir_lowering=False, num_devices=1)
    feeds, aps = {}, {}
    for name, v in arrays.items():
        v = np.ascontiguousarray(v)
        feeds[f"in_{name}"] = v
        aps[name] = nc.dram_tensor(f"in_{name}", v.shape, mybir.dt.from_np(v.dtype), kind="ExternalInput").ap()
    out = nc.dram_tensor("yT", (D, T), F32, kind="ExternalOutput").ap()
    build(nc, aps, out)
    r = run_bass_kernel_spmd(nc, [feeds], core_ids=[0])
    return np.ascontiguousarray(r.results[0]["yT"].T).reshape(1, T, D)
```

```python
from contextlib import ExitStack

import concourse.bass as bass
import numpy as np
from concourse import mybir

F32 = mybir.dt.float32
F32R = mybir.dt.float32r
I32 = mybir.dt.int32
U32 = mybir.dt.uint32
ALU = mybir.AluOpType
ACT = mybir.ActivationFunctionType
AX = mybir.AxisListType

P = 128
D = 1024
KT = D // P
T = 256
TT = T // P
DH = 64
HALF = DH // 2
HEADS = 8
EPS = 1e-6
NEG = -1e30
TAKEN = -3e38
CMP_LEN, CMP_STEP = 32, 16
NCMP = T // CMP_STEP - 1
TOPK_DSA = min(256, T // 4)
KEYS = 128
TOPK = 16

SPLITS = (512, 128, 128, 128, 128, 128, 128, 24, 512, 128, 512, 64, 8, 2048)
NAMES = ("q_n", "kc", "vc", "ks", "vs", "kw", "vw", "g_n", "q_d", "ckv", "qi", "ki", "wi", "g_m")
CHUNKS = (("qi",), ("kc", "ks", "kw", "ki", "g_n", "wi"), ("ckv", "vc", "vs", "vw"), ("q_d",), ("q_n",))
START = dict(zip(NAMES, np.cumsum((0,) + SPLITS[:-1]).tolist()))
SIZE = dict(zip(NAMES, SPLITS))
CHUNK_COLS = [sum(SIZE[n] for n in c) for c in CHUNKS]
CHUNK_AT = [sum(CHUNK_COLS[:i]) for i in range(len(CHUNKS))]

CAND = [(a, b) for a in range(TOPK) for b in range(TOPK) if (a + 1) * (b + 1) <= TOPK]
NCAND = len(CAND)
CAND_ROWS = [(a, TOPK // (a + 1)) for a in range(TOPK // 2)]

TAB = {}
_at = 0
for _n, _w in (("ident", P), ("cmask", T), ("iota", P), ("cos", TT * HALF), ("sin", TT * 2 * HALF),
               ("cmp_add", TT * NCMP), ("cmp_mul", TT * NCMP), ("bmask", HEADS), ("pos", NCAND)):
    TAB[_n] = (_at, _at + _w)
    _at += _w
TAB_W = _at

PAR = {}
_at = 0
for _n, _w in (("c", KT), ("ada_b", 6 * KT), ("g1", KT), ("g2", KT), ("gf", KT), ("kvg", 1)):
    PAR[_n] = (_at, _at + _w)
    _at += _w
PAR_W = _at

LOADS = [("ada", m) for m in range(4)] + [("win", m) for m in range(len(CHUNKS))]
LOADS += [("gate", 0)]
for _i in range(3):
    LOADS += [("gate", 1 + _i), ("ada", 4 + 2 * _i), ("ada", 5 + 2 * _i)]
LOADS += [("ada", 10), ("ada", 11), ("br", 0), ("br", 1), ("out", 0), ("out", 1), ("wq", 0), ("wq", 1)]
CHUNK_NO = {c: n for n, c in enumerate(LOADS)}
WSLOTS = 3
WCOLS = KT * 512

QI, QD, QN = 0, 8, 16
KC, KS, KW, KI, VC, KD = 0, 2, 4, 6, 7, 9
ROPES = [(0, 0), (0, 1), (1, 0), (1, 1), (3, 0), (3, 1), ("kd", 0), ("kd", 1), (4, 0), (4, 1)]
ROPE_HEADS = {0: 8, 1: 7, 3: 8, 4: 8, "kd": 1}


def transpose_jobs():
    jobs = []

    def heads(r):
        c, tt = ROPES[r]
        dst, first = {0: ("q", QI), 3: ("q", QD), 4: ("q", QN), 1: ("k", KC), "kd": ("k", KD)}[c]
        n = ROPE_HEADS[c]
        for h in range(0, n, 4):
            jobs.append(("rope", r, h, min(4, n - h), dst, first + h, tt))

    for r in (0, 1, 2, 3):
        heads(r)
    for tt in range(TT):
        jobs.append(("ckv", tt))
    for tt in range(TT):
        jobs.append(("kdvd", tt))
    for r in (4, 5, 6, 7, 8, 9):
        heads(r)
    return jobs


JOBS = transpose_jobs()
BRANCHES = (("slc", QN, KS, 1), ("win", QN, KW, 2), ("dsa", QD, KD, None))
UNITS = [(b, tt, hp) for b in range(3) for tt in range(TT) for hp in range(HEADS // 2)]
GROUPS = len(UNITS) // 4
UNIT_GATE = [4 + 2 * (u // 3) + u % 3 if u % 3 < 2 and u < 18 else None for u in range(len(UNITS))]
UNIT_ADA = [[(4 + u // 3, k) for k in ((0, 1, 2), (3, 4, 5), (6, 7))[u % 3]] for u in range(len(UNITS))]

TOKS = 4
SLOTS = 4
IH = KEYS // 2
WHOLE = 32
RT_TURN = 12


def build(nc, A, out):
    with ExitStack() as ctx:
        def sb(name, cols, parts=P, dt=F32):
            return ctx.enter_context(nc.sbuf_tensor(name, [parts, cols], dt))

        def sem(name):
            return ctx.enter_context(nc.semaphore(name))

        arena = sb("arena", KEYS * T)
        ring = sb("ring", SLOTS * D)
        tile_hi = sb("tile_hi", SLOTS * 512, dt=F32R)
        tile_lo = sb("tile_lo", SLOTS * 512, dt=F32R)
        h2_hi = sb("h2_hi", KT * T, dt=F32R)
        h2_lo = sb("h2_lo", KT * T, dt=F32R)
        a_hi = sb("a_hi", 2 * T, dt=F32R)
        a_lo = sb("a_lo", 2 * T, dt=F32R)
        xT = sb("xT", KT * T)
        oneh = sb("oneh", 4 * 512)
        tab = sb("tab", TAB_W)
        par = sb("par", PAR_W)
        mod = sb("mod", 6 * KT)
        scale1 = sb("scale1", KT)
        scale2 = sb("scale2", KT)
        silu = sb("silu", 3 * KT)
        ones = sb("ones", P)
        eps = sb("eps", 1)
        rstd = sb("rstd", T)
        ssig = sb("ssig", TT * 24)
        wis = sb("wis", TT * HEADS)
        small = sb("small", 16)
        rowmax = sb("rowmax", 4)
        negmax = sb("negmax", 4)
        rowsum = sb("rowsum", GROUPS * HEADS)
        recip = sb("recip", HEADS)
        best8 = sb("best8", 8)
        wukv = sb("wukv", 2 * DH)
        w2kv = sb("w2kv", 2 * DH, DH)
        posT = sb("posT", CMP_LEN, DH)
        routeT = sb("routeT", 3 * T)

        def table(name):
            return tab[:, TAB[name][0]:TAB[name][1]]

        def param(name):
            return par[:, PAR[name][0]:PAR[name][1]]

        ident = table("ident")
        x3 = xT[:, :].rearrange("p (k t) -> p k t", k=KT)

        def tiles(t, k):
            return t.rearrange("p (k t) -> p k t", k=k)

        wslot = [arena[:, s * WCOLS:(s + 1) * WCOLS] for s in range(WSLOTS)]
        at = WSLOTS * WCOLS
        hT = tiles(arena[:, at:at + KT * T], KT)
        at += KT * T
        q_at = at
        qT = tiles(arena[0:DH, at:at + 24 * T], 24)
        oT = arena[:, at:at + 8 * T].rearrange("p (b k t) -> p b k t", b=2, k=4)
        q2T = tiles(arena[:, at:at + KT * T], KT)
        sq1 = tiles(arena[:, at + 8 * T:at + 16 * T], KT)
        ada_sum = [arena[:, at + 16 * T + i * 512:at + 16 * T + (i + 1) * 512] for i in range(4)]
        skT = arena[:, at + 8 * T:at + 12 * T]
        at += 24 * T
        kT = tiles(arena[0:DH, at:at + 10 * T], 10)
        at += 10 * T
        blk = arena[0:DH, at:at + 2 * CMP_LEN * 2 * NCMP].rearrange("p (v l n) -> p v l n", v=2, l=CMP_LEN)
        gates = tiles(arena[:, at:at + 16 * T], 16)
        at += 16 * T
        ckvT = arena[:, at:at + T]
        kdv = arena[:, at + T:at + 2 * T].rearrange("p (a n) -> p a n", a=TT)
        at += 2 * T
        scr = arena[:, at:]
        zv = scr[:, 0:1024].rearrange("p (a n) -> p a n", a=TT)
        zk = scr[:, 1024:1088].rearrange("p (a n) -> p a n", a=TT)
        rope_a = scr[:, 1088:1600]
        rope_b = scr[:, 1600:2112]
        rq = [scr[:, 2112 + i * 512:2112 + (i + 1) * 512] for i in range(2)]
        hid = scr[0:DH, 3136:3496]
        hidrep = scr[0:DH, 3496:3616]
        kcmpT = scr[0:DH, 3616:3646]
        csum = scr[:, 3646:3654]
        score = scr[:, 3660:4172].rearrange("p (a n) -> p a n", a=TT)
        work = scr[:, 4172:4684].rearrange("p (a n) -> p a n", a=TT)
        assert at + 4684 <= KEYS * T
        relu = [rope_a, rope_b]
        vbd = rope_a
        pc = rope_b[:, 0:240].rearrange("p (a n) -> p a n", a=TT)
        pcT = [rope_b[:, 256 + i * 128:256 + (i + 1) * 128] for i in range(2)]
        otmp = rq[0]

        at = q_at + 12 * T
        eqbuf = arena[:, at:at + HEADS * TOPK * NCAND]
        at += HEADS * TOPK * NCAND
        assert q_at + 12 * T >= IH * T
        sub = [arena[:, at + i * 2048:at + (i + 1) * 2048].rearrange("p (s n) -> p s n", n=KEYS) for i in range(TT)]
        at += TT * 2048
        sq2 = tiles(arena[:, at:at + KT * T], KT)
        tk = arena[:, at:at + 3626]
        assert at + 3626 <= KEYS * T
        route = tk[:, 2730:2730 + 6 * P].rearrange("p (a i c) -> p a i c", a=TT, i=3)

        cidx = [tk[:, 1738 + i * 400:1738 + (i + 1) * 400].rearrange("p (h c) -> p h c", h=HEADS) for i in range(TT)]
        posf = [tk[:, 2540:2668], tk[:, 3498:3626]]

        def quarter(q):
            return eqbuf[:, q * 32 * NCAND:(q + 1) * 32 * NCAND]

        h2 = tiles(oneh[:, :], KT)
        gel = arena[:, :].rearrange("p (i t) -> p i t", t=T)
        sq3 = sq1
        y = tiles(arena[:, 0:KT * T], KT)
        acc = [arena[:, (24 + 2 * n) * T:(26 + 2 * n) * T] for n in range(4)]
        raw = [ring[:, s * D:(s + 1) * D] for s in range(SLOTS)]
        part_hi = [t[:, s * 512:(s + 1) * 512] for t in (tile_hi, h2_hi) for s in range(SLOTS)]
        part_lo = [t[:, s * 512:(s + 1) * 512] for t in (tile_lo, h2_lo) for s in range(SLOTS)]
        h2h, h2l = tiles(h2_hi[:, :], KT), tiles(h2_lo[:, :], KT)
        ohj = [oneh[:, s * P:(s + 1) * P] for s in range(2 * TOKS)]
        ohj4 = [oneh[:, s * 512:(s + 1) * 512].rearrange("p (t j) -> p t j", t=TOKS) for s in range(2)]
        ohi = [oneh[:, 1024 + s * IH:1024 + (s + 1) * IH] for s in range(2 * TOKS)]

        w1k = ring[0:DH, 0:2048].rearrange("p (l e) -> p l e", l=CMP_LEN)
        w1v = ring[0:DH, 2048:4096].rearrange("p (l e) -> p l e", l=CMP_LEN)
        ada_sum += [ring[:, 2048 + i * 512:2048 + (i + 1) * 512] for i in range(4)]
        ssb = [ring[:, i * 512:(i + 1) * 512] for i in range(2)]
        pT = [ring[:, 1024 + i * 512:1024 + (i + 1) * 512] for i in range(2)]
        o_nsa = [oneh[:, i * 512:(i + 1) * 512] for i in range(2)]
        o_dsa = [oneh[:, 1024 + i * 512:1024 + (i + 1) * 512] for i in range(2)]

        B = [ctx.enter_context(nc.psum_tensor(f"bank{i}", [P, 512], F32)) for i in range(8)]

        par_in, x_in, tab_in, sk_in = sem("par_in"), sem("x_in"), sem("tab_in"), sem("sk_in")
        w1_in, w2_in, out_done = sem("w1_in"), sem("w2_in"), sem("out_done")
        w_in = [sem(f"w_in{s}") for s in range(WSLOTS)]
        tile_in = [sem(f"tile_in{s}") for s in range(SLOTS)]
        const_set, dve_step, act_step = sem("const_set"), sem("dve_step"), sem("act_step")
        cexp, silu_ready, sq_ready, ssq_ready = sem("cexp"), sem("silu_ready"), sem("sq_ready"), sem("ssq_ready")
        root_ready, h_ready, ada_done = sem("root_ready"), sem("h_ready"), sem("ada_done")
        ada_first, ada_summed, rstd_ready, x_scaled = sem("ada_first"), sem("ada_summed"), sem("rstd_ready"), sem("x_scaled")
        z_done, z_read, zv_ready, zk_ready = sem("z_done"), sem("z_read"), sem("zv_ready"), sem("zk_ready")
        roped, job_done, job_out = sem("roped"), sem("job_done"), sem("job_out")
        ck_sum, ck_root, ck_ready = sem("ck_sum"), sem("ck_root"), sem("ck_ready")
        gexp = sem("gexp")
        logit_done, relu_done, relu_used = sem("logit_done"), sem("relu_done"), sem("relu_used")
        blk_ready, hid_done, hid_in, tanh_done = sem("blk_ready"), sem("hid_done"), sem("hid_in"), sem("tanh_done")
        hid_ready, cmpkv_done, cmpkv_ready = sem("hid_ready"), sem("cmpkv_done"), sem("cmpkv_ready")
        cs_done, cs_in, cexp_done, pc_ready = sem("cs_done"), sem("cs_in"), sem("cexp_done"), sem("pc_ready")
        pct_done, pct_ready, oc_done, oc_read = sem("pct_done"), sem("pct_ready"), sem("oc_done"), sem("oc_read")
        s_done, s_masked, p_ready, pt_done = sem("s_done"), sem("s_masked"), sem("p_ready"), sem("pt_done")
        pt_ready, o_unit, o_read = sem("pt_ready"), sem("o_unit"), sem("o_read")
        fill_done, fill_out = sem("fill_done"), sem("fill_out")
        o_ready, ot_done, ot_ready = sem("o_ready"), sem("ot_done"), sem("ot_ready")
        gates_ready, br_done, merged_ready = sem("gates_ready"), sem("br_done"), sem("merged_ready")
        mo_done, x1_ready, sq2_ready = sem("mo_done"), sem("x1_ready"), sem("sq2_ready")
        ssq2_ready, root2_ready, h2_ready = sem("ssq2_ready"), sem("root2_ready"), sem("h2_ready")
        h2_scaled = sem("h2_scaled")
        q2_done, q2_ready, sub_done, sub_ready = sem("q2_done"), sem("q2_ready"), sem("sub_done"), sem("sub_ready")
        pos_ready, matched, picked, eid_ready = sem("pos_ready"), sem("matched"), sem("picked"), sem("eid_ready")
        top_ready, gate_exp, route_ready = sem("top_ready"), sem("gate_exp"), sem("route_ready")
        rt_done, rt_ready = sem("rt_done"), sem("rt_ready")
        oh_ready, g_done, weighed = sem("oh_ready"), sem("g_done"), sem("weighed")
        h2_hi_ready, h2_lo_ready, tile_used = sem("h2_hi_ready"), sem("h2_lo_ready"), sem("tile_used")
        hi_ready, part_used = sem("hi_ready"), sem("part_used")
        lo_ready = [sem(f"lo_ready{half}") for half in range(2)]
        gelu_done, ah_ready, al_ready = sem("gelu_done"), sem("ah_ready"), sem("al_ready")
        acc_out, accT_done, accT_out = sem("acc_out"), sem("accT_done"), sem("accT_out")
        x2_ready, sq3_ready, ssq3_ready, root3_ready = sem("x2_ready"), sem("sq3_ready"), sem("ssq3_ready"), sem("root3_ready")
        y_ready = sem("y_ready")

        def chunk(eng, kind, m):
            n = CHUNK_NO[kind, m]
            eng.wait_ge(w_in[n % WSLOTS], 16 * (n // WSLOTS + 1))
            return wslot[n % WSLOTS]

        def ada_buffer(m, parity):
            return ada_sum[4 * (m >= 4) + 2 * (m % 2) + parity]

        block = ctx.enter_context(nc.Block())

        @block.sync
        def _(sp):
            sp.dma_start(par[:, :], A["par"]).then_inc(par_in, 16)
            sp.dma_start(x3, A["x"].rearrange("(k p) t -> p k t", p=P)).then_inc(x_in, 16)
            split = {"ada": A["ada_w"], "win": A["w_in"], "gate": A["w_gate"], "out": A["w_out"], "wq": A["peer_wq"]}
            for n, (kind, m) in enumerate(LOADS):
                if n >= WSLOTS:
                    old, i = LOADS[n - WSLOTS]
                    sp.wait_ge(*{"ada": (ada_summed, i + 1), "win": (z_done, 2 * i + 2), "gate": (fill_done, 4 * i + 4),
                                 "br": (br_done, KT), "out": (mo_done, 4 * i + 4)}[old])
                slot = wslot[n % WSLOTS]
                if kind == "br":
                    src = A["w_br"][m].rearrange("(k p) n -> p k n", p=P)
                    dst = slot.rearrange("p (k n) -> p k n", k=4)
                else:
                    first, cols = (CHUNK_AT[m], CHUNK_COLS[m]) if kind == "win" else (512 * m, 512)
                    src = split[kind].rearrange("(k p) n -> p k n", p=P)[:, :, first:first + cols]
                    dst = slot.rearrange("p (k n) -> p k n", k=KT)[:, :, 0:cols]
                sp.dma_start(dst, src).then_inc(w_in[n % WSLOTS], 16)
                if (kind, m) == ("win", 1):
                    sp.dma_start(w1k, A["cmp_w1_k"]).then_inc(w1_in, 16)
                    sp.dma_start(w1v, A["cmp_w1_v"]).then_inc(w1_in, 16)
            sp.wait_ge(ot_ready, 4)
            sp.dma_start(skT, A["subkeys"]).then_inc(sk_in, 16)
            for s in range(SLOTS):
                sp.dma_start(raw[s].rearrange("p (k j) -> p k j", k=KT), A["uT"][s]).then_inc(tile_in[s], 16)
            with sp.Fori(1, WHOLE // SLOTS + 1) as turn:
                for s in range(SLOTS):
                    sp.wait_ge(tile_used, turn * SLOTS + (s + 1 - SLOTS))
                    sp.dma_start(raw[s].rearrange("p (k j) -> p k j", k=KT),
                                 A["uT"][bass.ds(turn * SLOTS + s, 1)].rearrange("a p k j -> p (a k) j")).then_inc(tile_in[s], 16)
            with sp.Fori(WHOLE // SLOTS + 1, KEYS // SLOTS) as turn:
                for s in range(SLOTS):
                    for half in range(2):
                        sp.wait_ge(lo_ready[half], turn * SLOTS + (s + 1 - SLOTS - WHOLE))
                    sp.dma_start(raw[s].rearrange("p (k j) -> p k j", k=KT),
                                 A["uT"][bass.ds(turn * SLOTS + s, 1)].rearrange("a p k j -> p (a k) j")).then_inc(tile_in[s], 16)
            with sp.Fori(0, KEYS // SLOTS) as turn:
                for s in range(SLOTS):
                    for half in range(2):
                        sp.wait_ge(lo_ready[half], turn * SLOTS + (KEYS + s + 1 - SLOTS - WHOLE))
                    sp.dma_start(raw[s], A["v"][bass.ds(turn * SLOTS + s, 1)].rearrange("a p d -> p (a d)")).then_inc(tile_in[s], 16)
            for m in range(KT):
                sp.wait_ge(y_ready, m + 1)
                sp.dma_start(out[m * P:(m + 1) * P, :], y[:, m, :]).then_inc(out_done, 16)
            sp.wait_ge(out_done, 16 * KT)

        @block.tensor
        def _(pe):
            def ada(m):
                pe.wait_ge(ada_summed, m + 1)
                for c in range(4):
                    last = nc.tensor.matmul(B[7][:, 4 * m + c:4 * m + c + 1], ada_buffer(m, 0)[:, c * P:(c + 1) * P],
                                            ones[:, 0:1], start=True, stop=True)
                last.then_inc(ada_done, 1)

            def square_sum(bank, src, ready, done):
                for k in range(KT):
                    pe.wait_ge(ready, k + 1)
                    last = nc.tensor.matmul(B[bank][:, 0:T], ones[:, :], src[:, k, :], start=(k == 0), stop=(k == KT - 1))
                last.then_inc(done, 1)

            pe.wait_ge(const_set, 1)
            square_sum(0, sq1, sq_ready, ssq_ready)
            for m in range(4):
                ada(m)

            def project(c, pos):
                w = chunk(pe, "win", c).rearrange("p (k n) -> p k n", k=KT)
                for tt in range(TT):
                    n = 2 * pos + tt
                    if c == 0 and tt == 0:
                        pe.wait_ge(h_ready, KT)
                    if pos in (2, 3):
                        pe.wait_ge(z_read, n - 3)
                    if pos == 4:
                        pe.wait_ge(zv_ready, tt + 1)
                    for k in range(KT):
                        last = nc.tensor.matmul(B[n % 4][:, 0:CHUNK_COLS[c]], hT[:, k, tt * P:(tt + 1) * P],
                                                w[:, k, 0:CHUNK_COLS[c]], start=(k == 0), stop=(k == KT - 1))
                    last.then_inc(z_done, 1)

            def job(n):
                kind, *what = JOBS[n]
                bank = B[4 + n % 3]
                if n >= 3:
                    pe.wait_ge(job_out, n - 2)
                if kind == "rope":
                    r, h, count, _, _, _ = what
                    pe.wait_ge(roped, r + 1)
                    for i in range(count):
                        last = nc.tensor.transpose(bank[0:DH, i * P:(i + 1) * P],
                                                   rq[r % 2][:, (h + i) * DH:(h + i + 1) * DH], ident)
                elif kind == "ckv":
                    tt, = what
                    pe.wait_ge(ck_ready, tt + 1)
                    nc.tensor.transpose(bank[:, 0:P], zv[:, tt, 0:P], ident)
                    for g in range(2):
                        last = nc.tensor.transpose(bank[0:DH, (1 + g) * P:(2 + g) * P],
                                                   zv[:, tt, P + g * DH:P + (g + 1) * DH], ident)
                else:
                    tt, = what
                    pe.wait_ge(job_out, n - 1)
                    last = nc.tensor.matmul(bank[:, 0:2 * DH], ckvT[:, tt * P:(tt + 1) * P], wukv[:, :], start=True, stop=True)
                last.then_inc(job_done, 1)

            pe.wait_ge(tab_in, 16)
            project(0, 0)
            project(1, 1)
            for n in range(0, 4):
                job(n)
            project(2, 2)
            for n in range(4, 8):
                job(n)
            project(3, 3)
            job(8)
            job(9)
            project(4, 4)
            pe.wait_ge(w2_in, 48)
            for n in range(10, len(JOBS)):
                job(n)

            for q in range(8):
                tt, hp = divmod(q, 4)
                ns = (tt + 1) * P
                if q == 0:
                    pe.wait_ge(job_out, len(JOBS))
                    pe.wait_ge(z_read, 10 - 2)
                if q >= 4:
                    pe.wait_ge(relu_done, q - 3)
                for i in range(2):
                    last = nc.tensor.matmul(B[q % 4][:, i * ns:(i + 1) * ns], qT[:, QI + 2 * hp + i, tt * P:(tt + 1) * P],
                                            kT[:, KI, 0:ns], start=True, stop=True)
                last.then_inc(logit_done, 1)

            def gate(m):
                w = chunk(pe, "gate", m // 4).rearrange("p (k n) -> p k n", k=KT)
                if m:
                    pe.wait_ge(fill_out, m)
                for k in range(KT):
                    last = nc.tensor.matmul(B[6][:, 0:T], w[:, k, (m % 4) * P:(m % 4 + 1) * P], hT[:, k, :],
                                            start=(k == 0), stop=(k == KT - 1))
                last.then_inc(fill_done, 1)

            pe.wait_ge(w1_in, 32)
            pe.wait_ge(blk_ready, 1)
            for v, w1 in enumerate((w1k, w1v)):
                for l in range(CMP_LEN):
                    last = nc.tensor.matmul(B[4 + v][0:DH, 0:2 * NCMP], w1[:, l, :], blk[:, v, l, :],
                                            start=(l == 0), stop=(l == CMP_LEN - 1))
            last.then_inc(hid_done, 1)
            gate(0)
            pe.wait_ge(hid_ready, 1)
            nc.tensor.matmul(B[7][0:DH, P:P + 2 * NCMP], w2kv[:, 0:DH], hid[:, 300:330], start=True, stop=True)
            nc.tensor.matmul(B[7][0:HEADS * NCMP, T:T + DH], hidrep, w2kv[:, DH:2 * DH], start=True, stop=True).then_inc(cmpkv_done, 1)
            gate(1)
            pe.wait_ge(cmpkv_ready, 2)
            pe.wait_ge(relu_done, 8)
            for tt in range(TT):
                for h in range(HEADS):
                    last = nc.tensor.matmul(B[tt][:, h * NCMP:(h + 1) * NCMP], qT[:, QN + h, tt * P:(tt + 1) * P],
                                            kcmpT[:, (h // 4) * NCMP:(h // 4 + 1) * NCMP], start=True, stop=True)
                last.then_inc(cs_done, 1)
            gate(2)
            for tt in range(TT):
                pe.wait_ge(pc_ready, tt + 1)
                nc.tensor.transpose(B[2 + tt][0:HEADS * NCMP, 0:P], pc[:, tt, :], ident).then_inc(pct_done, 1)
            gate(3)
            for tt in range(TT):
                pe.wait_ge(pct_ready, tt + 1)
                nc.tensor.matmul(B[4 + tt][:, :], pcT[tt][0:HEADS * NCMP, :], vbd[0:HEADS * NCMP, :],
                                 start=True, stop=True).then_inc(oc_done, 1)

            for u in range(len(UNITS) + 2):
                if u < len(UNITS):
                    b, tt, hp = UNITS[u]
                    ns = (tt + 1) * P
                    _, q0, k0, _ = BRANCHES[b]
                    if u >= 2:
                        pe.wait_ge(s_masked, u - 1)
                    for i in range(2):
                        h = 2 * hp + i
                        kh = k0 if b == 2 else k0 + h // 4
                        last = nc.tensor.matmul(B[u % 2][:, i * ns:(i + 1) * ns], qT[:, q0 + h, tt * P:(tt + 1) * P],
                                                kT[:, kh, 0:ns], start=True, stop=True)
                    last.then_inc(s_done, 1)
                    if u and u % 3 == 0:
                        ada(3 + u // 3)
                    if UNIT_GATE[u] is not None:
                        gate(UNIT_GATE[u])
                if 0 <= u - 1 < len(UNITS):
                    b, tt, hp = UNITS[u - 1]
                    ns = (tt + 1) * P
                    pe.wait_ge(p_ready, u)
                    if u - 1 >= 2:
                        pe.wait_ge(pt_ready, u - 2)
                    for i in range(2):
                        for s in range(tt + 1):
                            last = nc.tensor.transpose(B[2 + (u - 1) % 2][:, (i * (tt + 1) + s) * P:(i * (tt + 1) + s + 1) * P],
                                                       ssb[(u - 1) % 2][:, i * ns + s * P:i * ns + (s + 1) * P], ident)
                    last.then_inc(pt_done, 1)
                if u - 2 >= 0:
                    b, tt, hp = UNITS[u - 2]
                    g = (u - 2) // 4
                    pe.wait_ge(pt_ready, u - 1)
                    if hp == 0:
                        if g < 2:
                            pe.wait_ge(oc_read, g + 1)
                        else:
                            pe.wait_ge(o_read, g - 1)
                    for i in range(2):
                        h = 2 * hp + i
                        for s in range(tt + 1):
                            if b == 2:
                                v = kdv[:, s, DH:2 * DH]
                            else:
                                first = (2 + b) * P + (h // 4) * DH
                                v = zv[:, s, first:first + DH]
                            last = nc.tensor.matmul(B[4 + g % 2][:, h * DH:(h + 1) * DH],
                                                    pT[(u - 2) % 2][:, (i * (tt + 1) + s) * P:(i * (tt + 1) + s + 1) * P],
                                                    v, start=(s == 0), stop=(s == tt))
                    last.then_inc(o_unit, 1)

            ada(11)
            for n in range(4):
                b, tt = divmod(n, 2)
                pe.wait_ge(o_ready, 1)
                src = (o_nsa, o_dsa)[b][tt]
                for k in range(4):
                    last = nc.tensor.transpose(B[n][:, k * P:(k + 1) * P], src[:, k * P:(k + 1) * P], ident)
                last.then_inc(ot_done, 1)
            wb = [chunk(pe, "br", b).rearrange("p (k n) -> p k n", k=4) for b in range(2)]
            pe.wait_ge(ot_ready, 4)
            for m in range(KT):
                if m >= 2:
                    pe.wait_ge(merged_ready, m - 1)
                for b in range(2):
                    for k in range(4):
                        last = nc.tensor.matmul(B[4 + m % 2][:, b * T:(b + 1) * T], wb[b][:, k, m * P:(m + 1) * P],
                                                oT[:, b, k, :], start=(k == 0), stop=(k == 3))
                last.then_inc(br_done, 1)
            pe.wait_ge(merged_ready, KT)
            for m in range(KT):
                if m % 4 == 0:
                    w = chunk(pe, "out", m // 4).rearrange("p (k n) -> p k n", k=KT)
                if m >= 2:
                    pe.wait_ge(x1_ready, m - 1)
                for k in range(KT):
                    last = nc.tensor.matmul(B[m % 2][:, 0:T], w[:, k, (m % 4) * P:(m % 4 + 1) * P], hT[:, k, :],
                                            start=(k == 0), stop=(k == KT - 1))
                last.then_inc(mo_done, 1)
            square_sum(2, sq2, sq2_ready, ssq2_ready)
            for m in range(KT):
                if m % 4 == 0:
                    w = chunk(pe, "wq", m // 4).rearrange("p (k n) -> p k n", k=KT)
                if m >= 2:
                    pe.wait_ge(q2_ready, m - 1)
                for k in range(KT):
                    if m == 0:
                        pe.wait_ge(h2_ready, k + 1)
                    last = nc.tensor.matmul(B[m % 2][:, 0:T], w[:, k, (m % 4) * P:(m % 4 + 1) * P], h2[:, k, :],
                                            start=(k == 0), stop=(k == KT - 1))
                last.then_inc(q2_done, 1)
            pe.wait_ge(q2_ready, KT)
            pe.wait_ge(sk_in, 16)
            for n in range(8):
                tt, hq, c = n // 4, n // 2 % 2, n % 2
                if n >= 4:
                    pe.wait_ge(sub_ready, n - 3)
                for i in range(4):
                    h = 4 * hq + i
                    last = nc.tensor.matmul(B[4 + n % 4][:, i * KEYS:(i + 1) * KEYS], q2T[c * DH:(c + 1) * DH, h, tt * P:(tt + 1) * P],
                                            skT[c * DH:(c + 1) * DH, h * KEYS:(h + 1) * KEYS], start=True, stop=True)
                last.then_inc(sub_done, 1)
            def act_tile(s, arrived):
                pe.wait_ge(tile_in[s], arrived)
                for k in range(KT):
                    last = nc.tensor.matmul(B[4 + s % 2][:, 0:T], raw[s][:, k * P:(k + 1) * P], h2[:, k, :],
                                            start=(k == 0), stop=(k == KT - 1))
                last.then_inc(tile_used, 1)

            def split_act_tile(s, tile):
                bank = B[4 + s % 2]
                for half in range(2):
                    slot = (2 * s + half) % SLOTS
                    pe.wait_ge(lo_ready[half], tile + 1)
                    w_hi = part_hi[slot].rearrange("p (k j) -> p k j", k=4)
                    w_lo = part_lo[slot].rearrange("p (k j) -> p k j", k=4)
                    for k in range(4):
                        kk = 4 * half + k
                        nc.tensor.matmul(bank[:, 0:T], w_hi[:, k, :], h2h[:, kk, :], start=(kk == 0), stop=False)
                        nc.tensor.matmul(bank[:, 0:T], w_hi[:, k, :], h2l[:, kk, :], start=False, stop=False)
                        last = nc.tensor.matmul(bank[:, 0:T], w_lo[:, k, :], h2h[:, kk, :], start=False, stop=(kk == KT - 1))
                    last.then_inc(part_used, 1)

            def route_group(group, slot):
                pe.wait_ge(oh_ready, group + 1)
                for t in range(TOKS):
                    s = slot * TOKS + t
                    last = nc.tensor.matmul(B[6 + slot][:, t * IH:(t + 1) * IH], ohj[s], ohi[s], start=True, stop=True)
                last.then_inc(g_done, 1)

            def v_tile(s, tile, n, start=False, stop=False):
                pe.wait_ge(al_ready, n + 1)
                for half in range(2):
                    slot = 2 * s + half
                    pe.wait_ge(lo_ready[half], tile + 1)
                    for tt in range(TT):
                        at = (s % 2) * T + tt * P
                        bank = B[2 * tt + half]
                        nc.tensor.matmul(bank[:, :], a_hi[:, at:at + P], part_hi[slot], start=start, stop=False)
                        nc.tensor.matmul(bank[:, :], a_hi[:, at:at + P], part_lo[slot], start=False, stop=False)
                        last = nc.tensor.matmul(bank[:, :], a_lo[:, at:at + P], part_hi[slot], start=False, stop=stop)
                    last.then_inc(part_used, 1)

            pe.wait_ge(sub_ready, 8)
            for s in range(SLOTS):
                if s >= 2:
                    pe.wait_ge(gelu_done, s - 1)
                act_tile(s, 16)
            with pe.Fori(1, WHOLE // SLOTS) as turn:
                for s in range(SLOTS):
                    pe.wait_ge(gelu_done, turn * SLOTS + (s - 1))
                    act_tile(s, turn * 16 + 16)
            pe.wait_ge(h2_lo_ready, 1)
            for first, end in ((WHOLE // SLOTS, RT_TURN), (RT_TURN, IH // SLOTS)):
                if first == RT_TURN:
                    pe.wait_ge(route_ready, 1)
                    for tt in range(TT):
                        for i in range(3):
                            last = nc.tensor.transpose(B[tt][:, i * P:(i + 1) * P], route[:, tt, i, :], ident)
                    last.then_inc(rt_done, 1)
                with pe.Fori(first, end) as turn:
                    for s in range(SLOTS):
                        pe.wait_ge(gelu_done, turn * SLOTS + (s - 1))
                        split_act_tile(s, turn * SLOTS + (s - WHOLE))
            def phase2(turn, first=False):
                for s in range(SLOTS):
                    pe.wait_ge(gelu_done, turn * SLOTS + (IH + s - 1))
                    split_act_tile(s, turn * SLOTS + (IH + s - WHOLE))
                    if s >= 2 or not first:
                        pe.wait_ge(weighed, turn * SLOTS + (s - 1))
                    route_group(turn * SLOTS + s, s % 2)

            phase2(0, first=True)
            with pe.Fori(1, IH // SLOTS) as turn:
                phase2(turn)

            def phase3(turn, first=False):
                for s in range(SLOTS):
                    v_tile(s, turn * SLOTS + (KEYS + s - WHOLE), turn * SLOTS + s, start=(first and s == 0))
                    pe.wait_ge(weighed, turn * SLOTS + (IH + s - 1))
                    route_group(turn * SLOTS + (IH + s), s % 2)

            phase3(0, first=True)
            with pe.Fori(1, IH // SLOTS) as turn:
                phase3(turn)
            with pe.Fori(IH // SLOTS, KEYS // SLOTS - 1) as turn:
                for s in range(SLOTS):
                    v_tile(s, turn * SLOTS + (KEYS + s - WHOLE), turn * SLOTS + s)
            for s in range(SLOTS):
                n = KEYS - SLOTS + s
                v_tile(s, KEYS - WHOLE + n, n, stop=(s == SLOTS - 1))
            pe.wait_ge(acc_out, 4)
            for n in range(4):
                for i in range(2):
                    k = 2 * n + i
                    for tt in range(TT):
                        src = acc[2 * tt + k // 4][:, (k % 4) * P:(k % 4 + 1) * P]
                        last = nc.tensor.transpose(B[4 + n][:, i * T + tt * P:i * T + (tt + 1) * P], src, ident)
                last.then_inc(accT_done, 1)
            square_sum(0, sq3, sq3_ready, ssq3_ready)

        @block.gpsimd
        def _(pool):
            pool.wait_ge(x_in, 16)
            pool.wait_ge(rstd_ready, 1)
            nc.gpsimd.tensor_tensor(hT, x3, rstd[:, :].unsqueeze(1).to_broadcast([P, KT, T]), ALU.mult).then_inc(x_scaled, 1)

            pool.wait_ge(h2_hi_ready, 1)
            nc.gpsimd.tensor_tensor(h2_lo[:, :], oneh[:, :], h2_hi[:, :].bitcast(F32), ALU.subtract).then_inc(h2_lo_ready, 1)

            for tt in range(TT):
                for q in range(4):
                    pool.wait_ge(matched, 4 * tt + q + 1)
                    eq = quarter(q).rearrange("p (h k c) -> p h k c", h=2, k=TOPK)
                    nc.gpsimd.tensor_tensor(eq, eq, cidx[tt][:, 2 * q:2 * q + 2, :].unsqueeze(2).to_broadcast([P, 2, TOPK, NCAND]),
                                            ALU.mult).then_inc(picked, 1)

            def lo_part(s, slot, tile):
                pool.wait_ge(hi_ready, tile * 2 + 2)
                nc.gpsimd.tensor_tensor(part_lo[slot], raw[s][:, 512:1024], part_hi[slot].bitcast(F32),
                                        ALU.subtract).then_inc(lo_ready[1], 1)

            def a_part(n, s):
                pool.wait_ge(ah_ready, n + 1)
                at = (s % 2) * T
                nc.gpsimd.tensor_tensor(a_lo[:, at:at + T], gel[:, bass.ds(n, 1), :].rearrange("p a t -> p (a t)"),
                                        a_hi[:, at:at + T].bitcast(F32), ALU.subtract).then_inc(al_ready, 1)

            with pool.Fori(0, (KEYS - WHOLE) // SLOTS) as turn:
                for s in range(SLOTS):
                    lo_part(s, (2 * s + 1) % SLOTS, turn * SLOTS + s)
            for s in range(2):
                lo_part(s, 2 * s + 1, KEYS - WHOLE + s)

            def v_body(turn, end=False):
                for s in range(SLOTS):
                    n = turn * SLOTS + s
                    if not (isinstance(n, int) and n + 2 >= KEYS):
                        lo_part((s + 2) % SLOTS, (2 * s + 5) % (2 * SLOTS), n + (KEYS - WHOLE + 2))
                    if not (end and s == SLOTS - 1):
                        a_part(n + 1, s + 1)

            for half in range(2):
                a_part(half * IH, 0)
                with pool.Fori(half * (IH // SLOTS), (half + 1) * (IH // SLOTS) - 1) as turn:
                    v_body(turn)
                v_body((half + 1) * (IH // SLOTS) - 1, end=True)

        @block.scalar
        def _(act):
            steps = [0]

            def link(ins):
                steps[0] += 1
                ins.then_inc(act_step, 1)
                act.wait_ge(act_step, steps[0])

            act.dma_start(tab[:, :], A["tab"]).then_inc(tab_in, 16)
            act.dma_start(wukv[:, :], A["w_ukv"]).then_inc(w2_in, 16)
            act.dma_start(w2kv[:, :], A["cmp_w2"]).then_inc(w2_in, 16)
            act.dma_start(posT[:, :], A["cmp_pos"]).then_inc(w2_in, 16)
            act.wait_ge(par_in, 16)
            nc.scalar.activation(silu[:, KT:2 * KT], param("c"), ACT.Exp, scale=-1.0).then_inc(cexp, 1)
            act.wait_ge(x_in, 16)
            for k in range(KT):
                nc.scalar.activation(sq1[:, k, :], x3[:, k, :], ACT.Square).then_inc(sq_ready, 1)
            act.wait_ge(const_set, 1)
            act.wait_ge(ssq_ready, 1)
            nc.scalar.activation(rstd[:, :], B[0][:, 0:T], ACT.Sqrt, bias=eps[:, 0:1], scale=1.0 / D).then_inc(root_ready, 1)

            def ada_start(m):
                w = chunk(act, "ada", m).rearrange("p (k n) -> p k n", k=KT)
                if m >= 2:
                    act.wait_ge(ada_done, m - 1)
                for k in range(2):
                    nc.scalar.activation(ada_buffer(m, k), w[:, k, :], ACT.Identity, scale=silu[:, k:k + 1]).then_inc(ada_first, 1)

            act.wait_ge(silu_ready, 1)
            for m in range(4):
                ada_start(m)

            def job_copy(n):
                kind, *what = JOBS[n]
                bank = B[4 + n % 3]
                act.wait_ge(job_done, n + 1)
                if kind == "rope":
                    r, _, count, to, head, tt = what
                    dst = (qT if to == "q" else kT)[:, head:head + count, tt * P:(tt + 1) * P]
                    last = nc.scalar.activation(dst, bank[0:DH, 0:count * P].rearrange("p (h t) -> p h t", h=count), ACT.Copy)
                elif kind == "ckv":
                    tt, = what
                    nc.scalar.activation(kT[:, VC:VC + 2, tt * P:(tt + 1) * P],
                                         bank[0:DH, P:3 * P].rearrange("p (h t) -> p h t", h=2), ACT.Copy)
                    last = nc.scalar.activation(ckvT[:, tt * P:(tt + 1) * P], bank[:, 0:P], ACT.Identity, scale=param("kvg"))
                else:
                    tt, = what
                    last = nc.scalar.activation(kdv[:, tt, :], bank[:, 0:2 * DH], ACT.Copy)
                last.then_inc(job_out, 1)

            for n in range(0, 4):
                job_copy(n)
            for tt in range(TT):
                act.wait_ge(z_done, 4 + tt + 1)
                nc.scalar.activation(zv[:, tt, :], B[tt][:, :], ACT.Copy).then_inc(zv_ready, 1)
            for n in range(4, 8):
                job_copy(n)
            for tt in range(TT):
                act.wait_ge(ck_sum, tt + 1)
                nc.scalar.activation(small[:, 2 + tt:3 + tt], small[:, tt:tt + 1], ACT.Sqrt,
                                     bias=eps[:, 0:1], scale=1.0 / P).then_inc(ck_root, 1)
            for n in range(8, len(JOBS)):
                job_copy(n)

            act.wait_ge(zk_ready, 2)
            nc.scalar.activation(ssig[:, :].rearrange("p (a n) -> p a n", a=TT), zk[:, :, 0:24], ACT.Exp, scale=-1.0).then_inc(gexp, 1)
            for q in range(8):
                ns = (q // 4 + 1) * P
                act.wait_ge(logit_done, q + 1)
                if q >= 2:
                    act.wait_ge(relu_used, q - 1)
                nc.scalar.activation(relu[q % 2][:, 0:2 * ns], B[q % 4][:, 0:2 * ns], ACT.Relu, scale=DH ** -0.5).then_inc(relu_done, 1)
            def gate_copy(m):
                act.wait_ge(fill_done, m + 1)
                nc.scalar.activation(gates[:, m, :], B[6][:, 0:T], ACT.Copy).then_inc(fill_out, 1)

            act.wait_ge(hid_in, 1)
            nc.scalar.activation(hid[:, 120:180], hid[:, 120:180], ACT.Tanh, scale=float(np.sqrt(2.0 / np.pi))).then_inc(tanh_done, 1)
            act.wait_ge(hid_done, 1)
            gate_copy(0)
            gate_copy(1)
            for tt in range(TT):
                act.wait_ge(cs_in, tt + 1)
                nc.scalar.activation(pc[:, tt, :], pc[:, tt, :], ACT.Exp, scale=DH ** -0.5).then_inc(cexp_done, 1)
            gate_copy(2)
            for tt in range(TT):
                act.wait_ge(pct_done, tt + 1)
                nc.scalar.activation(pcT[tt][0:HEADS * NCMP, :], B[2 + tt][0:HEADS * NCMP, 0:P], ACT.Copy).then_inc(pct_ready, 1)
            gate_copy(3)

            for u in range(len(UNITS) + 1):
                if u < len(UNITS):
                    b, tt, hp = UNITS[u]
                    ns = (tt + 1) * P
                    act.wait_ge(s_masked, u + 1)
                    for i in range(2):
                        last = nc.scalar.activation(ssb[u % 2][:, i * ns:(i + 1) * ns], ssb[u % 2][:, i * ns:(i + 1) * ns], ACT.Exp,
                                                    bias=negmax[:, 2 * (u % 2) + i:2 * (u % 2) + i + 1],
                                                    accum_out=rowsum[:, 2 * u + i:2 * u + i + 1])
                    last.then_inc(p_ready, 1)
                if u >= 1:
                    tt = UNITS[u - 1][1]
                    n = 2 * (tt + 1) * P
                    act.wait_ge(pt_done, u)
                    if u - 1 >= 2:
                        act.wait_ge(o_unit, u - 2)
                    nc.scalar.activation(pT[(u - 1) % 2][:, 0:n], B[2 + (u - 1) % 2][:, 0:n], ACT.Copy).then_inc(pt_ready, 1)
                if u < len(UNITS):
                    if UNIT_GATE[u] is not None:
                        gate_copy(UNIT_GATE[u])
            act.wait_ge(fill_out, 16)
            for i in range(KT // 2):
                g = gates.rearrange("p (b m) t -> p b m t", b=2)[:, :, 2 * i:2 * i + 2, :]
                nc.scalar.activation(g, g, ACT.Sigmoid).then_inc(gates_ready, 1)
            for n in range(4):
                b, tt = divmod(n, 2)
                act.wait_ge(ot_done, n + 1)
                nc.scalar.activation(oT[:, b, :, tt * P:(tt + 1) * P], B[n][:, :].rearrange("p (k t) -> p k t", k=4),
                                     ACT.Copy).then_inc(ot_ready, 1)
            nc.scalar.activation(small[:, 9:10], eps[:, 0:1], ACT.Sqrt)
            for k in range(KT):
                act.wait_ge(x1_ready, k + 1)
                nc.scalar.activation(sq2[:, k, :], x3[:, k, :], ACT.Square).then_inc(sq2_ready, 1)
            act.wait_ge(ssq2_ready, 1)
            nc.scalar.activation(rstd[:, :], B[2][:, 0:T], ACT.Sqrt, bias=eps[:, 0:1], scale=1.0 / D).then_inc(root2_ready, 1)
            for k in range(KT):
                act.wait_ge(h2_scaled, k + 1)
                nc.scalar.activation(h2[:, k, :], h2[:, k, :], ACT.Identity, bias=mod[:, 3 * KT + k:3 * KT + k + 1]).then_inc(h2_ready, 1)
            for m in range(KT):
                act.wait_ge(q2_done, m + 1)
                nc.scalar.activation(q2T[:, m, :], B[m % 2][:, 0:T], ACT.Copy).then_inc(q2_ready, 1)
            for n in range(8):
                tt, hq, c = n // 4, n // 2 % 2, n % 2
                act.wait_ge(sub_done, n + 1)
                nc.scalar.activation(sub[tt].rearrange("p (h c) n -> p h c n", c=2)[:, 4 * hq:4 * hq + 4, c, :], B[4 + n % 4][:, :].rearrange("p (s n) -> p s n", s=4),
                                     ACT.Copy).then_inc(sub_ready, 1)

            act.wait_ge(h2_ready, KT)
            nc.scalar.activation(h2_hi[:, :], oneh[:, :], ACT.Copy).then_inc(h2_hi_ready, 1)

            def gelu(n, s):
                return nc.scalar.activation(gel[:, bass.ds(n, 1), :].rearrange("p a t -> p (a t)"), B[4 + s % 2][:, 0:T], ACT.Gelu)

            def hi_part(s, half, slot, arrived, used):
                if half == 0:
                    act.wait_ge(tile_in[s], arrived)
                if used is not None:
                    act.wait_ge(part_used, used)
                nc.scalar.activation(part_hi[slot], raw[s][:, half * 512:(half + 1) * 512], ACT.Copy).then_inc(hi_ready, 1)

            def u_body(turn):
                for s in range(SLOTS):
                    n = turn * SLOTS + s
                    gelu(n, s).then_inc(gelu_done, 1)
                    if isinstance(n, int) and n == KEYS - 1:
                        return
                    s3, arrived = (s + 3) % SLOTS, (turn + ((s + 3) // SLOTS + 1)) * 16
                    act.wait_ge(part_used, n * 2 + (4 - 2 * WHOLE))
                    for half in range(2):
                        hi_part(s3, half, (2 * s3 + half) % SLOTS, arrived, None)

            def a_part(n, s):
                if not (isinstance(n, int) and n < 2):
                    act.wait_ge(part_used, n * 2 + 2 * (KEYS - WHOLE - 1))
                nc.scalar.activation(a_hi[:, (s % 2) * T:(s % 2 + 1) * T], gel[:, bass.ds(n, 1), :].rearrange("p a t -> p (a t)"),
                                     ACT.Copy).then_inc(ah_ready, 1)

            def v_body(turn, start=False, end=False):
                for s in range(SLOTS):
                    n = turn * SLOTS + s
                    s2, arrived = (s + 2) % SLOTS, (turn + (KEYS // SLOTS + (s + 2) // SLOTS + 1)) * 16
                    more = not (isinstance(n, int) and n + 2 >= KEYS)

                    def used(half):
                        return 2 * (KEYS - WHOLE) if start and s < 2 else n * 2 + (2 * (KEYS - WHOLE - 2) + half + 1)

                    if more:
                        for half in range(2):
                            hi_part(s2, half, 2 * s2 + half, arrived, used(half))
                    if not (end and s == SLOTS - 1):
                        a_part(n + 1, s + 1)

            bounds = (0, 5, WHOLE // SLOTS - 1)
            for tt in range(TT):
                with act.Fori(bounds[tt], bounds[tt + 1]) as turn:
                    for s in range(SLOTS):
                        act.wait_ge(tile_used, turn * SLOTS + (s + 1))
                        gelu(turn * SLOTS + s, s).then_inc(gelu_done, 1)
                if tt:
                    for s in range(SLOTS):
                        n = WHOLE - SLOTS + s
                        act.wait_ge(tile_used, n + 1)
                        gelu(n, s).then_inc(gelu_done, 1)
                        for half in range(2):
                            if s >= 2:
                                hi_part(s - 2, half, 2 * (s - 2) + half, 16 * (WHOLE // SLOTS + 1), None)
                act.wait_ge(top_ready, tt + 1)
                nc.scalar.activation(route[:, tt, 2, :], route[:, tt, 2, :], ACT.Exp).then_inc(gate_exp, 1)
            act.wait_ge(part_used, 2)
            for half in range(2):
                hi_part(2, half, half, 16 * (WHOLE // SLOTS + 1), None)
            with act.Fori(WHOLE // SLOTS, RT_TURN) as turn:
                u_body(turn)
            act.wait_ge(rt_done, 1)
            for tt in range(TT):
                nc.scalar.activation(tiles(routeT[:, :], 3)[:, :, tt * P:(tt + 1) * P], tiles(B[tt][:, 0:3 * P], 3),
                                     ACT.Copy).then_inc(rt_ready, 1)
            with act.Fori(RT_TURN, KEYS // SLOTS - 1) as turn:
                u_body(turn)
            u_body(KEYS // SLOTS - 1)
            for half in range(2):
                act.wait_ge(weighed, (half + 1) * (T // TOKS))
                a_part(half * IH, 0)
                first = half * (IH // SLOTS)
                if half == 0:
                    v_body(0, start=True)
                    first = 1
                with act.Fori(first, (half + 1) * (IH // SLOTS) - 1) as turn:
                    v_body(turn)
                v_body((half + 1) * (IH // SLOTS) - 1, end=True)
            act.wait_ge(part_used, 4 * KEYS - 2 * WHOLE)
            for n in range(2):
                nc.scalar.activation(acc[n], B[n][:, :], ACT.Copy).then_inc(acc_out, 1)
            nc.scalar.activation(small[:, 10:11], eps[:, 0:1], ACT.Sqrt)
            for k in range(KT):
                act.wait_ge(x2_ready, k + 1)
                nc.scalar.activation(sq3[:, k, :], x3[:, k, :], ACT.Square).then_inc(sq3_ready, 1)
            act.wait_ge(ssq3_ready, 1)
            nc.scalar.activation(rstd[:, :], B[0][:, 0:T], ACT.Sqrt, bias=eps[:, 0:1], scale=1.0 / D).then_inc(root3_ready, 1)

        @block.vector
        def _(dve):
            steps = [0]
            V = nc.vector

            def link(ins):
                steps[0] += 1
                ins.then_inc(dve_step, 1)
                dve.wait_ge(dve_step, steps[0])

            V.memset(eps[:, :], EPS)
            V.memset(ones[:, :], 1.0).then_inc(const_set, 1)
            dve.wait_ge(cexp, 1)
            link(V.tensor_scalar(silu[:, KT:2 * KT], silu[:, KT:2 * KT], 1.0, None, ALU.add))
            link(V.reciprocal(silu[:, 2 * KT:3 * KT], silu[:, KT:2 * KT]))
            V.tensor_tensor(silu[:, 0:KT], silu[:, 2 * KT:3 * KT], param("c"), ALU.mult).then_inc(silu_ready, 1)

            summed = {}

            def ada_step(m, k):
                w = chunk(dve, "ada", m).rearrange("p (k n) -> p k n", k=KT)[:, k, :]
                acc = ada_buffer(m, k % 2)
                if m >= 6 and k == 0:
                    dve.wait_ge(ada_done, m - 1)
                if m < 4 and k < 4:
                    dve.wait_ge(ada_first, 2 * m + k - 1)
                elif k >= 2:
                    dve.wait_ge(dve_step, summed[m, k - 2])
                if k < 2:
                    ins = V.tensor_scalar(acc, w, silu[:, k:k + 1], None, ALU.mult)
                else:
                    ins = V.scalar_tensor_tensor(acc, w, silu[:, k:k + 1], acc, ALU.mult, ALU.add)
                ins.then_inc(dve_step, 1)
                steps[0] += 1
                summed[m, k] = steps[0]
                if k == KT - 1:
                    dve.wait_ge(dve_step, steps[0])
                    V.tensor_tensor(ada_buffer(m, 0), ada_buffer(m, 0), acc, ALU.add).then_inc(ada_summed, 1)

            dve.wait_ge(silu_ready, 1)
            for m in range(4):
                if m == 1:
                    dve.wait_ge(root_ready, 1)
                    V.reciprocal(rstd[:, :], rstd[:, :]).then_inc(rstd_ready, 1)
                for k in range(2, KT):
                    ada_step(m, k)

            dve.wait_ge(ada_done, 4)
            link(V.tensor_tensor(mod[:, 0:2 * KT], B[7][:, 0:2 * KT], param("ada_b")[:, 0:2 * KT], ALU.add))
            link(V.tensor_scalar(scale1[:, :], mod[:, KT:2 * KT], 1.0, None, ALU.add))
            link(V.tensor_tensor(scale1[:, :], scale1[:, :], param("g1"), ALU.mult))
            dve.wait_ge(x_scaled, 1)
            for k in range(KT):
                V.tensor_scalar(hT[:, k, :], hT[:, k, :], scale1[:, k:k + 1], mod[:, k:k + 1], ALU.mult, ALU.add).then_inc(h_ready, 1)

            def rope(r):
                c, tt = ROPES[r]
                n = ROPE_HEADS[c]
                cols = n * DH
                if c == "kd":
                    dve.wait_ge(job_out, 10 + tt + 1)
                    src = kdv[:, tt, 0:DH]
                else:
                    pos = c
                    dve.wait_ge(z_done, 2 * pos + tt + 1)
                    src = B[(2 * pos + tt) % 4][:, 0:cols]
                z = src.rearrange("p (h s d) -> p h s d", s=2, d=HALF)
                ra = rope_a[:, 0:cols].rearrange("p (h s d) -> p h s d", s=2, d=HALF)
                rb = rope_b[:, 0:cols].rearrange("p (h s d) -> p h s d", s=2, d=HALF)
                cos = table("cos").rearrange("p (a d) -> p a d", a=TT)[:, tt, :]
                sin = table("sin").rearrange("p (a s d) -> p a s d", a=TT, s=2)[:, tt, :, :]
                cosb = cos.unsqueeze(1).unsqueeze(1).to_broadcast([P, n, 2, HALF])
                if r:
                    dve.wait_ge(roped, r)
                V.tensor_tensor(ra, z, cosb, ALU.mult)
                V.tensor_tensor(rb[:, :, 0, :], z[:, :, 1, :], sin[:, 0, :].unsqueeze(1).to_broadcast([P, n, HALF]), ALU.mult)
                last = V.tensor_tensor(rb[:, :, 1, :], z[:, :, 0, :], sin[:, 1, :].unsqueeze(1).to_broadcast([P, n, HALF]), ALU.mult)
                if c == "kd":
                    link(last)
                else:
                    last.then_inc(z_read, 1)
                    read[0] += 1
                    dve.wait_ge(z_read, read[0])
                if r >= 2:
                    dve.wait_ge(job_done, 1 + max(j for j, w in enumerate(JOBS) if w[0] == "rope" and w[1] == r - 2))
                V.tensor_tensor(rq[r % 2][:, 0:cols], rope_a[:, 0:cols], rope_b[:, 0:cols], ALU.add).then_inc(roped, 1)

            read = [0]
            dve.wait_ge(tab_in, 16)
            for r in range(2):
                rope(r)
            for r in range(2, 4):
                tt = ROPES[r][1]
                dve.wait_ge(z_done, 2 + tt + 1)
                V.tensor_copy(zk[:, tt, :], B[2 + tt][:, 448:480]).then_inc(zk_ready, 1)
                rope(r)
            for tt in range(TT):
                dve.wait_ge(zv_ready, tt + 1)
                dve.wait_ge(*((ck_sum, tt) if tt else (roped, 4)))
                V.tensor_tensor_reduce(out=rope_a[:, 0:P], in0=zv[:, tt, 0:P], in1=zv[:, tt, 0:P], scale=1.0, scalar=0.0,
                                       op0=ALU.mult, op1=ALU.add, accum_out=small[:, tt:tt + 1]).then_inc(ck_sum, 1)
            for tt in range(TT):
                dve.wait_ge(ck_root, tt + 1)
                link(V.reciprocal(small[:, 4 + tt:5 + tt], small[:, 2 + tt:3 + tt]))
                V.tensor_scalar(zv[:, tt, 0:P], zv[:, tt, 0:P], small[:, 4 + tt:5 + tt], None, ALU.mult).then_inc(ck_ready, 1)
            dve.wait_ge(ck_ready, 2)
            for r in range(4, len(ROPES)):
                rope(r)

            dve.wait_ge(gexp, 1)
            link(V.tensor_scalar(ssig[:, :], ssig[:, :], 1.0, None, ALU.add))
            link(V.reciprocal(ssig[:, :], ssig[:, :]))
            dve.wait_ge(zk_ready, 2)
            link(V.tensor_scalar(wis[:, :].rearrange("p (a n) -> p a n", a=TT), zk[:, :, 24:32], HEADS ** -0.5, None, ALU.mult))
            dve.wait_ge(job_out, len(JOBS))
            dve.wait_ge(w2_in, 48)
            for v, first in enumerate((KC, VC)):
                for half in range(2):
                    src = kT[:, first:first + 2, half * CMP_STEP:half * CMP_STEP + NCMP * CMP_STEP].rearrange(
                        "p g (n l) -> p g n l", l=CMP_STEP)
                    dst = blk[:, v, half * CMP_STEP:(half + 1) * CMP_STEP, :].rearrange("p l (g n) -> p g n l", g=2)
                    pos = posT[:, half * CMP_STEP:(half + 1) * CMP_STEP].unsqueeze(1).unsqueeze(1).to_broadcast(
                        [DH, 2, NCMP, CMP_STEP])
                    last = V.tensor_tensor(dst, src, pos, ALU.add)
            last.then_inc(blk_ready, 1)

            for q in range(8):
                tt, hp = divmod(q, 4)
                ns = (tt + 1) * P
                sc = score[:, tt, 0:ns]
                for i in range(2):
                    h = 2 * hp + i
                    r = relu[q % 2][:, i * ns:(i + 1) * ns]
                    wh = wis[:, tt * HEADS + h:tt * HEADS + h + 1]
                    if i == 0:
                        dve.wait_ge(relu_done, q + 1)
                    if h == 0:
                        link(V.tensor_scalar(sc, r, wh, None, ALU.mult))
                    elif i == 0:
                        link(V.scalar_tensor_tensor(sc, r, wh, sc, ALU.mult, ALU.add))
                    else:
                        V.scalar_tensor_tensor(sc, r, wh, sc, ALU.mult, ALU.add).then_inc(relu_used, 1)
                        dve.wait_ge(relu_used, q + 1)
                if hp == 3:
                    link(V.tensor_tensor(sc, sc, table("cmask")[:, T - ns:T], ALU.add))

            dve.wait_ge(hid_done, 1)
            V.tensor_copy(hid[:, 0:30], B[4][0:DH, 0:30])
            link(V.tensor_copy(hid[:, 30:60], B[5][0:DH, 0:30]))
            x = hid[:, 0:60]
            link(V.tensor_tensor(hid[:, 60:120], x, x, ALU.mult))
            link(V.tensor_scalar(hid[:, 60:120], hid[:, 60:120], 0.044715, 1.0, ALU.mult, ALU.add))
            V.tensor_tensor(hid[:, 120:180], hid[:, 60:120], x, ALU.mult).then_inc(hid_in, 1)
            dve.wait_ge(tanh_done, 1)
            link(V.tensor_scalar(hid[:, 180:240], hid[:, 120:180], 1.0, 0.5, ALU.add, ALU.mult))
            link(V.tensor_tensor(hid[:, 300:360], hid[:, 180:240], x, ALU.mult))
            V.tensor_copy(hidrep.rearrange("p (g r n) -> p g r n", g=2, r=4),
                          hid[:, 330:360].rearrange("p (g n) -> p g n", g=2).unsqueeze(2).to_broadcast([DH, 2, 4, NCMP])).then_inc(hid_ready, 1)
            dve.wait_ge(cmpkv_done, 1)
            V.tensor_copy(kcmpT, B[7][0:DH, P:P + 2 * NCMP]).then_inc(cmpkv_ready, 1)
            rows = HEADS * NCMP
            V.tensor_tensor(vbd[0:rows, :].rearrange("p (h f) -> p h f", h=HEADS),
                            B[7][0:rows, T:T + DH].unsqueeze(1).to_broadcast([rows, HEADS, DH]),
                            table("bmask")[0:rows, :].unsqueeze(2).to_broadcast([rows, HEADS, DH]), ALU.mult).then_inc(cmpkv_ready, 1)
            for tt in range(TT):
                dve.wait_ge(cs_done, tt + 1)
                s = pc[:, tt, :].rearrange("p (h n) -> p h n", h=HEADS)
                add = table("cmp_add").rearrange("p (a n) -> p a n", a=TT)[:, tt, :].unsqueeze(1).to_broadcast([P, HEADS, NCMP])
                link(V.tensor_tensor(s, B[tt][:, 0:rows].rearrange("p (h n) -> p h n", h=HEADS), add, ALU.add))
                link(V.tensor_reduce(csum[:, 0:8], s, AX.X, ALU.max))
                V.tensor_tensor(s, s, csum[:, 0:8].unsqueeze(2).to_broadcast([P, HEADS, NCMP]), ALU.subtract).then_inc(cs_in, 1)
            for tt in range(TT):
                dve.wait_ge(cexp_done, tt + 1)
                s = pc[:, tt, :].rearrange("p (h n) -> p h n", h=HEADS)
                mul = table("cmp_mul").rearrange("p (a n) -> p a n", a=TT)[:, tt, :].unsqueeze(1).to_broadcast([P, HEADS, NCMP])
                link(V.tensor_tensor(s, s, mul, ALU.mult))
                link(V.tensor_reduce(csum[:, 0:8], s, AX.X, ALU.add))
                link(V.tensor_scalar(csum[:, 0:8], csum[:, 0:8], 1e-30, None, ALU.max))
                link(V.reciprocal(csum[:, 0:8], csum[:, 0:8]))
                V.tensor_tensor(s, s, csum[:, 0:8].unsqueeze(2).to_broadcast([P, HEADS, NCMP]), ALU.mult).then_inc(pc_ready, 1)
            gate3 = ssig[:, :].rearrange("p (a h b) -> p a h b", a=TT, b=3)
            for tt in range(TT):
                dve.wait_ge(oc_done, tt + 1)
                V.tensor_tensor(o_nsa[tt].rearrange("p (h f) -> p h f", h=HEADS), B[4 + tt][:, :].rearrange("p (h f) -> p h f", h=HEADS),
                                gate3[:, tt, :, 0].unsqueeze(2).to_broadcast([P, HEADS, DH]), ALU.mult).then_inc(oc_read, 1)
            dve.wait_ge(oc_read, 2)

            def finish(g):
                b, tt, _ = UNITS[4 * g]
                dve.wait_ge(o_unit, 4 * g + 4)
                r = recip[:, 0:HEADS]
                link(V.tensor_scalar(r, rowsum[:, g * HEADS:(g + 1) * HEADS], 1e-30, None, ALU.max))
                link(V.reciprocal(r, r))
                o = B[4 + g % 2][:, :].rearrange("p (h f) -> p h f", h=HEADS)
                if b == 2:
                    V.tensor_tensor(o_dsa[tt].rearrange("p (h f) -> p h f", h=HEADS), o,
                                    r.unsqueeze(2).to_broadcast([P, HEADS, DH]), ALU.mult).then_inc(o_read, 1)
                    dve.wait_ge(o_read, g + 1)
                else:
                    link(V.tensor_tensor(r, r, gate3[:, tt, :, BRANCHES[b][3]], ALU.mult))
                    V.tensor_tensor(otmp.rearrange("p (h f) -> p h f", h=HEADS), o,
                                    r.unsqueeze(2).to_broadcast([P, HEADS, DH]), ALU.mult).then_inc(o_read, 1)
                    dve.wait_ge(o_read, g + 1)
                    link(V.tensor_tensor(o_nsa[tt], o_nsa[tt], otmp, ALU.add))

            for u in range(len(UNITS)):
                b, tt, hp = UNITS[u]
                ns = (tt + 1) * P
                dve.wait_ge(s_done, u + 1)
                if u >= 2:
                    dve.wait_ge(pt_done, u - 1)
                if u == 0:
                    dve.wait_ge(pct_ready, 2)
                for i in range(2):
                    mask = work[:, tt, 0:ns] if b == 2 else table("cmask")[:, T - ns:T]
                    last = V.tensor_tensor_reduce(out=ssb[u % 2][:, i * ns:(i + 1) * ns], in0=B[u % 2][:, i * ns:(i + 1) * ns], in1=mask,
                                                  scale=DH ** -0.5, scalar=-3.0e38, op0=ALU.add, op1=ALU.max,
                                                  accum_out=rowmax[:, 2 * (u % 2) + i:2 * (u % 2) + i + 1])
                link(last)
                V.tensor_scalar(negmax[:, 2 * (u % 2):2 * (u % 2) + 2], rowmax[:, 2 * (u % 2):2 * (u % 2) + 2], -1.0, None,
                                ALU.mult).then_inc(s_masked, 1)
                if u < 16:
                    t2, rnd = divmod(u, 8)
                    n2 = (t2 + 1) * P
                    left = score[:, t2, 0:n2] if rnd == 0 else work[:, t2, 0:n2]
                    link(V.max(best8[:, :], left))
                    link(V.match_replace(work[:, t2, 0:n2], best8[:, :], left, TAKEN))
                    if rnd == TOPK_DSA // 8 - 1:
                        link(V.tensor_scalar(work[:, t2, 0:n2], work[:, t2, 0:n2], TAKEN / 2, NEG, ALU.is_gt, ALU.mult))
                        link(V.tensor_tensor(work[:, t2, 0:n2], work[:, t2, 0:n2], table("cmask")[:, T - n2:T], ALU.add))
                for m, k in UNIT_ADA[u]:
                    ada_step(m, k)
                if u >= 5 and (u - 5) % 4 == 0:
                    finish((u - 5) // 4)
            finish(GROUPS - 1)
            dve.wait_ge(o_read, GROUPS)
            V.tensor_copy(small[:, 8:9], small[:, 4:5]).then_inc(o_ready, 1)

            dve.wait_ge(ada_done, 12)
            link(V.tensor_tensor(mod[:, 2 * KT:6 * KT], B[7][:, 2 * KT:6 * KT], param("ada_b")[:, 2 * KT:6 * KT], ALU.add))
            link(V.tensor_scalar(scale2[:, :], mod[:, 4 * KT:5 * KT], 1.0, None, ALU.add))
            link(V.tensor_tensor(scale2[:, :], scale2[:, :], param("g2"), ALU.mult))
            for m in range(KT):
                dve.wait_ge(br_done, m + 1)
                dve.wait_ge(gates_ready, m // 2 + 1)
                if m == 0:
                    dve.wait_ge(fill_done, 16)
                link(V.tensor_tensor(hT[:, m, :], B[4 + m % 2][:, 0:T], gates[:, m, :], ALU.mult))
                link(V.tensor_tensor(gates[:, m, :], B[4 + m % 2][:, T:2 * T], gates[:, KT + m, :], ALU.mult))
                V.tensor_tensor(hT[:, m, :], hT[:, m, :], gates[:, m, :], ALU.add).then_inc(merged_ready, 1)
            for m in range(KT):
                dve.wait_ge(mo_done, m + 1)
                V.scalar_tensor_tensor(x3[:, m, :], B[m % 2][:, 0:T], mod[:, 2 * KT + m:2 * KT + m + 1], x3[:, m, :],
                                       ALU.mult, ALU.add).then_inc(x1_ready, 1)
            dve.wait_ge(root2_ready, 1)
            link(V.reciprocal(rstd[:, :], rstd[:, :]))
            for k in range(KT):
                V.scalar_tensor_tensor(h2[:, k, :], x3[:, k, :], scale2[:, k:k + 1], rstd[:, :], ALU.mult, ALU.mult).then_inc(h2_scaled, 1)

            def lo_part(s, slot, tile):
                dve.wait_ge(hi_ready, tile * 2 + 1)
                V.tensor_tensor(part_lo[slot], raw[s][:, 0:512], part_hi[slot].bitcast(F32), ALU.subtract).then_inc(lo_ready[0], 1)

            val = tk[:, 0:256].rearrange("p (s k) -> p s k", s=16)
            val4 = tk[:, 0:256].rearrange("p (h c k) -> p h c k", h=HEADS, c=2)
            idx = tk[:, 256:512].bitcast(U32)
            idx_s = idx.rearrange("p (s k) -> p s k", s=16)
            idxf = tk[:, 512:768].rearrange("p (h c k) -> p h c k", h=HEADS, c=2)
            cand = tk[:, 768:768 + HEADS * NCAND].rearrange("p (h c) -> p h c", h=HEADS)
            cwork = tk[:, 1168:1168 + NCAND]
            iwork = tk[:, 1218:1218 + KEYS]
            top = tk[:, 1346:1346 + P].rearrange("p (h k) -> p h k", h=HEADS)
            pos = tk[:, 1474:1474 + P].bitcast(U32)
            pos_h = pos.rearrange("p (h k) -> p h k", h=HEADS)
            eid = tk[:, 1602:1730]
            eid_i, part_i, part_j = (tk[:, 1346 + i * P:1346 + (i + 1) * P].bitcast(I32) for i in range(3))
            gsum = tk[:, 1730:1738]

            def sum_picked(tt, q):
                dve.wait_ge(picked, 4 * tt + q + 1)
                V.tensor_reduce(eid[:, q * 32:(q + 1) * 32], quarter(q).rearrange("p (k c) -> p k c", c=NCAND),
                                AX.X, ALU.add).then_inc(eid_ready, 1)
                dve.wait_ge(eid_ready, 4 * tt + q + 1)

            def split_number(tt):
                link(V.tensor_copy(eid_i, eid))
                V.tensor_scalar(part_i, eid_i, 7, None, ALU.logical_shift_right)
                link(V.tensor_scalar(part_j, eid_i, KEYS - 1, None, ALU.bitwise_and))
                V.tensor_copy(route[:, tt, 0, :], part_i)
                link(V.tensor_copy(route[:, tt, 1, :], part_j))

            for tt in range(TT):
                for s in range(16):
                    if s % 8 == 0:
                        dve.wait_ge(sub_ready, 4 * tt + s // 4 + 2)
                    src = sub[tt][:, s, :]
                    link(V.max(val[:, s, 0:8], src))
                    V.max_index(idx_s[:, s, 0:8], val[:, s, 0:8], src)
                    link(V.match_replace(iwork, val[:, s, 0:8], src, TAKEN))
                    link(V.max(val[:, s, 8:16], iwork))
                    link(V.max_index(idx_s[:, s, 8:16], val[:, s, 8:16], iwork))
                link(V.tensor_copy(tk[:, 512:768], idx))
                link(V.tensor_scalar(idxf[:, :, 0, :], idxf[:, :, 0, :], float(KEYS), None, ALU.mult))
                for dst, src in ((cand, val4), (cidx[tt], idxf)):
                    c0 = 0
                    for a, n in CAND_ROWS:
                        V.tensor_tensor(dst[:, :, c0:c0 + n], src[:, :, 0, a:a + 1].to_broadcast([P, HEADS, n]), src[:, :, 1, 0:n], ALU.add)
                        c0 += n
                    link(V.tensor_tensor(dst[:, :, c0:NCAND], src[:, :, 0, TOPK // 2:TOPK],
                                         src[:, :, 1, 0:1].to_broadcast([P, HEADS, TOPK // 2]), ALU.add))
                for h in range(HEADS):
                    src = cand[:, h, :]
                    link(V.max(top[:, h, 0:8], src))
                    V.max_index(pos_h[:, h, 0:8], top[:, h, 0:8], src)
                    link(V.match_replace(cwork, top[:, h, 0:8], src, TAKEN))
                    link(V.max(top[:, h, 8:16], cwork))
                    link(V.max_index(pos_h[:, h, 8:16], top[:, h, 8:16], cwork))
                w = route[:, tt, 2, :].rearrange("p (h k) -> p h k", h=HEADS)
                V.tensor_tensor(w, top, top[:, :, 0:1].to_broadcast([P, HEADS, TOPK]), ALU.subtract).then_inc(top_ready, 1)
                V.tensor_copy(posf[tt], pos).then_inc(pos_ready, 1)
                dve.wait_ge(pos_ready, tt + 1)
                for q in range(4):
                    if tt:
                        sum_picked(tt - 1, q)
                    V.tensor_tensor(quarter(q).rearrange("p (k c) -> p k c", c=NCAND),
                                    table("pos").unsqueeze(1).to_broadcast([P, 32, NCAND]),
                                    posf[tt][:, q * 32:(q + 1) * 32].unsqueeze(2).to_broadcast([P, 32, NCAND]),
                                    ALU.is_equal).then_inc(matched, 1)
                if tt:
                    split_number(tt - 1)
            for q in range(4):
                sum_picked(TT - 1, q)
            split_number(TT - 1)
            for tt in range(TT):
                w = route[:, tt, 2, :].rearrange("p (h k) -> p h k", h=HEADS)
                dve.wait_ge(gate_exp, tt + 1)
                link(V.tensor_reduce(gsum, w, AX.X, ALU.add))
                link(V.reciprocal(gsum, gsum))
                last = V.tensor_tensor(w, w, gsum.unsqueeze(2).to_broadcast([P, HEADS, TOPK]), ALU.mult)
                if tt < TT - 1:
                    link(last)
            last.then_inc(route_ready, 1)

            iT, jT, wT = (routeT[:, i * T:(i + 1) * T] for i in range(3))

            def one_hots(slot, first, half):
                V.tensor_tensor(ohj4[slot], table("iota").unsqueeze(1).to_broadcast([P, TOKS, P]),
                                jT[:, bass.ds(first, TOKS)].unsqueeze(2).to_broadcast([P, TOKS, P]), ALU.is_equal)
                for t in range(TOKS):
                    last = V.tensor_scalar(ohi[slot * TOKS + t], table("iota")[:, half * IH:(half + 1) * IH], iT[:, bass.ds(first + t, 1)],
                                           wT[:, bass.ds(first + t, 1)], ALU.is_equal, ALU.mult)
                last.then_inc(oh_ready, 1)

            def weigh(group, slot, first, half):
                dve.wait_ge(g_done, group + 1)
                g = gel[:, half * IH:(half + 1) * IH, bass.ds(first, TOKS)]
                V.tensor_tensor(g, g, B[6 + slot][:, 0:TOKS * IH].rearrange("p (t i) -> p i t", t=TOKS), ALU.mult).then_inc(weighed, 1)

            def body(turn, half, start=False):
                for s in range(SLOTS):
                    n = turn * SLOTS + s
                    s2 = (s + 2) % SLOTS
                    if not (start and s < 2):
                        dve.wait_ge(g_done, n + (half * IH - 1))
                    one_hots(s % 2, n * TOKS, half)
                    lo_part(s2, 2 * s2 if half else 2 * s2 % SLOTS, n + (half * IH + (IH - WHOLE + 2)))
                    if start and s == 1:
                        dve.wait_ge(gelu_done, (half + 1) * IH)
                    if not (start and s == 0):
                        weigh(n + (half * IH - 1), (s + 1) % 2, (n - 1) * TOKS, half)

            turns = IH // SLOTS
            assert T // TOKS == IH
            with dve.Fori(0, (IH - WHOLE) // SLOTS) as turn:
                for s in range(SLOTS):
                    lo_part(s, 2 * s % SLOTS, turn * SLOTS + s)
            for s in range(2):
                lo_part(s, 2 * s, IH - WHOLE + s)
            dve.wait_ge(rt_ready, TT)
            for half in range(2):
                body(0, half, start=True)
                with dve.Fori(1, turns) as turn:
                    body(turn, half)
                weigh((half + 1) * IH - 1, 1, T - TOKS, half)
            with dve.Fori(turns, 2 * turns - 1) as turn:
                for s in range(SLOTS):
                    s2 = (s + 2) % SLOTS
                    lo_part(s2, 2 * s2, turn * SLOTS + (KEYS - WHOLE + s + 2))
            for s in range(2):
                lo_part(s + 2, 2 * (s + 2), 2 * KEYS - WHOLE - 2 + s)
            dve.wait_ge(part_used, 4 * KEYS - 2 * WHOLE)
            for n in range(2, 4):
                V.tensor_copy(acc[n], B[n][:, :]).then_inc(acc_out, 1)
            for m in range(KT):
                dve.wait_ge(accT_done, m // 2 + 1)
                V.scalar_tensor_tensor(x3[:, m, :], B[4 + m // 2][:, (m % 2) * T:(m % 2 + 1) * T], mod[:, 5 * KT + m:5 * KT + m + 1],
                                       x3[:, m, :], ALU.mult, ALU.add).then_inc(x2_ready, 1)
            dve.wait_ge(root3_ready, 1)
            link(V.reciprocal(rstd[:, :], rstd[:, :]))
            for m in range(KT):
                V.scalar_tensor_tensor(y[:, m, :], x3[:, m, :], param("gf")[:, m:m + 1], rstd[:, :], ALU.mult, ALU.mult).then_inc(y_ready, 1)


def constants():
    tab = np.zeros((P, TAB_W), np.float32)

    def put(name, a):
        tab[:a.shape[0], TAB[name][0]:TAB[name][0] + a.shape[1]] = a

    t = np.arange(T)
    p = np.arange(P)
    put("ident", np.eye(P))
    put("cmask", np.concatenate([np.zeros((P, P)), np.where(p[None, :] <= p[:, None], 0.0, NEG)], 1))
    put("iota", np.tile(p.astype(np.float32), (P, 1)))
    inv = np.float32(10000.0) ** (-np.arange(HALF, dtype=np.float32) / np.float32(HALF))
    ang = t.astype(np.float32)[:, None] * inv.astype(np.float32)[None, :]
    cos, sin = np.cos(ang), np.sin(ang)
    put("cos", cos.reshape(TT, P, HALF).transpose(1, 0, 2).reshape(P, -1))
    put("sin", np.stack([-sin, sin], 1).reshape(TT, P, 2 * HALF).transpose(1, 0, 2).reshape(P, -1))
    ok = (np.arange(NCMP) * CMP_STEP + CMP_LEN - 1)[None, :] <= t[:, None]
    put("cmp_add", np.where(ok, 0.0, NEG).reshape(TT, P, NCMP).transpose(1, 0, 2).reshape(P, -1))
    put("cmp_mul", ok.astype(np.float32).reshape(TT, P, NCMP).transpose(1, 0, 2).reshape(P, -1))
    put("bmask", (np.arange(HEADS * NCMP)[:, None] // NCMP == np.arange(HEADS)[None, :]).astype(np.float32))
    put("pos", np.tile(np.arange(NCAND, dtype=np.float32), (P, 1)))
    return tab


def kernel(**inputs):
    import concourse.bacc as bacc
    from concourse.bass_utils import run_bass_kernel_spmd

    a = {k: np.asarray(v) for k, v in inputs.items()}

    def feature_tiles(v):
        return v.reshape(-1, P).T

    w_in = a["w_in"][0]
    par = np.concatenate([feature_tiles(a["c"][0]), feature_tiles(a["ada_b"][0]), feature_tiles(a["norm1_g"][0]),
                          feature_tiles(a["norm2_g"][0]), feature_tiles(a["final_g"]), a["kv_norm_g"][0][:, None]], 1)
    arrays = {
        "par": par,
        "tab": constants(),
        "x": a["x"][0].T,
        "ada_w": a["ada_w"][0],
        "w_in": np.concatenate([w_in[:, START[n]:START[n] + SIZE[n]] for c in CHUNKS for n in c], 1),
        "w_gate": w_in[:, START["g_m"]:],
        "w_br": np.stack([a["w_br_nsa"][0], a["w_br_dsa"][0]]),
        "w_out": a["w_out"][0],
        "peer_wq": a["peer_wq"][0],
        "w_ukv": np.concatenate([a["w_uk"][0], a["w_uv"][0]], 1),
        "cmp_w2": np.concatenate([a["cmp_w2_k"][0], a["cmp_w2_v"][0]], 1),
        "cmp_pos": a["cmp_pos"][0].T,
        "cmp_w1_k": a["cmp_w1_k"][0].transpose(1, 0, 2),
        "cmp_w1_v": a["cmp_w1_v"][0].transpose(1, 0, 2),
        "subkeys": a["peer_subkeys"][0].transpose(1, 3, 0, 2).reshape(P, HEADS * KEYS),
        "uT": a["peer_u"][0].reshape(KEYS, KEYS, KT, P).transpose(0, 3, 2, 1),
        "v": a["peer_v"][0].reshape(KEYS, KEYS, D),
    }
    nc = bacc.Bacc("TRN2", target_bir_lowering=False, num_devices=1)
    feeds, aps = {}, {}
    for name, v in arrays.items():
        v = np.ascontiguousarray(v)
        feeds[f"in_{name}"] = v
        aps[name] = nc.dram_tensor(f"in_{name}", v.shape, mybir.dt.from_np(v.dtype), kind="ExternalInput").ap()
    out = nc.dram_tensor("yT", (D, T), F32, kind="ExternalOutput").ap()
    build(nc, aps, out)
    r = run_bass_kernel_spmd(nc, [feeds], core_ids=[0])
    return np.ascontiguousarray(r.results[0]["yT"].T).reshape(1, T, D)
```

```python
from contextlib import ExitStack

import concourse.bass as bass
import numpy as np
from concourse import mybir

F32 = mybir.dt.float32
F32R = mybir.dt.float32r
I32 = mybir.dt.int32
U32 = mybir.dt.uint32
ALU = mybir.AluOpType
ACT = mybir.ActivationFunctionType
AX = mybir.AxisListType

P = 128
D = 1024
KT = D // P
T = 256
TT = T // P
DH = 64
HALF = DH // 2
HEADS = 8
EPS = 1e-6
NEG = -1e30
TAKEN = -3e38
CMP_LEN, CMP_STEP = 32, 16
NCMP = T // CMP_STEP - 1
TOPK_DSA = min(256, T // 4)
KEYS = 128
TOPK = 16

SPLITS = (512, 128, 128, 128, 128, 128, 128, 24, 512, 128, 512, 64, 8, 2048)
NAMES = ("q_n", "kc", "vc", "ks", "vs", "kw", "vw", "g_n", "q_d", "ckv", "qi", "ki", "wi", "g_m")
CHUNKS = (("qi",), ("kc", "ks", "kw", "ki", "g_n", "wi"), ("ckv", "vc", "vs", "vw"), ("q_d",), ("q_n",))
START = dict(zip(NAMES, np.cumsum((0,) + SPLITS[:-1]).tolist()))
SIZE = dict(zip(NAMES, SPLITS))
CHUNK_COLS = [sum(SIZE[n] for n in c) for c in CHUNKS]
CHUNK_AT = [sum(CHUNK_COLS[:i]) for i in range(len(CHUNKS))]

CAND = [(a, b) for a in range(TOPK) for b in range(TOPK) if (a + 1) * (b + 1) <= TOPK]
NCAND = len(CAND)
CAND_ROWS = [(a, TOPK // (a + 1)) for a in range(TOPK // 2)]

TAB = {}
_at = 0
for _n, _w in (("ident", P), ("cmask", T), ("iota", P), ("cos", TT * HALF), ("sin", TT * 2 * HALF),
               ("cmp_add", TT * NCMP), ("cmp_mul", TT * NCMP), ("bmask", HEADS), ("pos", NCAND)):
    TAB[_n] = (_at, _at + _w)
    _at += _w
TAB_W = _at

PAR = {}
_at = 0
for _n, _w in (("c", KT), ("ada_b", 6 * KT), ("g1", KT), ("g2", KT), ("gf", KT), ("kvg", 1)):
    PAR[_n] = (_at, _at + _w)
    _at += _w
PAR_W = _at

LOADS = [("ada", m) for m in range(4)] + [("win", m) for m in range(len(CHUNKS))]
LOADS += [("gate", 0), ("ada", 4), ("gate", 1), ("ada", 5), ("gate", 2), ("ada", 6), ("ada", 7), ("gate", 3)]
LOADS += [("ada", m) for m in range(8, 12)]
LOADS += [("br", 0), ("br", 1), ("out", 0), ("out", 1), ("wq", 0), ("wq", 1)]
CHUNK_NO = {c: n for n, c in enumerate(LOADS)}
WSLOTS = 3
WCOLS = KT * 512

QI, QD, QN = 0, 8, 16
KC, KS, KW, KI, VC, KD = 0, 2, 4, 6, 7, 9
ROPES = [(0, 0), (0, 1), (1, 0), (1, 1), (3, 0), (3, 1), ("kd", 0), ("kd", 1), (4, 0), (4, 1)]
ROPE_HEADS = {0: 8, 1: 7, 3: 8, 4: 8, "kd": 1}


def transpose_jobs():
    jobs = []

    def heads(r):
        c, tt = ROPES[r]
        dst, first = {0: ("q", QI), 3: ("q", QD), 4: ("q", QN), 1: ("k", KC), "kd": ("k", KD)}[c]
        n = ROPE_HEADS[c]
        for h in range(0, n, 4):
            jobs.append(("rope", r, h, min(4, n - h), dst, first + h, tt))

    for r in (0, 1, 2, 3):
        heads(r)
    for tt in range(TT):
        jobs.append(("ckv", tt))
    for tt in range(TT):
        jobs.append(("kdvd", tt))
    for r in (4, 5, 6, 7, 8, 9):
        heads(r)
    return jobs


JOBS = transpose_jobs()
BRANCHES = (("slc", QN, KS, 1), ("win", QN, KW, 2), ("dsa", QD, KD, None))
UNITS = [(b, tt, hp) for b in range(3) for tt in range(TT) for hp in range(HEADS // 2)]
GROUPS = len(UNITS) // 4
GATE_UNITS = (0, 1, 3, 4, 5, 6, 7, 8, 11, 12, 13, 14)
UNIT_GATE = [4 + GATE_UNITS.index(u) if u in GATE_UNITS else None for u in range(len(UNITS))]
UNIT_ADA = [[(4 + u // 3, k) for k in ((0, 1, 2), (3, 4, 5), (6, 7))[u % 3]] for u in range(len(UNITS))]

TOKS = 4
SLOTS = 4
IH = KEYS // 2
WHOLE = 20
RT_TURN = 9


def build(nc, A, out):
    with ExitStack() as ctx:
        def sb(name, cols, parts=P, dt=F32):
            return ctx.enter_context(nc.sbuf_tensor(name, [parts, cols], dt))

        def sem(name):
            return ctx.enter_context(nc.semaphore(name))

        arena = sb("arena", KEYS * T)
        ring = sb("ring", SLOTS * D)
        tile_hi = sb("tile_hi", SLOTS * 512, dt=F32R)
        tile_lo = sb("tile_lo", SLOTS * 512, dt=F32R)
        h2_hi = sb("h2_hi", KT * T, dt=F32R)
        h2_lo = sb("h2_lo", KT * T, dt=F32R)
        a_hi = sb("a_hi", 2 * T, dt=F32R)
        a_lo = sb("a_lo", 2 * T, dt=F32R)
        xT = sb("xT", KT * T)
        ohj_r = sb("ohj_r", 2 * TOKS * P, dt=F32R)
        ohi_r = sb("ohi_r", 2 * TOKS * 2 * IH, dt=F32R)
        mask_i = sb("mask_i", TOKS * IH)
        w_parts = sb("w_parts", 2 * T)
        tab = sb("tab", TAB_W)
        par = sb("par", PAR_W)
        mod = sb("mod", 6 * KT)
        scale1 = sb("scale1", KT)
        scale2 = sb("scale2", KT)
        silu = sb("silu", 3 * KT)
        ones = sb("ones", P)
        eps = sb("eps", 1)
        rstd = sb("rstd", T)
        small = sb("small", 16)
        rowmax = sb("rowmax", 4)
        negmax = sb("negmax", 4)
        recip = sb("recip", HEADS)
        best8 = sb("best8", 8)
        routeT = sb("routeT", 3 * T)

        def table(name):
            return tab[:, TAB[name][0]:TAB[name][1]]

        def param(name):
            return par[:, PAR[name][0]:PAR[name][1]]

        ident = table("ident")
        x3 = xT[:, :].rearrange("p (k t) -> p k t", k=KT)

        def tiles(t, k):
            return t.rearrange("p (k t) -> p k t", k=k)

        wslot = [arena[:, s * WCOLS:(s + 1) * WCOLS] for s in range(WSLOTS)]
        at = WSLOTS * WCOLS
        hT = tiles(arena[:, at:at + KT * T], KT)
        at += KT * T
        q_at = at
        qT = tiles(arena[0:DH, at:at + 24 * T], 24)
        oT = arena[:, at:at + 8 * T].rearrange("p (b k t) -> p b k t", b=2, k=4)
        q2T = tiles(arena[:, at:at + KT * T], KT)
        sq1 = tiles(arena[:, at + 8 * T:at + 16 * T], KT)
        ada_sum = [arena[:, at + 16 * T + i * 512:at + 16 * T + (i + 1) * 512] for i in range(4)]
        skT = arena[:, at + 8 * T:at + 12 * T]
        at += 24 * T
        kT = tiles(arena[0:DH, at:at + 10 * T], 10)
        at += 10 * T
        blk = arena[:, at:at + CMP_LEN * 2 * NCMP].rearrange("p (v l n) -> p v l n", v=2, l=CMP_LEN // 2)
        gates = tiles(arena[:, at:at + 16 * T], 16)
        at += 16 * T
        ckvT = arena[:, at:at + T]
        kdv = arena[:, at + T:at + 2 * T].rearrange("p (a n) -> p a n", a=TT)
        at += 2 * T
        scr = arena[:, at:]
        zv = scr[:, 0:1024].rearrange("p (a n) -> p a n", a=TT)
        zk = scr[:, 1024:1088].rearrange("p (a n) -> p a n", a=TT)
        rope_a = scr[:, 1088:1600]
        rope_b = scr[:, 1600:2112]
        rq = [scr[:, 2112 + i * 512:2112 + (i + 1) * 512] for i in range(2)]
        hid = scr[0:DH, 3136:3496]
        hidrep = scr[0:DH, 3496:3616]
        kcmpT = scr[0:DH, 3616:3646]
        csum = scr[:, 3646:3654]
        score = scr[:, 3660:4172].rearrange("p (a n) -> p a n", a=TT)
        work = scr[:, 4172:4684].rearrange("p (a n) -> p a n", a=TT)
        wukv = scr[:, 4684:4812]
        w2kv = scr[0:DH, 4812:4940]
        posT = scr[0:DH, 4940:4972]
        ssig = scr[:, 4972:4972 + TT * 24]
        wis = scr[:, 5020:5020 + TT * HEADS]
        rowsum = scr[:, 5036:5036 + GROUPS * HEADS]
        assert at + 5084 <= KEYS * T
        relu = [rope_a, rope_b]
        vbd = rope_a
        pc = rope_b[:, 0:240].rearrange("p (a n) -> p a n", a=TT)
        pcT = [rope_b[:, 256 + i * 128:256 + (i + 1) * 128] for i in range(2)]
        otmp = rq[0]

        at = q_at + 12 * T
        eqbuf = arena[:, at:at + HEADS * TOPK * NCAND]
        at += HEADS * TOPK * NCAND
        assert q_at + 12 * T >= IH * T
        sub = [arena[:, at + i * 2048:at + (i + 1) * 2048].rearrange("p (s n) -> p s n", n=KEYS) for i in range(TT)]
        at += TT * 2048
        sq2 = tiles(arena[:, at:at + KT * T], KT)
        tk = arena[:, at:at + 3754 + NCAND]
        assert at + 3754 + NCAND <= KEYS * T
        route = tk[:, 2730:2730 + 6 * P].rearrange("p (a i c) -> p a i c", a=TT, i=3)

        cidx = [tk[:, 1738 + i * 400:1738 + (i + 1) * 400].rearrange("p (h c) -> p h c", h=HEADS) for i in range(TT)]
        posf = [tk[:, 2540:2668], tk[:, 3498:3626]]

        def quarter(q):
            return eqbuf[:, q * 32 * NCAND:(q + 1) * 32 * NCAND]

        h2 = hT
        gel = arena[:, :].rearrange("p (i t) -> p i t", t=T)
        sq3 = sq1
        y = tiles(arena[:, 0:KT * T], KT)
        acc = [arena[:, (24 + 2 * n) * T:(26 + 2 * n) * T] for n in range(4)]
        raw = [ring[:, s * D:(s + 1) * D] for s in range(SLOTS)]
        part_hi = [t[:, s * 512:(s + 1) * 512] for t in (tile_hi, h2_hi) for s in range(SLOTS)]
        part_lo = [t[:, s * 512:(s + 1) * 512] for t in (tile_lo, h2_lo) for s in range(SLOTS)]
        h2h, h2l = tiles(h2_hi[:, :], KT), tiles(h2_lo[:, :], KT)
        ohj = [ohj_r[:, s * P:(s + 1) * P] for s in range(2 * TOKS)]
        ohj4 = [ohj_r[:, s * 512:(s + 1) * 512].rearrange("p (t j) -> p t j", t=TOKS) for s in range(2)]
        ohi = [ohi_r[:, s * 2 * IH:(s + 1) * 2 * IH] for s in range(2 * TOKS)]
        ohi4 = [ohi_r[:, s * 512:(s + 1) * 512].rearrange("p (t c i) -> p t c i", t=TOKS, c=2) for s in range(2)]
        mask4 = mask_i[:, :].rearrange("p (t i) -> p t i", t=TOKS)
        g_low = [a.rearrange("p (t i) -> p t i", t=TOKS) for a in (rstd[:, :], table("cmask"))]
        w2 = w_parts[:, :].rearrange("p (t c) -> p t c", c=2)

        w1k = ring[:, 0:1024].rearrange("p (l e) -> p l e", l=CMP_LEN // 2)
        w1v = ring[:, 1024:2048].rearrange("p (l e) -> p l e", l=CMP_LEN // 2)
        ada_sum += [ring[:, 2048 + i * 512:2048 + (i + 1) * 512] for i in range(2)]
        ssb = [ring[:, i * 512:(i + 1) * 512] for i in range(2)]
        pT = [ring[:, 1024 + i * 512:1024 + (i + 1) * 512] for i in range(2)]
        o_nsa = [ring[:, 3072 + i * 512:3072 + (i + 1) * 512] for i in range(2)]
        o_dsa = [rope_a, rope_b]

        B = [ctx.enter_context(nc.psum_tensor(f"bank{i}", [P, 512], F32)) for i in range(8)]

        par_in, x_in, tab_in, sk_in = sem("par_in"), sem("x_in"), sem("tab_in"), sem("sk_in")
        w1_in, w2_in, out_done = sem("w1_in"), sem("w2_in"), sem("out_done")
        w_in = [sem(f"w_in{s}") for s in range(WSLOTS)]
        tile_in = [sem(f"tile_in{s}") for s in range(SLOTS)]
        const_set, dve_step, act_step = sem("const_set"), sem("dve_step"), sem("act_step")
        cexp, silu_ready, sq_ready, ssq_ready = sem("cexp"), sem("silu_ready"), sem("sq_ready"), sem("ssq_ready")
        root_ready, h_ready, ada_done = sem("root_ready"), sem("h_ready"), sem("ada_done")
        ada_first, ada_summed, rstd_ready, x_scaled = sem("ada_first"), sem("ada_summed"), sem("rstd_ready"), sem("x_scaled")
        z_done, z_read, zv_ready, zk_ready = sem("z_done"), sem("z_read"), sem("zv_ready"), sem("zk_ready")
        roped, job_done, job_out = sem("roped"), sem("job_done"), sem("job_out")
        ck_sum, ck_root, ck_ready = sem("ck_sum"), sem("ck_root"), sem("ck_ready")
        gexp = sem("gexp")
        logit_done, relu_done, relu_used = sem("logit_done"), sem("relu_done"), sem("relu_used")
        blk_ready, hid_done, hid_in, tanh_done = sem("blk_ready"), sem("hid_done"), sem("hid_in"), sem("tanh_done")
        hid_ready, cmpkv_done, cmpkv_ready = sem("hid_ready"), sem("cmpkv_done"), sem("cmpkv_ready")
        cs_done, cs_in, cexp_done, pc_ready = sem("cs_done"), sem("cs_in"), sem("cexp_done"), sem("pc_ready")
        pct_done, pct_ready, oc_done, oc_read = sem("pct_done"), sem("pct_ready"), sem("oc_done"), sem("oc_read")
        s_done, s_masked, p_ready, pt_done = sem("s_done"), sem("s_masked"), sem("p_ready"), sem("pt_done")
        pt_ready, o_unit, o_read = sem("pt_ready"), sem("o_unit"), sem("o_read")
        fill_done, fill_out = sem("fill_done"), sem("fill_out")
        o_ready, ot_done, ot_ready = sem("o_ready"), sem("ot_done"), sem("ot_ready")
        gates_ready, br_done, merged_ready = sem("gates_ready"), sem("br_done"), sem("merged_ready")
        mo_done, x1_ready, sq2_ready = sem("mo_done"), sem("x1_ready"), sem("sq2_ready")
        ssq2_ready, root2_ready, h2_ready = sem("ssq2_ready"), sem("root2_ready"), sem("h2_ready")
        h2_scaled = sem("h2_scaled")
        q2_done, q2_ready, sub_done, sub_ready = sem("q2_done"), sem("q2_ready"), sem("sub_done"), sem("sub_ready")
        pos_ready, matched, picked, eid_ready = sem("pos_ready"), sem("matched"), sem("picked"), sem("eid_ready")
        top_ready, gate_exp, route_ready = sem("top_ready"), sem("gate_exp"), sem("route_ready")
        rt_done, rt_ready = sem("rt_done"), sem("rt_ready")
        oh_ready, g_done, weighed = sem("oh_ready"), sem("g_done"), sem("weighed")
        w_split, mask_ready, g_summed = sem("w_split"), sem("mask_ready"), sem("g_summed")
        g_copied = sem("g_copied")
        h2_hi_ready, h2_lo_ready, tile_used = sem("h2_hi_ready"), sem("h2_lo_ready"), sem("tile_used")
        hi_ready, part_used = sem("hi_ready"), sem("part_used")
        lo_ready = [sem(f"lo_ready{half}") for half in range(2)]
        gelu_done, ah_ready, al_ready = sem("gelu_done"), sem("ah_ready"), sem("al_ready")
        acc_out, accT_done, accT_out = sem("acc_out"), sem("accT_done"), sem("accT_out")
        x2_ready, sq3_ready, ssq3_ready, root3_ready = sem("x2_ready"), sem("sq3_ready"), sem("ssq3_ready"), sem("root3_ready")
        y_ready = sem("y_ready")

        def chunk(eng, kind, m):
            n = CHUNK_NO[kind, m]
            eng.wait_ge(w_in[n % WSLOTS], 16 * (n // WSLOTS + 1))
            return wslot[n % WSLOTS]

        def ada_buffer(m, parity):
            if m < 4:
                return ada_sum[2 * (m % 2) + parity]
            return ada_sum[5] if parity else (ada_sum[4], rq[1])[m % 2]

        block = ctx.enter_context(nc.Block())

        @block.sync
        def _(sp):
            sp.dma_start(par[:, :], A["par"]).then_inc(par_in, 16)
            sp.dma_start(x3, A["x"].rearrange("(k p) t -> p k t", p=P)).then_inc(x_in, 16)
            split = {"ada": A["ada_w"], "win": A["w_in"], "gate": A["w_gate"], "out": A["w_out"], "wq": A["peer_wq"]}
            for n, (kind, m) in enumerate(LOADS):
                if n >= WSLOTS:
                    old, i = LOADS[n - WSLOTS]
                    sp.wait_ge(*{"ada": (ada_summed, i + 1), "win": (z_done, 2 * i + 2), "gate": (fill_done, 4 * i + 4),
                                 "br": (br_done, KT), "out": (mo_done, 4 * i + 4)}[old])
                slot = wslot[n % WSLOTS]
                if kind == "br":
                    src = A["w_br"][m].rearrange("(k p) n -> p k n", p=P)
                    dst = slot.rearrange("p (k n) -> p k n", k=4)
                else:
                    first, cols = (CHUNK_AT[m], CHUNK_COLS[m]) if kind == "win" else (512 * m, 512)
                    src = split[kind].rearrange("(k p) n -> p k n", p=P)[:, :, first:first + cols]
                    dst = slot.rearrange("p (k n) -> p k n", k=KT)[:, :, 0:cols]
                sp.dma_start(dst, src).then_inc(w_in[n % WSLOTS], 16)
                if (kind, m) == ("win", 1):
                    sp.dma_start(w1k, A["cmp_w1_k"]).then_inc(w1_in, 16)
                    sp.dma_start(w1v, A["cmp_w1_v"]).then_inc(w1_in, 16)
            sp.wait_ge(ot_ready, 4)
            sp.dma_start(skT, A["subkeys"]).then_inc(sk_in, 16)
            for s in range(SLOTS):
                sp.dma_start(raw[s].rearrange("p (k j) -> p k j", k=KT), A["uT"][s]).then_inc(tile_in[s], 16)
            with sp.Fori(1, WHOLE // SLOTS + 1) as turn:
                for s in range(SLOTS):
                    sp.wait_ge(tile_used, turn * SLOTS + (s + 1 - SLOTS))
                    sp.dma_start(raw[s].rearrange("p (k j) -> p k j", k=KT),
                                 A["uT"][bass.ds(turn * SLOTS + s, 1)].rearrange("a p k j -> p (a k) j")).then_inc(tile_in[s], 16)
            with sp.Fori(WHOLE // SLOTS + 1, KEYS // SLOTS) as turn:
                for s in range(SLOTS):
                    for half in range(2):
                        sp.wait_ge(lo_ready[half], turn * SLOTS + (s + 1 - SLOTS - WHOLE))
                    sp.dma_start(raw[s].rearrange("p (k j) -> p k j", k=KT),
                                 A["uT"][bass.ds(turn * SLOTS + s, 1)].rearrange("a p k j -> p (a k) j")).then_inc(tile_in[s], 16)
            with sp.Fori(0, KEYS // SLOTS) as turn:
                for s in range(SLOTS):
                    for half in range(2):
                        sp.wait_ge(lo_ready[half], turn * SLOTS + (KEYS + s + 1 - SLOTS - WHOLE))
                    sp.dma_start(raw[s], A["v"][bass.ds(turn * SLOTS + s, 1)].rearrange("a p d -> p (a d)")).then_inc(tile_in[s], 16)
            for m in range(KT):
                sp.wait_ge(y_ready, m + 1)
                sp.dma_start(out[m * P:(m + 1) * P, :], y[:, m, :]).then_inc(out_done, 16)
            sp.wait_ge(out_done, 16 * KT)

        @block.tensor
        def _(pe):
            def ada(m):
                pe.wait_ge(ada_summed, m + 1)
                for c in range(4):
                    last = nc.tensor.matmul(B[7][:, 4 * m + c:4 * m + c + 1], ada_buffer(m, 0)[:, c * P:(c + 1) * P],
                                            ones[:, 0:1], start=True, stop=True)
                last.then_inc(ada_done, 1)

            def square_sum(bank, src, ready, done):
                for k in range(KT):
                    pe.wait_ge(ready, k + 1)
                    last = nc.tensor.matmul(B[bank][:, 0:T], ones[:, :], src[:, k, :], start=(k == 0), stop=(k == KT - 1))
                last.then_inc(done, 1)

            pe.wait_ge(const_set, 1)
            square_sum(0, sq1, sq_ready, ssq_ready)
            for m in range(4):
                ada(m)

            def project(c, pos):
                w = chunk(pe, "win", c).rearrange("p (k n) -> p k n", k=KT)
                for tt in range(TT):
                    n = 2 * pos + tt
                    if c == 0 and tt == 0:
                        pe.wait_ge(h_ready, KT)
                    if pos in (2, 3):
                        pe.wait_ge(z_read, n - 3)
                    if pos == 4:
                        pe.wait_ge(zv_ready, tt + 1)
                    for k in range(KT):
                        last = nc.tensor.matmul(B[n % 4][:, 0:CHUNK_COLS[c]], hT[:, k, tt * P:(tt + 1) * P],
                                                w[:, k, 0:CHUNK_COLS[c]], start=(k == 0), stop=(k == KT - 1))
                    last.then_inc(z_done, 1)

            def job(n):
                kind, *what = JOBS[n]
                bank = B[4 + n % 3]
                if n >= 3:
                    pe.wait_ge(job_out, n - 2)
                if kind == "rope":
                    r, h, count, _, _, _ = what
                    pe.wait_ge(roped, r + 1)
                    for i in range(count):
                        last = nc.tensor.transpose(bank[0:DH, i * P:(i + 1) * P],
                                                   rq[r % 2][:, (h + i) * DH:(h + i + 1) * DH], ident)
                elif kind == "ckv":
                    tt, = what
                    pe.wait_ge(ck_ready, tt + 1)
                    nc.tensor.transpose(bank[:, 0:P], zv[:, tt, 0:P], ident)
                    for g in range(2):
                        last = nc.tensor.transpose(bank[0:DH, (1 + g) * P:(2 + g) * P],
                                                   zv[:, tt, P + g * DH:P + (g + 1) * DH], ident)
                else:
                    tt, = what
                    pe.wait_ge(job_out, n - 1)
                    last = nc.tensor.matmul(bank[:, 0:2 * DH], ckvT[:, tt * P:(tt + 1) * P], wukv, start=True, stop=True)
                last.then_inc(job_done, 1)

            pe.wait_ge(tab_in, 16)
            project(0, 0)
            project(1, 1)
            for n in range(0, 4):
                job(n)
            project(2, 2)
            for n in range(4, 8):
                job(n)
            project(3, 3)
            job(8)
            job(9)
            project(4, 4)
            pe.wait_ge(w2_in, 48)
            first_qn = min(j for j, w in enumerate(JOBS) if w[0] == "rope" and w[1] == 8)
            for n in range(10, first_qn):
                job(n)
            pe.wait_ge(w1_in, 32)
            pe.wait_ge(blk_ready, 1)
            for v, w1 in enumerate((w1k, w1v)):
                for l in range(CMP_LEN // 2):
                    last = nc.tensor.matmul(B[7][0:DH, 320 + 64 * v:320 + 64 * v + 2 * NCMP], w1[:, l, :], blk[:, v, l, :],
                                            start=(l == 0), stop=(l == CMP_LEN // 2 - 1))
            last.then_inc(hid_done, 1)
            for n in range(first_qn, len(JOBS)):
                job(n)

            for q in range(8):
                tt, hp = divmod(q, 4)
                ns = (tt + 1) * P
                if q == 0:
                    pe.wait_ge(job_out, len(JOBS))
                    pe.wait_ge(z_read, 10 - 2)
                if q >= 4:
                    pe.wait_ge(relu_done, q - 3)
                for i in range(2):
                    last = nc.tensor.matmul(B[q % 4][:, i * ns:(i + 1) * ns], qT[:, QI + 2 * hp + i, tt * P:(tt + 1) * P],
                                            kT[:, KI, 0:ns], start=True, stop=True)
                last.then_inc(logit_done, 1)

            def gate(m):
                w = chunk(pe, "gate", m // 4).rearrange("p (k n) -> p k n", k=KT)
                if m:
                    pe.wait_ge(fill_out, m)
                for k in range(KT):
                    last = nc.tensor.matmul(B[6][:, 0:T], w[:, k, (m % 4) * P:(m % 4 + 1) * P], hT[:, k, :],
                                            start=(k == 0), stop=(k == KT - 1))
                last.then_inc(fill_done, 1)

            gate(0)
            pe.wait_ge(hid_ready, 1)
            nc.tensor.matmul(B[7][0:DH, P:P + 2 * NCMP], w2kv[:, 0:DH], hid[:, 300:330], start=True, stop=True)
            nc.tensor.matmul(B[7][0:HEADS * NCMP, T:T + DH], hidrep, w2kv[:, DH:2 * DH], start=True, stop=True).then_inc(cmpkv_done, 1)
            gate(1)
            pe.wait_ge(cmpkv_ready, 2)
            pe.wait_ge(relu_done, 8)
            for tt in range(TT):
                for h in range(HEADS):
                    last = nc.tensor.matmul(B[tt][:, h * NCMP:(h + 1) * NCMP], qT[:, QN + h, tt * P:(tt + 1) * P],
                                            kcmpT[:, (h // 4) * NCMP:(h // 4 + 1) * NCMP], start=True, stop=True)
                last.then_inc(cs_done, 1)
            gate(2)
            for tt in range(TT):
                pe.wait_ge(pc_ready, tt + 1)
                nc.tensor.transpose(B[2 + tt][0:HEADS * NCMP, 0:P], pc[:, tt, :], ident).then_inc(pct_done, 1)
            gate(3)
            for tt in range(TT):
                pe.wait_ge(pct_ready, tt + 1)
                nc.tensor.matmul(B[4 + tt][:, :], pcT[tt][0:HEADS * NCMP, :], vbd[0:HEADS * NCMP, :],
                                 start=True, stop=True).then_inc(oc_done, 1)

            for u in range(len(UNITS) + 2):
                if u < len(UNITS):
                    b, tt, hp = UNITS[u]
                    ns = (tt + 1) * P
                    _, q0, k0, _ = BRANCHES[b]
                    if u >= 2:
                        pe.wait_ge(s_masked, u - 1)
                    for i in range(2):
                        h = 2 * hp + i
                        kh = k0 if b == 2 else k0 + h // 4
                        last = nc.tensor.matmul(B[u % 2][:, i * ns:(i + 1) * ns], qT[:, q0 + h, tt * P:(tt + 1) * P],
                                                kT[:, kh, 0:ns], start=True, stop=True)
                    last.then_inc(s_done, 1)
                    if u >= 3 and u % 3 == 1:
                        ada(3 + u // 3)
                    if UNIT_GATE[u] is not None:
                        gate(UNIT_GATE[u])
                if 0 <= u - 1 < len(UNITS):
                    b, tt, hp = UNITS[u - 1]
                    ns = (tt + 1) * P
                    pe.wait_ge(p_ready, u)
                    if u - 1 >= 2:
                        pe.wait_ge(pt_ready, u - 2)
                    for i in range(2):
                        for s in range(tt + 1):
                            last = nc.tensor.transpose(B[2 + (u - 1) % 2][:, (i * (tt + 1) + s) * P:(i * (tt + 1) + s + 1) * P],
                                                       ssb[(u - 1) % 2][:, i * ns + s * P:i * ns + (s + 1) * P], ident)
                    last.then_inc(pt_done, 1)
                if u - 2 >= 0:
                    b, tt, hp = UNITS[u - 2]
                    g = (u - 2) // 4
                    pe.wait_ge(pt_ready, u - 1)
                    if hp == 0:
                        if g < 2:
                            pe.wait_ge(oc_read, g + 1)
                        else:
                            pe.wait_ge(o_read, g - 1)
                    for i in range(2):
                        h = 2 * hp + i
                        for s in range(tt + 1):
                            if b == 2:
                                v = kdv[:, s, DH:2 * DH]
                            else:
                                first = (2 + b) * P + (h // 4) * DH
                                v = zv[:, s, first:first + DH]
                            last = nc.tensor.matmul(B[4 + g % 2][:, h * DH:(h + 1) * DH],
                                                    pT[(u - 2) % 2][:, (i * (tt + 1) + s) * P:(i * (tt + 1) + s + 1) * P],
                                                    v, start=(s == 0), stop=(s == tt))
                    last.then_inc(o_unit, 1)

            ada(11)
            for n in range(4):
                b, tt = divmod(n, 2)
                pe.wait_ge(o_ready, 1)
                src = (o_nsa, o_dsa)[b][tt]
                for k in range(4):
                    last = nc.tensor.transpose(B[n][:, k * P:(k + 1) * P], src[:, k * P:(k + 1) * P], ident)
                last.then_inc(ot_done, 1)
            wb = [chunk(pe, "br", b).rearrange("p (k n) -> p k n", k=4) for b in range(2)]
            pe.wait_ge(ot_ready, 4)
            for m in range(KT):
                if m >= 2:
                    pe.wait_ge(merged_ready, m - 1)
                for b in range(2):
                    for k in range(4):
                        last = nc.tensor.matmul(B[4 + m % 2][:, b * T:(b + 1) * T], wb[b][:, k, m * P:(m + 1) * P],
                                                oT[:, b, k, :], start=(k == 0), stop=(k == 3))
                last.then_inc(br_done, 1)
            pe.wait_ge(merged_ready, KT)
            for m in range(KT):
                if m % 4 == 0:
                    w = chunk(pe, "out", m // 4).rearrange("p (k n) -> p k n", k=KT)
                if m >= 2:
                    pe.wait_ge(x1_ready, m - 1)
                for k in range(KT):
                    last = nc.tensor.matmul(B[m % 2][:, 0:T], w[:, k, (m % 4) * P:(m % 4 + 1) * P], hT[:, k, :],
                                            start=(k == 0), stop=(k == KT - 1))
                last.then_inc(mo_done, 1)
            square_sum(2, sq2, sq2_ready, ssq2_ready)
            for m in range(KT):
                if m % 4 == 0:
                    w = chunk(pe, "wq", m // 4).rearrange("p (k n) -> p k n", k=KT)
                if m >= 2:
                    pe.wait_ge(q2_ready, m - 1)
                for k in range(KT):
                    if m == 0:
                        pe.wait_ge(h2_ready, k + 1)
                    last = nc.tensor.matmul(B[m % 2][:, 0:T], w[:, k, (m % 4) * P:(m % 4 + 1) * P], h2[:, k, :],
                                            start=(k == 0), stop=(k == KT - 1))
                last.then_inc(q2_done, 1)
            pe.wait_ge(q2_ready, KT)
            pe.wait_ge(sk_in, 16)
            for n in range(8):
                tt, hq, c = n // 4, n // 2 % 2, n % 2
                if n >= 4:
                    pe.wait_ge(sub_ready, n - 3)
                for i in range(4):
                    h = 4 * hq + i
                    last = nc.tensor.matmul(B[4 + n % 4][:, i * KEYS:(i + 1) * KEYS], q2T[c * DH:(c + 1) * DH, h, tt * P:(tt + 1) * P],
                                            skT[c * DH:(c + 1) * DH, h * KEYS:(h + 1) * KEYS], start=True, stop=True)
                last.then_inc(sub_done, 1)
            def act_tile(s, arrived):
                pe.wait_ge(tile_in[s], arrived)
                for k in range(KT):
                    last = nc.tensor.matmul(B[4 + s % 2][:, 0:T], raw[s][:, k * P:(k + 1) * P], h2[:, k, :],
                                            start=(k == 0), stop=(k == KT - 1))
                last.then_inc(tile_used, 1)

            def split_act_tile(s, tile):
                bank = B[4 + s % 2]
                for half in range(2):
                    slot = (2 * s + half) % SLOTS
                    pe.wait_ge(lo_ready[half], tile + 1)
                    w_hi = part_hi[slot].rearrange("p (k j) -> p k j", k=4)
                    w_lo = part_lo[slot].rearrange("p (k j) -> p k j", k=4)
                    for k in range(4):
                        kk = 4 * half + k
                        nc.tensor.matmul(bank[:, 0:T], w_hi[:, k, :], h2h[:, kk, :], start=(kk == 0), stop=False)
                        nc.tensor.matmul(bank[:, 0:T], w_hi[:, k, :], h2l[:, kk, :], start=False, stop=False)
                        last = nc.tensor.matmul(bank[:, 0:T], w_lo[:, k, :], h2h[:, kk, :], start=False, stop=(kk == KT - 1))
                    last.then_inc(part_used, 1)

            def route_group(group, slot):
                pe.wait_ge(oh_ready, group + 1)
                for t in range(TOKS):
                    s = slot * TOKS + t
                    last = nc.tensor.matmul(B[6 + slot][:, t * 2 * IH:(t + 1) * 2 * IH], ohj[s], ohi[s], start=True, stop=True)
                last.then_inc(g_done, 1)

            def v_tile(s, tile, n, start=False, stop=False):
                pe.wait_ge(al_ready, n + 1)
                for half in range(2):
                    slot = 2 * s + half
                    pe.wait_ge(lo_ready[half], tile + 1)
                    for tt in range(TT):
                        at = (s % 2) * T + tt * P
                        bank = B[2 * tt + half]
                        nc.tensor.matmul(bank[:, :], a_hi[:, at:at + P], part_hi[slot], start=start, stop=False)
                        nc.tensor.matmul(bank[:, :], a_hi[:, at:at + P], part_lo[slot], start=False, stop=False)
                        last = nc.tensor.matmul(bank[:, :], a_lo[:, at:at + P], part_hi[slot], start=False, stop=stop)
                    last.then_inc(part_used, 1)

            pe.wait_ge(sub_ready, 8)
            for s in range(SLOTS):
                if s >= 2:
                    pe.wait_ge(gelu_done, s - 1)
                act_tile(s, 16)
            with pe.Fori(1, WHOLE // SLOTS) as turn:
                for s in range(SLOTS):
                    pe.wait_ge(gelu_done, turn * SLOTS + (s - 1))
                    act_tile(s, turn * 16 + 16)
            pe.wait_ge(h2_lo_ready, 1)
            for first, end in ((WHOLE // SLOTS, RT_TURN), (RT_TURN, IH // SLOTS)):
                if first == RT_TURN:
                    pe.wait_ge(route_ready, 1)
                    for tt in range(TT):
                        for i in range(3):
                            last = nc.tensor.transpose(B[tt][:, i * P:(i + 1) * P], route[:, tt, i, :], ident)
                    last.then_inc(rt_done, 1)
                with pe.Fori(first, end) as turn:
                    for s in range(SLOTS):
                        pe.wait_ge(gelu_done, turn * SLOTS + (s - 1))
                        split_act_tile(s, turn * SLOTS + (s - WHOLE))
            def phase2(turn, first=False):
                for s in range(SLOTS):
                    pe.wait_ge(gelu_done, turn * SLOTS + (IH + s - 1))
                    split_act_tile(s, turn * SLOTS + (IH + s - WHOLE))
                    if s >= 2 or not first:
                        pe.wait_ge(weighed, turn * SLOTS + (s - 1))
                    route_group(turn * SLOTS + s, s % 2)

            phase2(0, first=True)
            with pe.Fori(1, IH // SLOTS) as turn:
                phase2(turn)

            def phase3(turn, first=False):
                for s in range(SLOTS):
                    v_tile(s, turn * SLOTS + (KEYS + s - WHOLE), turn * SLOTS + s, start=(first and s == 0))
                    pe.wait_ge(weighed, turn * SLOTS + (IH + s - 1))
                    route_group(turn * SLOTS + (IH + s), s % 2)

            phase3(0, first=True)
            with pe.Fori(1, IH // SLOTS) as turn:
                phase3(turn)
            with pe.Fori(IH // SLOTS, KEYS // SLOTS - 1) as turn:
                for s in range(SLOTS):
                    v_tile(s, turn * SLOTS + (KEYS + s - WHOLE), turn * SLOTS + s)
            for s in range(SLOTS):
                n = KEYS - SLOTS + s
                v_tile(s, KEYS - WHOLE + n, n, stop=(s == SLOTS - 1))
            pe.wait_ge(acc_out, 4)
            for n in range(4):
                for i in range(2):
                    k = 2 * n + i
                    for tt in range(TT):
                        src = acc[2 * tt + k // 4][:, (k % 4) * P:(k % 4 + 1) * P]
                        last = nc.tensor.transpose(B[4 + n][:, i * T + tt * P:i * T + (tt + 1) * P], src, ident)
                last.then_inc(accT_done, 1)
            square_sum(0, sq3, sq3_ready, ssq3_ready)

        @block.gpsimd
        def _(pool):
            pool.wait_ge(x_in, 16)
            pool.wait_ge(rstd_ready, 1)
            nc.gpsimd.tensor_tensor(hT, x3, rstd[:, :].unsqueeze(1).to_broadcast([P, KT, T]), ALU.mult).then_inc(x_scaled, 1)

            pool.wait_ge(h2_hi_ready, 1)
            nc.gpsimd.tensor_tensor(h2_lo[:, :], h2.rearrange("p k t -> p (k t)"), h2_hi[:, :].bitcast(F32), ALU.subtract).then_inc(h2_lo_ready, 1)

            def pick(tt, q):
                pool.wait_ge(matched, 4 * tt + q + 1)
                eq = quarter(q).rearrange("p (h k c) -> p h k c", h=2, k=TOPK)
                nc.gpsimd.tensor_tensor(eq, eq, cidx[tt][:, 2 * q:2 * q + 2, :].unsqueeze(2).to_broadcast([P, 2, TOPK, NCAND]),
                                        ALU.mult).then_inc(picked, 1)

            for tt in range(TT):
                for q in range(4):
                    pick(tt, q)

            def lo_part(s, slot, tile):
                pool.wait_ge(hi_ready, tile * 2 + 2)
                nc.gpsimd.tensor_tensor(part_lo[slot], raw[s][:, 512:1024], part_hi[slot].bitcast(F32),
                                        ALU.subtract).then_inc(lo_ready[1], 1)

            def weight_mask(group, slot, first):
                pool.wait_ge(mask_ready, group + 1)
                nc.gpsimd.tensor_tensor(ohi4[slot], mask4.unsqueeze(2).to_broadcast([P, TOKS, 2, IH]),
                                        w2[:, bass.ds(first, TOKS), :].unsqueeze(3).to_broadcast([P, TOKS, 2, IH]),
                                        ALU.mult).then_inc(oh_ready, 1)

            with pool.Fori(0, (IH - WHOLE) // SLOTS) as turn:
                for s in range(SLOTS):
                    lo_part(s, (2 * s + 1) % SLOTS, turn * SLOTS + s)
            for s in range(2):
                lo_part(s, 2 * s + 1, IH - WHOLE + s)
            pool.wait_ge(w_split, 3)
            def body(turn, half, end=False):
                for s in range(SLOTS):
                    n = turn * SLOTS + s
                    s2 = (s + 2) % SLOTS
                    if not (end and s == SLOTS - 1):
                        weight_mask(n + (half * IH + 1), (s + 1) % 2, (n + 1) * TOKS)
                    lo_part(s2, 2 * s2 + 1 if half else (2 * s2 + 1) % SLOTS, n + (half * IH + IH - WHOLE + 2))

            for half in range(2):
                weight_mask(half * IH, 0, 0)
                with pool.Fori(0, IH // SLOTS - 1) as turn:
                    body(turn, half)
                body(IH // SLOTS - 1, half, end=True)
            with pool.Fori(IH // SLOTS, KEYS // SLOTS - 1) as turn:
                for s in range(SLOTS):
                    s2 = (s + 2) % SLOTS
                    lo_part(s2, 2 * s2 + 1, turn * SLOTS + (KEYS - WHOLE + s + 2))
            for s in range(2, SLOTS):
                lo_part(s, 2 * s + 1, 2 * KEYS - WHOLE - SLOTS + s)

        @block.scalar
        def _(act):
            steps = [0]

            def link(ins):
                steps[0] += 1
                ins.then_inc(act_step, 1)
                act.wait_ge(act_step, steps[0])

            act.dma_start(tab[:, :], A["tab"]).then_inc(tab_in, 16)
            act.dma_start(wukv, A["w_ukv"]).then_inc(w2_in, 16)
            act.dma_start(w2kv, A["cmp_w2"]).then_inc(w2_in, 16)
            act.dma_start(posT, A["cmp_pos"]).then_inc(w2_in, 16)
            act.wait_ge(par_in, 16)
            nc.scalar.activation(silu[:, KT:2 * KT], param("c"), ACT.Exp, scale=-1.0).then_inc(cexp, 1)
            act.wait_ge(x_in, 16)
            for k in range(KT):
                nc.scalar.activation(sq1[:, k, :], x3[:, k, :], ACT.Square).then_inc(sq_ready, 1)
            act.wait_ge(const_set, 1)
            act.wait_ge(ssq_ready, 1)
            nc.scalar.activation(rstd[:, :], B[0][:, 0:T], ACT.Sqrt, bias=eps[:, 0:1], scale=1.0 / D).then_inc(root_ready, 1)

            def ada_start(m):
                w = chunk(act, "ada", m).rearrange("p (k n) -> p k n", k=KT)
                if m >= 2:
                    act.wait_ge(ada_done, m - 1)
                for k in range(2):
                    nc.scalar.activation(ada_buffer(m, k), w[:, k, :], ACT.Identity, scale=silu[:, k:k + 1]).then_inc(ada_first, 1)

            act.wait_ge(silu_ready, 1)
            for m in range(4):
                ada_start(m)

            def job_copy(n):
                kind, *what = JOBS[n]
                bank = B[4 + n % 3]
                act.wait_ge(job_done, n + 1)
                if kind == "rope":
                    r, _, count, to, head, tt = what
                    dst = (qT if to == "q" else kT)[:, head:head + count, tt * P:(tt + 1) * P]
                    last = nc.scalar.activation(dst, bank[0:DH, 0:count * P].rearrange("p (h t) -> p h t", h=count), ACT.Copy)
                elif kind == "ckv":
                    tt, = what
                    nc.scalar.activation(kT[:, VC:VC + 2, tt * P:(tt + 1) * P],
                                         bank[0:DH, P:3 * P].rearrange("p (h t) -> p h t", h=2), ACT.Copy)
                    last = nc.scalar.activation(ckvT[:, tt * P:(tt + 1) * P], bank[:, 0:P], ACT.Identity, scale=param("kvg"))
                else:
                    tt, = what
                    last = nc.scalar.activation(kdv[:, tt, :], bank[:, 0:2 * DH], ACT.Copy)
                last.then_inc(job_out, 1)

            for n in range(0, 4):
                job_copy(n)
            for tt in range(TT):
                act.wait_ge(z_done, 4 + tt + 1)
                nc.scalar.activation(zv[:, tt, :], B[tt][:, :], ACT.Copy).then_inc(zv_ready, 1)
            for n in range(4, 8):
                job_copy(n)
            for tt in range(TT):
                act.wait_ge(ck_sum, tt + 1)
                nc.scalar.activation(small[:, 2 + tt:3 + tt], small[:, tt:tt + 1], ACT.Sqrt,
                                     bias=eps[:, 0:1], scale=1.0 / P).then_inc(ck_root, 1)
            for n in range(8, len(JOBS)):
                job_copy(n)

            act.wait_ge(zk_ready, 2)
            nc.scalar.activation(ssig.rearrange("p (a n) -> p a n", a=TT), zk[:, :, 0:24], ACT.Exp, scale=-1.0).then_inc(gexp, 1)
            for q in range(8):
                ns = (q // 4 + 1) * P
                act.wait_ge(logit_done, q + 1)
                if q >= 2:
                    act.wait_ge(relu_used, q - 1)
                nc.scalar.activation(relu[q % 2][:, 0:2 * ns], B[q % 4][:, 0:2 * ns], ACT.Relu, scale=DH ** -0.5).then_inc(relu_done, 1)
            def gate_copy(m):
                act.wait_ge(fill_done, m + 1)
                nc.scalar.activation(gates[:, m, :], B[6][:, 0:T], ACT.Copy).then_inc(fill_out, 1)

            act.wait_ge(hid_in, 1)
            nc.scalar.activation(hid[:, 120:180], hid[:, 120:180], ACT.Tanh, scale=float(np.sqrt(2.0 / np.pi))).then_inc(tanh_done, 1)
            act.wait_ge(hid_done, 1)
            gate_copy(0)
            gate_copy(1)
            for tt in range(TT):
                act.wait_ge(cs_in, tt + 1)
                nc.scalar.activation(pc[:, tt, :], pc[:, tt, :], ACT.Exp, scale=DH ** -0.5).then_inc(cexp_done, 1)
            gate_copy(2)
            for tt in range(TT):
                act.wait_ge(pct_done, tt + 1)
                nc.scalar.activation(pcT[tt][0:HEADS * NCMP, :], B[2 + tt][0:HEADS * NCMP, 0:P], ACT.Copy).then_inc(pct_ready, 1)
            gate_copy(3)

            for u in range(len(UNITS) + 1):
                if u < len(UNITS):
                    b, tt, hp = UNITS[u]
                    ns = (tt + 1) * P
                    act.wait_ge(s_masked, u + 1)
                    for i in range(2):
                        last = nc.scalar.activation(ssb[u % 2][:, i * ns:(i + 1) * ns], ssb[u % 2][:, i * ns:(i + 1) * ns], ACT.Exp,
                                                    bias=negmax[:, 2 * (u % 2) + i:2 * (u % 2) + i + 1],
                                                    accum_out=rowsum[:, 2 * u + i:2 * u + i + 1])
                    last.then_inc(p_ready, 1)
                if u >= 1:
                    tt = UNITS[u - 1][1]
                    n = 2 * (tt + 1) * P
                    act.wait_ge(pt_done, u)
                    if u - 1 >= 2:
                        act.wait_ge(o_unit, u - 2)
                    nc.scalar.activation(pT[(u - 1) % 2][:, 0:n], B[2 + (u - 1) % 2][:, 0:n], ACT.Copy).then_inc(pt_ready, 1)
                if u < len(UNITS):
                    if UNIT_GATE[u] is not None:
                        gate_copy(UNIT_GATE[u])
            act.wait_ge(fill_out, 16)
            for i in range(KT // 2):
                g = gates.rearrange("p (b m) t -> p b m t", b=2)[:, :, 2 * i:2 * i + 2, :]
                nc.scalar.activation(g, g, ACT.Sigmoid).then_inc(gates_ready, 1)
            for n in range(4):
                b, tt = divmod(n, 2)
                act.wait_ge(ot_done, n + 1)
                nc.scalar.activation(oT[:, b, :, tt * P:(tt + 1) * P], B[n][:, :].rearrange("p (k t) -> p k t", k=4),
                                     ACT.Copy).then_inc(ot_ready, 1)
            nc.scalar.activation(small[:, 9:10], eps[:, 0:1], ACT.Sqrt)
            for k in range(KT):
                act.wait_ge(x1_ready, k + 1)
                nc.scalar.activation(sq2[:, k, :], x3[:, k, :], ACT.Square).then_inc(sq2_ready, 1)
            act.wait_ge(ssq2_ready, 1)
            nc.scalar.activation(rstd[:, :], B[2][:, 0:T], ACT.Sqrt, bias=eps[:, 0:1], scale=1.0 / D).then_inc(root2_ready, 1)
            for k in range(KT):
                act.wait_ge(h2_scaled, k + 1)
                nc.scalar.activation(h2[:, k, :], h2[:, k, :], ACT.Identity, bias=mod[:, 3 * KT + k:3 * KT + k + 1]).then_inc(h2_ready, 1)
            for m in range(KT):
                act.wait_ge(q2_done, m + 1)
                nc.scalar.activation(q2T[:, m, :], B[m % 2][:, 0:T], ACT.Copy).then_inc(q2_ready, 1)
            for n in range(8):
                tt, hq, c = n // 4, n // 2 % 2, n % 2
                act.wait_ge(sub_done, n + 1)
                nc.scalar.activation(sub[tt].rearrange("p (h c) n -> p h c n", c=2)[:, 4 * hq:4 * hq + 4, c, :],
                                     B[4 + n % 4][:, :].rearrange("p (s n) -> p s n", s=4),
                                     ACT.Copy).then_inc(sub_ready, 1)

            act.wait_ge(h2_ready, KT)
            nc.scalar.activation(h2_hi[:, :], h2.rearrange("p k t -> p (k t)"), ACT.Copy).then_inc(h2_hi_ready, 1)

            def gelu(n, s):
                return nc.scalar.activation(gel[:, bass.ds(n, 1), :].rearrange("p a t -> p (a t)"), B[4 + s % 2][:, 0:T], ACT.Gelu)

            def hi_part(s, half, slot, arrived, used):
                if half == 0:
                    act.wait_ge(tile_in[s], arrived)
                if used is not None:
                    act.wait_ge(part_used, used)
                nc.scalar.activation(part_hi[slot], raw[s][:, half * 512:(half + 1) * 512], ACT.Copy).then_inc(hi_ready, 1)

            def g_copy(group, slot, first=False):
                act.wait_ge(g_done, group + 1)
                if not first:
                    act.wait_ge(weighed, group - 1)
                low = g_low[slot]
                nc.scalar.activation(low, B[6 + slot][:, :].rearrange("p (t c i) -> p c t i", t=TOKS, c=2)[:, 1, :, :],
                                     ACT.Copy).then_inc(g_copied, 1)

            def u_body(turn, groups=False, first=False):
                for s in range(SLOTS):
                    n = turn * SLOTS + s
                    gelu(n, s).then_inc(gelu_done, 1)
                    if groups:
                        g_copy(n - IH, s % 2, first=(first and s < 2))
                    if isinstance(n, int) and n == KEYS - 1:
                        return
                    s3, arrived = (s + 3) % SLOTS, (turn + ((s + 3) // SLOTS + 1)) * 16
                    act.wait_ge(part_used, n * 2 + (4 - 2 * WHOLE))
                    for half in range(2):
                        hi_part(s3, half, (2 * s3 + half) % SLOTS, arrived, None)

            def a_part(n, s):
                if not (isinstance(n, int) and n < 2):
                    act.wait_ge(part_used, n * 2 + 2 * (KEYS - WHOLE - 1))
                nc.scalar.activation(a_hi[:, (s % 2) * T:(s % 2 + 1) * T], gel[:, bass.ds(n, 1), :].rearrange("p a t -> p (a t)"),
                                     ACT.Copy).then_inc(ah_ready, 1)

            def v_body(turn, start=False, end=False, groups=False):
                for s in range(SLOTS):
                    n = turn * SLOTS + s
                    s2, arrived = (s + 2) % SLOTS, (turn + (KEYS // SLOTS + (s + 2) // SLOTS + 1)) * 16
                    more = not (isinstance(n, int) and n + 2 >= KEYS)

                    def used(half):
                        return 2 * (KEYS - WHOLE) if start and s < 2 else n * 2 + (2 * (KEYS - WHOLE - 2) + half + 1)

                    if more:
                        for half in range(2):
                            hi_part(s2, half, 2 * s2 + half, arrived, used(half))
                    if not (end and s == SLOTS - 1):
                        a_part(n + 1, s + 1)
                    if groups and not (start and s == 0):
                        g_copy(n + (IH - 1), (s + 1) % 2)

            bounds = (0, 2, WHOLE // SLOTS - 1)
            for tt in range(TT):
                with act.Fori(bounds[tt], bounds[tt + 1]) as turn:
                    for s in range(SLOTS):
                        act.wait_ge(tile_used, turn * SLOTS + (s + 1))
                        gelu(turn * SLOTS + s, s).then_inc(gelu_done, 1)
                if tt:
                    for s in range(SLOTS):
                        n = WHOLE - SLOTS + s
                        act.wait_ge(tile_used, n + 1)
                        gelu(n, s).then_inc(gelu_done, 1)
                        for half in range(2):
                            if s >= 2:
                                hi_part(s - 2, half, 2 * (s - 2) + half, 16 * (WHOLE // SLOTS + 1), None)
                act.wait_ge(top_ready, tt + 1)
                nc.scalar.activation(route[:, tt, 2, :], route[:, tt, 2, :], ACT.Exp).then_inc(gate_exp, 1)
            act.wait_ge(part_used, 2)
            for half in range(2):
                hi_part(2, half, half, 16 * (WHOLE // SLOTS + 1), None)
            with act.Fori(WHOLE // SLOTS, RT_TURN) as turn:
                u_body(turn)
            act.wait_ge(rt_done, 1)
            for tt in range(TT):
                nc.scalar.activation(tiles(routeT[:, :], 3)[:, :, tt * P:(tt + 1) * P], tiles(B[tt][:, 0:3 * P], 3),
                                     ACT.Copy).then_inc(rt_ready, 1)
            with act.Fori(RT_TURN, IH // SLOTS) as turn:
                u_body(turn)
            u_body(IH // SLOTS, groups=True, first=True)
            with act.Fori(IH // SLOTS + 1, KEYS // SLOTS - 1) as turn:
                u_body(turn, groups=True)
            u_body(KEYS // SLOTS - 1, groups=True)
            act.wait_ge(weighed, T // TOKS)
            a_part(0, 0)
            v_body(0, start=True, groups=True)
            with act.Fori(1, IH // SLOTS - 1) as turn:
                v_body(turn, groups=True)
            v_body(IH // SLOTS - 1, end=True, groups=True)
            g_copy(2 * IH - 1, 1)
            act.wait_ge(weighed, 2 * (T // TOKS))
            a_part(IH, 0)
            with act.Fori(IH // SLOTS, KEYS // SLOTS - 1) as turn:
                v_body(turn)
            v_body(KEYS // SLOTS - 1, end=True)
            act.wait_ge(part_used, 4 * KEYS - 2 * WHOLE)
            for n in range(2):
                nc.scalar.activation(acc[n], B[n][:, :], ACT.Copy).then_inc(acc_out, 1)
            nc.scalar.activation(small[:, 10:11], eps[:, 0:1], ACT.Sqrt)
            for k in range(KT):
                act.wait_ge(x2_ready, k + 1)
                nc.scalar.activation(sq3[:, k, :], x3[:, k, :], ACT.Square).then_inc(sq3_ready, 1)
            act.wait_ge(ssq3_ready, 1)
            nc.scalar.activation(rstd[:, :], B[0][:, 0:T], ACT.Sqrt, bias=eps[:, 0:1], scale=1.0 / D).then_inc(root3_ready, 1)

        @block.vector
        def _(dve):
            steps = [0]
            V = nc.vector

            def link(ins):
                steps[0] += 1
                ins.then_inc(dve_step, 1)
                dve.wait_ge(dve_step, steps[0])

            V.memset(eps[:, :], EPS)
            V.memset(ones[:, :], 1.0).then_inc(const_set, 1)
            dve.wait_ge(cexp, 1)
            link(V.tensor_scalar(silu[:, KT:2 * KT], silu[:, KT:2 * KT], 1.0, None, ALU.add))
            link(V.reciprocal(silu[:, 2 * KT:3 * KT], silu[:, KT:2 * KT]))
            V.tensor_tensor(silu[:, 0:KT], silu[:, 2 * KT:3 * KT], param("c"), ALU.mult).then_inc(silu_ready, 1)

            summed = {}

            def ada_step(m, k):
                w = chunk(dve, "ada", m).rearrange("p (k n) -> p k n", k=KT)[:, k, :]
                acc = ada_buffer(m, k % 2)
                if m >= 6 and k == 0:
                    dve.wait_ge(ada_done, m - 1)
                if m >= 5 and k == 1:
                    dve.wait_ge(ada_summed, m)
                if m < 4 and k < 4:
                    dve.wait_ge(ada_first, 2 * m + k - 1)
                elif k >= 2:
                    dve.wait_ge(dve_step, summed[m, k - 2])
                if k < 2:
                    ins = V.tensor_scalar(acc, w, silu[:, k:k + 1], None, ALU.mult)
                else:
                    ins = V.scalar_tensor_tensor(acc, w, silu[:, k:k + 1], acc, ALU.mult, ALU.add)
                ins.then_inc(dve_step, 1)
                steps[0] += 1
                summed[m, k] = steps[0]
                if k == KT - 1:
                    dve.wait_ge(dve_step, steps[0])
                    V.tensor_tensor(ada_buffer(m, 0), ada_buffer(m, 0), acc, ALU.add).then_inc(ada_summed, 1)

            dve.wait_ge(silu_ready, 1)
            for m in range(4):
                if m == 1:
                    dve.wait_ge(root_ready, 1)
                    V.reciprocal(rstd[:, :], rstd[:, :]).then_inc(rstd_ready, 1)
                for k in range(2, KT):
                    ada_step(m, k)

            dve.wait_ge(ada_done, 4)
            link(V.tensor_tensor(mod[:, 0:2 * KT], B[7][:, 0:2 * KT], param("ada_b")[:, 0:2 * KT], ALU.add))
            link(V.tensor_scalar(scale1[:, :], mod[:, KT:2 * KT], 1.0, None, ALU.add))
            link(V.tensor_tensor(scale1[:, :], scale1[:, :], param("g1"), ALU.mult))
            dve.wait_ge(x_scaled, 1)
            for k in range(KT):
                V.tensor_scalar(hT[:, k, :], hT[:, k, :], scale1[:, k:k + 1], mod[:, k:k + 1], ALU.mult, ALU.add).then_inc(h_ready, 1)

            def rope(r):
                c, tt = ROPES[r]
                n = ROPE_HEADS[c]
                cols = n * DH
                if c == "kd":
                    dve.wait_ge(job_out, 10 + tt + 1)
                    src = kdv[:, tt, 0:DH]
                else:
                    pos = c
                    dve.wait_ge(z_done, 2 * pos + tt + 1)
                    src = B[(2 * pos + tt) % 4][:, 0:cols]
                z = src.rearrange("p (h s d) -> p h s d", s=2, d=HALF)
                ra = rope_a[:, 0:cols].rearrange("p (h s d) -> p h s d", s=2, d=HALF)
                rb = rope_b[:, 0:cols].rearrange("p (h s d) -> p h s d", s=2, d=HALF)
                cos = table("cos").rearrange("p (a d) -> p a d", a=TT)[:, tt, :]
                sin = table("sin").rearrange("p (a s d) -> p a s d", a=TT, s=2)[:, tt, :, :]
                cosb = cos.unsqueeze(1).unsqueeze(1).to_broadcast([P, n, 2, HALF])
                if r:
                    dve.wait_ge(roped, r)
                V.tensor_tensor(ra, z, cosb, ALU.mult)
                V.tensor_tensor(rb[:, :, 0, :], z[:, :, 1, :], sin[:, 0, :].unsqueeze(1).to_broadcast([P, n, HALF]), ALU.mult)
                last = V.tensor_tensor(rb[:, :, 1, :], z[:, :, 0, :], sin[:, 1, :].unsqueeze(1).to_broadcast([P, n, HALF]), ALU.mult)
                if c == "kd":
                    link(last)
                else:
                    last.then_inc(z_read, 1)
                    read[0] += 1
                    dve.wait_ge(z_read, read[0])
                if r >= 2:
                    dve.wait_ge(job_done, 1 + max(j for j, w in enumerate(JOBS) if w[0] == "rope" and w[1] == r - 2))
                V.tensor_tensor(rq[r % 2][:, 0:cols], rope_a[:, 0:cols], rope_b[:, 0:cols], ALU.add).then_inc(roped, 1)

            read = [0]
            dve.wait_ge(tab_in, 16)
            for r in range(2):
                rope(r)
            for r in range(2, 4):
                tt = ROPES[r][1]
                dve.wait_ge(z_done, 2 + tt + 1)
                V.tensor_copy(zk[:, tt, :], B[2 + tt][:, 448:480]).then_inc(zk_ready, 1)
                rope(r)
            for tt in range(TT):
                dve.wait_ge(zv_ready, tt + 1)
                dve.wait_ge(*((ck_sum, tt) if tt else (roped, 4)))
                V.tensor_tensor_reduce(out=rope_a[:, 0:P], in0=zv[:, tt, 0:P], in1=zv[:, tt, 0:P], scale=1.0, scalar=0.0,
                                       op0=ALU.mult, op1=ALU.add, accum_out=small[:, tt:tt + 1]).then_inc(ck_sum, 1)
            for tt in range(TT):
                dve.wait_ge(ck_root, tt + 1)
                link(V.reciprocal(small[:, 4 + tt:5 + tt], small[:, 2 + tt:3 + tt]))
                V.tensor_scalar(zv[:, tt, 0:P], zv[:, tt, 0:P], small[:, 4 + tt:5 + tt], None, ALU.mult).then_inc(ck_ready, 1)
            dve.wait_ge(ck_ready, 2)
            for r in range(4, 8):
                rope(r)
            dve.wait_ge(job_out, 10)
            dve.wait_ge(w2_in, 48)
            for v, first in enumerate((KC, VC)):
                for half in range(2):
                    for odd in range(2):
                        lh = CMP_STEP // 2
                        src = kT[:, first:first + 2, half * CMP_STEP:half * CMP_STEP + NCMP * CMP_STEP].rearrange(
                            "p g (n l o) -> p g n l o", l=lh, o=2)[:, :, :, :, odd]
                        dst = blk[odd * DH:(odd + 1) * DH, v, half * lh:(half + 1) * lh, :].rearrange("p l (g n) -> p g n l", g=2)
                        pos = posT[:, half * CMP_STEP:(half + 1) * CMP_STEP].rearrange("p (l o) -> p l o", o=2)[:, :, odd]
                        last = V.tensor_tensor(dst, src, pos.unsqueeze(1).unsqueeze(1).to_broadcast([DH, 2, NCMP, lh]), ALU.add)
            last.then_inc(blk_ready, 1)
            for r in range(8, len(ROPES)):
                rope(r)

            dve.wait_ge(gexp, 1)
            link(V.tensor_scalar(ssig, ssig, 1.0, None, ALU.add))
            link(V.reciprocal(ssig, ssig))
            dve.wait_ge(zk_ready, 2)
            link(V.tensor_scalar(wis.rearrange("p (a n) -> p a n", a=TT), zk[:, :, 24:32], HEADS ** -0.5, None, ALU.mult))

            for q in range(8):
                tt, hp = divmod(q, 4)
                ns = (tt + 1) * P
                sc = score[:, tt, 0:ns]
                for i in range(2):
                    h = 2 * hp + i
                    r = relu[q % 2][:, i * ns:(i + 1) * ns]
                    wh = wis[:, tt * HEADS + h:tt * HEADS + h + 1]
                    if i == 0:
                        dve.wait_ge(relu_done, q + 1)
                    if h == 0:
                        link(V.tensor_scalar(sc, r, wh, None, ALU.mult))
                    elif i == 0:
                        link(V.scalar_tensor_tensor(sc, r, wh, sc, ALU.mult, ALU.add))
                    else:
                        V.scalar_tensor_tensor(sc, r, wh, sc, ALU.mult, ALU.add).then_inc(relu_used, 1)
                        dve.wait_ge(relu_used, q + 1)
                if hp == 3:
                    link(V.tensor_tensor(sc, sc, table("cmask")[:, T - ns:T], ALU.add))

            dve.wait_ge(hid_done, 1)
            V.tensor_copy(hid[:, 0:30], B[7][0:DH, 320:350])
            link(V.tensor_copy(hid[:, 30:60], B[7][0:DH, 384:414]))
            x = hid[:, 0:60]
            link(V.tensor_tensor(hid[:, 60:120], x, x, ALU.mult))
            link(V.tensor_scalar(hid[:, 60:120], hid[:, 60:120], 0.044715, 1.0, ALU.mult, ALU.add))
            V.tensor_tensor(hid[:, 120:180], hid[:, 60:120], x, ALU.mult).then_inc(hid_in, 1)
            dve.wait_ge(tanh_done, 1)
            link(V.tensor_scalar(hid[:, 180:240], hid[:, 120:180], 1.0, 0.5, ALU.add, ALU.mult))
            link(V.tensor_tensor(hid[:, 300:360], hid[:, 180:240], x, ALU.mult))
            V.tensor_copy(hidrep.rearrange("p (g r n) -> p g r n", g=2, r=4),
                          hid[:, 330:360].rearrange("p (g n) -> p g n", g=2).unsqueeze(2).to_broadcast([DH, 2, 4, NCMP])).then_inc(hid_ready, 1)
            dve.wait_ge(cmpkv_done, 1)
            V.tensor_copy(kcmpT, B[7][0:DH, P:P + 2 * NCMP]).then_inc(cmpkv_ready, 1)
            rows = HEADS * NCMP
            V.tensor_tensor(vbd[0:rows, :].rearrange("p (h f) -> p h f", h=HEADS),
                            B[7][0:rows, T:T + DH].unsqueeze(1).to_broadcast([rows, HEADS, DH]),
                            table("bmask")[0:rows, :].unsqueeze(2).to_broadcast([rows, HEADS, DH]), ALU.mult).then_inc(cmpkv_ready, 1)
            for tt in range(TT):
                dve.wait_ge(cs_done, tt + 1)
                s = pc[:, tt, :].rearrange("p (h n) -> p h n", h=HEADS)
                add = table("cmp_add").rearrange("p (a n) -> p a n", a=TT)[:, tt, :].unsqueeze(1).to_broadcast([P, HEADS, NCMP])
                link(V.tensor_tensor(s, B[tt][:, 0:rows].rearrange("p (h n) -> p h n", h=HEADS), add, ALU.add))
                link(V.tensor_reduce(csum[:, 0:8], s, AX.X, ALU.max))
                V.tensor_tensor(s, s, csum[:, 0:8].unsqueeze(2).to_broadcast([P, HEADS, NCMP]), ALU.subtract).then_inc(cs_in, 1)
            for tt in range(TT):
                dve.wait_ge(cexp_done, tt + 1)
                s = pc[:, tt, :].rearrange("p (h n) -> p h n", h=HEADS)
                mul = table("cmp_mul").rearrange("p (a n) -> p a n", a=TT)[:, tt, :].unsqueeze(1).to_broadcast([P, HEADS, NCMP])
                link(V.tensor_tensor(s, s, mul, ALU.mult))
                link(V.tensor_reduce(csum[:, 0:8], s, AX.X, ALU.add))
                link(V.tensor_scalar(csum[:, 0:8], csum[:, 0:8], 1e-30, None, ALU.max))
                link(V.reciprocal(csum[:, 0:8], csum[:, 0:8]))
                V.tensor_tensor(s, s, csum[:, 0:8].unsqueeze(2).to_broadcast([P, HEADS, NCMP]), ALU.mult).then_inc(pc_ready, 1)
            gate3 = ssig.rearrange("p (a h b) -> p a h b", a=TT, b=3)
            for tt in range(TT):
                dve.wait_ge(oc_done, tt + 1)
                V.tensor_tensor(o_nsa[tt].rearrange("p (h f) -> p h f", h=HEADS), B[4 + tt][:, :].rearrange("p (h f) -> p h f", h=HEADS),
                                gate3[:, tt, :, 0].unsqueeze(2).to_broadcast([P, HEADS, DH]), ALU.mult).then_inc(oc_read, 1)
            dve.wait_ge(oc_read, 2)

            def finish(g):
                b, tt, _ = UNITS[4 * g]
                dve.wait_ge(o_unit, 4 * g + 4)
                r = recip[:, 0:HEADS]
                link(V.tensor_scalar(r, rowsum[:, g * HEADS:(g + 1) * HEADS], 1e-30, None, ALU.max))
                link(V.reciprocal(r, r))
                o = B[4 + g % 2][:, :].rearrange("p (h f) -> p h f", h=HEADS)
                if b == 2:
                    V.tensor_tensor(o_dsa[tt].rearrange("p (h f) -> p h f", h=HEADS), o,
                                    r.unsqueeze(2).to_broadcast([P, HEADS, DH]), ALU.mult).then_inc(o_read, 1)
                    dve.wait_ge(o_read, g + 1)
                else:
                    link(V.tensor_tensor(r, r, gate3[:, tt, :, BRANCHES[b][3]], ALU.mult))
                    V.tensor_tensor(otmp.rearrange("p (h f) -> p h f", h=HEADS), o,
                                    r.unsqueeze(2).to_broadcast([P, HEADS, DH]), ALU.mult).then_inc(o_read, 1)
                    dve.wait_ge(o_read, g + 1)
                    link(V.tensor_tensor(o_nsa[tt], o_nsa[tt], otmp, ALU.add))

            for u in range(len(UNITS)):
                b, tt, hp = UNITS[u]
                ns = (tt + 1) * P
                dve.wait_ge(s_done, u + 1)
                if u >= 2:
                    dve.wait_ge(pt_done, u - 1)
                if u == 0:
                    dve.wait_ge(pct_ready, 2)
                for i in range(2):
                    mask = work[:, tt, 0:ns] if b == 2 else table("cmask")[:, T - ns:T]
                    last = V.tensor_tensor_reduce(out=ssb[u % 2][:, i * ns:(i + 1) * ns], in0=B[u % 2][:, i * ns:(i + 1) * ns], in1=mask,
                                                  scale=DH ** -0.5, scalar=-3.0e38, op0=ALU.add, op1=ALU.max,
                                                  accum_out=rowmax[:, 2 * (u % 2) + i:2 * (u % 2) + i + 1])
                link(last)
                V.tensor_scalar(negmax[:, 2 * (u % 2):2 * (u % 2) + 2], rowmax[:, 2 * (u % 2):2 * (u % 2) + 2], -1.0, None,
                                ALU.mult).then_inc(s_masked, 1)
                if u < 16:
                    t2, rnd = divmod(u, 8)
                    n2 = (t2 + 1) * P
                    left = score[:, t2, 0:n2] if rnd == 0 else work[:, t2, 0:n2]
                    link(V.max(best8[:, :], left))
                    link(V.match_replace(work[:, t2, 0:n2], best8[:, :], left, TAKEN))
                    if rnd == TOPK_DSA // 8 - 1:
                        link(V.tensor_scalar(work[:, t2, 0:n2], work[:, t2, 0:n2], TAKEN / 2, NEG, ALU.is_gt, ALU.mult))
                        link(V.tensor_tensor(work[:, t2, 0:n2], work[:, t2, 0:n2], table("cmask")[:, T - n2:T], ALU.add))
                for m, k in UNIT_ADA[u]:
                    ada_step(m, k)
                if u >= 6 and (u - 6) % 4 == 0:
                    finish((u - 6) // 4)
            finish(GROUPS - 1)
            dve.wait_ge(o_read, GROUPS)
            V.tensor_copy(small[:, 8:9], small[:, 4:5]).then_inc(o_ready, 1)

            dve.wait_ge(ada_done, 12)
            link(V.tensor_tensor(mod[:, 2 * KT:6 * KT], B[7][:, 2 * KT:6 * KT], param("ada_b")[:, 2 * KT:6 * KT], ALU.add))
            link(V.tensor_scalar(scale2[:, :], mod[:, 4 * KT:5 * KT], 1.0, None, ALU.add))
            link(V.tensor_tensor(scale2[:, :], scale2[:, :], param("g2"), ALU.mult))
            for m in range(KT):
                dve.wait_ge(br_done, m + 1)
                dve.wait_ge(gates_ready, m // 2 + 1)
                if m == 0:
                    dve.wait_ge(fill_done, 16)
                link(V.tensor_tensor(hT[:, m, :], B[4 + m % 2][:, 0:T], gates[:, m, :], ALU.mult))
                link(V.tensor_tensor(gates[:, m, :], B[4 + m % 2][:, T:2 * T], gates[:, KT + m, :], ALU.mult))
                V.tensor_tensor(hT[:, m, :], hT[:, m, :], gates[:, m, :], ALU.add).then_inc(merged_ready, 1)
            for m in range(KT):
                dve.wait_ge(mo_done, m + 1)
                V.scalar_tensor_tensor(x3[:, m, :], B[m % 2][:, 0:T], mod[:, 2 * KT + m:2 * KT + m + 1], x3[:, m, :],
                                       ALU.mult, ALU.add).then_inc(x1_ready, 1)
            dve.wait_ge(root2_ready, 1)
            link(V.reciprocal(rstd[:, :], rstd[:, :]))
            for k in range(KT):
                V.scalar_tensor_tensor(h2[:, k, :], x3[:, k, :], scale2[:, k:k + 1], rstd[:, :], ALU.mult, ALU.mult).then_inc(h2_scaled, 1)

            def lo_part(s, slot, tile):
                dve.wait_ge(hi_ready, tile * 2 + 1)
                V.tensor_tensor(part_lo[slot], raw[s][:, 0:512], part_hi[slot].bitcast(F32), ALU.subtract).then_inc(lo_ready[0], 1)

            val = tk[:, 0:256].rearrange("p (s k) -> p s k", s=16)
            val4 = tk[:, 0:256].rearrange("p (h c k) -> p h c k", h=HEADS, c=2)
            idx = tk[:, 256:512].bitcast(U32)
            idx_s = idx.rearrange("p (s k) -> p s k", s=16)
            idxf = tk[:, 512:768].rearrange("p (h c k) -> p h c k", h=HEADS, c=2)
            cand = tk[:, 768:768 + HEADS * NCAND].rearrange("p (h c) -> p h c", h=HEADS)
            cwork = [tk[:, 1168:1168 + NCAND], tk[:, 3754:3754 + NCAND]]
            iwork = [tk[:, 1218:1218 + KEYS], tk[:, 3626:3626 + KEYS]]
            top = tk[:, 1346:1346 + P].rearrange("p (h k) -> p h k", h=HEADS)
            pos = tk[:, 1474:1474 + P].bitcast(U32)
            pos_h = pos.rearrange("p (h k) -> p h k", h=HEADS)
            eid = tk[:, 1602:1730]
            eid_i, part_i, part_j = (tk[:, 1346 + i * P:1346 + (i + 1) * P].bitcast(I32) for i in range(3))
            gsum = tk[:, 1730:1738]

            def mark(ins):
                steps[0] += 1
                ins.then_inc(dve_step, 1)
                return steps[0]

            def best16(srcs, values, indices, works, before):
                two = range(2)
                done = [mark(V.max(values[i][:, 0:8], srcs[i])) for i in two]
                dve.wait_ge(dve_step, before)
                for i in two:
                    dve.wait_ge(dve_step, done[i])
                    V.max_index(indices[i][:, 0:8], values[i][:, 0:8], srcs[i])
                    done[i] = mark(V.match_replace(works[i], values[i][:, 0:8], srcs[i], TAKEN))
                for i in two:
                    dve.wait_ge(dve_step, done[i])
                    done[i] = mark(V.max(values[i][:, 8:16], works[i]))
                for i in two:
                    dve.wait_ge(dve_step, done[i])
                    last = mark(V.max_index(indices[i][:, 8:16], values[i][:, 8:16], works[i]))
                return last

            def sum_picked(tt, q):
                dve.wait_ge(picked, 4 * tt + q + 1)
                V.tensor_reduce(eid[:, q * 32:(q + 1) * 32], quarter(q).rearrange("p (k c) -> p k c", c=NCAND),
                                AX.X, ALU.add).then_inc(eid_ready, 1)
                dve.wait_ge(eid_ready, 4 * tt + q + 1)

            def split_number(tt):
                link(V.tensor_copy(eid_i, eid))
                V.tensor_scalar(part_i, eid_i, 7, None, ALU.logical_shift_right)
                link(V.tensor_scalar(part_j, eid_i, KEYS - 1, None, ALU.bitwise_and))
                V.tensor_copy(route[:, tt, 0, :], part_i)
                link(V.tensor_copy(route[:, tt, 1, :], part_j))

            for tt in range(TT):
                last = steps[0]
                for s in range(0, 16, 2):
                    if s % 8 == 0:
                        dve.wait_ge(sub_ready, 4 * tt + s // 4 + 2)
                    last = best16([sub[tt][:, s + i, :] for i in range(2)], [val[:, s + i, :] for i in range(2)],
                                  [idx_s[:, s + i, :] for i in range(2)], iwork, last)
                dve.wait_ge(dve_step, last)
                link(V.tensor_copy(tk[:, 512:768], idx))
                link(V.tensor_scalar(idxf[:, :, 0, :], idxf[:, :, 0, :], float(KEYS), None, ALU.mult))
                for dst, src in ((cand, val4), (cidx[tt], idxf)):
                    c0 = 0
                    for a, n in CAND_ROWS:
                        V.tensor_tensor(dst[:, :, c0:c0 + n], src[:, :, 0, a:a + 1].to_broadcast([P, HEADS, n]), src[:, :, 1, 0:n], ALU.add)
                        c0 += n
                    link(V.tensor_tensor(dst[:, :, c0:NCAND], src[:, :, 0, TOPK // 2:TOPK],
                                         src[:, :, 1, 0:1].to_broadcast([P, HEADS, TOPK // 2]), ALU.add))
                last = steps[0]
                for h in range(0, HEADS, 2):
                    last = best16([cand[:, h + i, :] for i in range(2)], [top[:, h + i, :] for i in range(2)],
                                  [pos_h[:, h + i, :] for i in range(2)], cwork, last)
                dve.wait_ge(dve_step, last)
                w = route[:, tt, 2, :].rearrange("p (h k) -> p h k", h=HEADS)
                V.tensor_tensor(w, top, top[:, :, 0:1].to_broadcast([P, HEADS, TOPK]), ALU.subtract).then_inc(top_ready, 1)
                V.tensor_copy(posf[tt], pos).then_inc(pos_ready, 1)
                dve.wait_ge(pos_ready, tt + 1)
                for q in range(4):
                    if tt:
                        sum_picked(tt - 1, q)
                    V.tensor_tensor(quarter(q).rearrange("p (k c) -> p k c", c=NCAND),
                                    table("pos").unsqueeze(1).to_broadcast([P, 32, NCAND]),
                                    posf[tt][:, q * 32:(q + 1) * 32].unsqueeze(2).to_broadcast([P, 32, NCAND]),
                                    ALU.is_equal).then_inc(matched, 1)
                if tt:
                    split_number(tt - 1)
            for n in range(2):
                lo_part(n, 2 * n, n)
            for q in range(4):
                sum_picked(TT - 1, q)
                if q % 2:
                    n = 2 + q // 2
                    lo_part(n, 2 * n % SLOTS, n)
            split_number(TT - 1)
            for tt in range(TT):
                w = route[:, tt, 2, :].rearrange("p (h k) -> p h k", h=HEADS)
                dve.wait_ge(gate_exp, tt + 1)
                link(V.tensor_reduce(gsum, w, AX.X, ALU.add))
                link(V.reciprocal(gsum, gsum))
                last = V.tensor_tensor(w, w, gsum.unsqueeze(2).to_broadcast([P, HEADS, TOPK]), ALU.mult)
                if tt < TT - 1:
                    link(last)
            last.then_inc(route_ready, 1)

            iT, jT, wT = (routeT[:, i * T:(i + 1) * T] for i in range(3))

            def one_hots(group, slot, first, half):
                V.tensor_tensor(ohj4[slot], table("iota").unsqueeze(1).to_broadcast([P, TOKS, P]),
                                jT[:, bass.ds(first, TOKS)].unsqueeze(2).to_broadcast([P, TOKS, P]), ALU.is_equal)
                if not (isinstance(group, int) and group == 0):
                    dve.wait_ge(oh_ready, group)
                V.tensor_tensor(mask4, table("iota")[:, half * IH:(half + 1) * IH].unsqueeze(1).to_broadcast([P, TOKS, IH]),
                                iT[:, bass.ds(first, TOKS)].unsqueeze(2).to_broadcast([P, TOKS, IH]), ALU.is_equal).then_inc(mask_ready, 1)

            def weigh(group, slot, first, half):
                dve.wait_ge(g_copied, group + 1)
                g = gel[:, half * IH:(half + 1) * IH, bass.ds(first, TOKS)]
                high = B[6 + slot][:, :].rearrange("p (t c i) -> p c t i", t=TOKS, c=2)[:, 0, :, :]
                low = g_low[slot]
                V.tensor_tensor(low, high, low, ALU.add).then_inc(g_summed, 1)
                dve.wait_ge(g_summed, group + 1)
                V.tensor_tensor(g, g, low.rearrange("p t i -> p i t"), ALU.mult).then_inc(weighed, 1)

            def a_part(n, s):
                dve.wait_ge(ah_ready, n + 1)
                at = (s % 2) * T
                V.tensor_tensor(a_lo[:, at:at + T], gel[:, bass.ds(n, 1), :].rearrange("p a t -> p (a t)"),
                                a_hi[:, at:at + T].bitcast(F32), ALU.subtract).then_inc(al_ready, 1)

            def body(turn, half, start=False, end=False):
                for s in range(SLOTS):
                    n = turn * SLOTS + s
                    s2 = (s + 2) % SLOTS
                    if start and s == 1:
                        dve.wait_ge(gelu_done, (half + 1) * IH)
                    if not (start and s == 0):
                        weigh(n + (half * IH - 1), (s + 1) % 2, (n - 1) * TOKS, half)
                    if half and not (end and s == SLOTS - 1):
                        a_part(n + 1, s + 1)
                    if not (end and s == SLOTS - 1):
                        one_hots(n + (half * IH + 1), (s + 1) % 2, (n + 1) * TOKS, half)
                    lo_part(s2, 2 * s2 if half else 2 * s2 % SLOTS, n + (half * IH + (IH - WHOLE + 2)))

            turns = IH // SLOTS
            assert T // TOKS == IH
            with dve.Fori(1, (IH - WHOLE) // SLOTS) as turn:
                for s in range(SLOTS):
                    lo_part(s, 2 * s % SLOTS, turn * SLOTS + s)
            for s in range(2):
                lo_part(s, 2 * s, IH - WHOLE + s)
            dve.wait_ge(rt_ready, TT)
            w_hi = a_hi[:, 0:T]
            V.tensor_copy(w_hi, wT).then_inc(w_split, 1)
            dve.wait_ge(w_split, 1)
            V.tensor_copy(w2[:, :, 0], w_hi.bitcast(F32)).then_inc(w_split, 1)
            V.tensor_tensor(w2[:, :, 1], wT, w_hi.bitcast(F32), ALU.subtract).then_inc(w_split, 1)
            for half in range(2):
                one_hots(half * IH, 0, 0, half)
                if half:
                    weigh(IH - 1, 1, T - TOKS, 0)
                    a_part(0, 0)
                body(0, half, start=True)
                with dve.Fori(1, turns - 1) as turn:
                    body(turn, half)
                body(turns - 1, half, end=True)
            weigh(2 * IH - 1, 1, T - TOKS, 1)
            a_part(IH, 0)
            with dve.Fori(turns, 2 * turns - 1) as turn:
                for s in range(SLOTS):
                    s2 = (s + 2) % SLOTS
                    lo_part(s2, 2 * s2, turn * SLOTS + (KEYS - WHOLE + s + 2))
                    a_part(turn * SLOTS + (s + 1), s + 1)
            for s in range(SLOTS - 1):
                if s < 2:
                    lo_part(s + 2, 2 * (s + 2), 2 * KEYS - WHOLE - 2 + s)
                a_part(KEYS - SLOTS + s + 1, s + 1)
            dve.wait_ge(part_used, 4 * KEYS - 2 * WHOLE)
            for n in range(2, 4):
                V.tensor_copy(acc[n], B[n][:, :]).then_inc(acc_out, 1)
            for m in range(KT):
                dve.wait_ge(accT_done, m // 2 + 1)
                V.scalar_tensor_tensor(x3[:, m, :], B[4 + m // 2][:, (m % 2) * T:(m % 2 + 1) * T], mod[:, 5 * KT + m:5 * KT + m + 1],
                                       x3[:, m, :], ALU.mult, ALU.add).then_inc(x2_ready, 1)
            dve.wait_ge(root3_ready, 1)
            link(V.reciprocal(rstd[:, :], rstd[:, :]))
            for m in range(KT):
                V.scalar_tensor_tensor(y[:, m, :], x3[:, m, :], param("gf")[:, m:m + 1], rstd[:, :], ALU.mult, ALU.mult).then_inc(y_ready, 1)


def constants():
    tab = np.zeros((P, TAB_W), np.float32)

    def put(name, a):
        tab[:a.shape[0], TAB[name][0]:TAB[name][0] + a.shape[1]] = a

    t = np.arange(T)
    p = np.arange(P)
    put("ident", np.eye(P))
    put("cmask", np.concatenate([np.zeros((P, P)), np.where(p[None, :] <= p[:, None], 0.0, NEG)], 1))
    put("iota", np.tile(p.astype(np.float32), (P, 1)))
    inv = np.float32(10000.0) ** (-np.arange(HALF, dtype=np.float32) / np.float32(HALF))
    ang = t.astype(np.float32)[:, None] * inv.astype(np.float32)[None, :]
    cos, sin = np.cos(ang), np.sin(ang)
    put("cos", cos.reshape(TT, P, HALF).transpose(1, 0, 2).reshape(P, -1))
    put("sin", np.stack([-sin, sin], 1).reshape(TT, P, 2 * HALF).transpose(1, 0, 2).reshape(P, -1))
    ok = (np.arange(NCMP) * CMP_STEP + CMP_LEN - 1)[None, :] <= t[:, None]
    put("cmp_add", np.where(ok, 0.0, NEG).reshape(TT, P, NCMP).transpose(1, 0, 2).reshape(P, -1))
    put("cmp_mul", ok.astype(np.float32).reshape(TT, P, NCMP).transpose(1, 0, 2).reshape(P, -1))
    put("bmask", (np.arange(HEADS * NCMP)[:, None] // NCMP == np.arange(HEADS)[None, :]).astype(np.float32))
    put("pos", np.tile(np.arange(NCAND, dtype=np.float32), (P, 1)))
    return tab


def kernel(**inputs):
    import concourse.bacc as bacc
    from concourse.bass_utils import run_bass_kernel_spmd

    a = {k: np.asarray(v) for k, v in inputs.items()}

    def feature_tiles(v):
        return v.reshape(-1, P).T

    w_in = a["w_in"][0]
    par = np.concatenate([feature_tiles(a["c"][0]), feature_tiles(a["ada_b"][0]), feature_tiles(a["norm1_g"][0]),
                          feature_tiles(a["norm2_g"][0]), feature_tiles(a["final_g"]), a["kv_norm_g"][0][:, None]], 1)
    arrays = {
        "par": par,
        "tab": constants(),
        "x": a["x"][0].T,
        "ada_w": a["ada_w"][0],
        "w_in": np.concatenate([w_in[:, START[n]:START[n] + SIZE[n]] for c in CHUNKS for n in c], 1),
        "w_gate": w_in[:, START["g_m"]:],
        "w_br": np.stack([a["w_br_nsa"][0], a["w_br_dsa"][0]]),
        "w_out": a["w_out"][0],
        "peer_wq": a["peer_wq"][0],
        "w_ukv": np.concatenate([a["w_uk"][0], a["w_uv"][0]], 1),
        "cmp_w2": np.concatenate([a["cmp_w2_k"][0], a["cmp_w2_v"][0]], 1),
        "cmp_pos": a["cmp_pos"][0].T,
        "cmp_w1_k": a["cmp_w1_k"][0].reshape(CMP_LEN // 2, P, DH).transpose(1, 0, 2),
        "cmp_w1_v": a["cmp_w1_v"][0].reshape(CMP_LEN // 2, P, DH).transpose(1, 0, 2),
        "subkeys": a["peer_subkeys"][0].transpose(1, 3, 0, 2).reshape(P, HEADS * KEYS),
        "uT": a["peer_u"][0].reshape(KEYS, KEYS, KT, P).transpose(0, 3, 2, 1),
        "v": a["peer_v"][0].reshape(KEYS, KEYS, D),
    }
    nc = bacc.Bacc("TRN2", target_bir_lowering=False, num_devices=1)
    feeds, aps = {}, {}
    for name, v in arrays.items():
        v = np.ascontiguousarray(v)
        feeds[f"in_{name}"] = v
        aps[name] = nc.dram_tensor(f"in_{name}", v.shape, mybir.dt.from_np(v.dtype), kind="ExternalInput").ap()
    out = nc.dram_tensor("yT", (D, T), F32, kind="ExternalOutput").ap()
    build(nc, aps, out)
    r = run_bass_kernel_spmd(nc, [feeds], core_ids=[0])
    return np.ascontiguousarray(r.results[0]["yT"].T).reshape(1, T, D)
```
